# Optimizing a Trainium2 kernel written in Bass

```python
import math
import jax
import jax.numpy as jnp
from jax import lax
import numpy as np

D_MODEL = 1024
BATCH = 1
SEQ = 512
DEPTH = 1
DEC_BATCH = 8
DEC_SEQ = 8
PAST_LEN = 1024
PAGE_SIZE = 128

SSM_WIDTH = D_MODEL // 2
SSM_GROUP = 16
SSM_GROUPS = SSM_WIDTH // SSM_GROUP
SSM_STATE = 64
HEAD_DIM = 64
N_HEADS = (D_MODEL // 2) // HEAD_DIM
N_KV_HEADS = 2
HEADS_PER_KV = N_HEADS // N_KV_HEADS
Q_DIM = N_HEADS * HEAD_DIM
KV_DIM = N_KV_HEADS * HEAD_DIM
L_CMP = 32
L_STRIDE = L_CMP // 2
CMP_HIDDEN = HEAD_DIM
L_SEL = 64
N_SEL = 16
WINDOW = 512
Q_BLOCK = 128
ROPE_THETA = 10000.0
FORCE_SCORE = 1.0e4
N_KV_SLOTS = 4
N_EXPERT_GROUPS = 4
EXPERTS_PER_GROUP = 8
N_EXPERTS = N_EXPERT_GROUPS * EXPERTS_PER_GROUP
TOP_K = 2
D_EXPERT = 512
EXPERT_BLOCK = 128
NORM_EPS = 1e-6
IN_DIM = SSM_WIDTH + Q_DIM + 6 * KV_DIM + 3 * N_HEADS + 2 * D_MODEL

kernel_name = "hybrid_s5_nsa_hmoe_step"

def rms_norm(x, g):
    xf = x.astype(jnp.float32)
    y = xf * lax.rsqrt(jnp.mean(xf * xf, axis=-1, keepdims=True) + NORM_EPS)
    return (y * g.astype(jnp.float32)).astype(x.dtype)

def rope(x, pos):
    half = HEAD_DIM // 2
    inv = ROPE_THETA ** (-jnp.arange(half, dtype=jnp.float32) / half)
    ang = pos.astype(jnp.float32)[:, None] * inv[None, :]
    cos = jnp.cos(ang)[None, :, None, :]
    sin = jnp.sin(ang)[None, :, None, :]
    xf = x.astype(jnp.float32)
    x1, x2 = xf[..., :half], xf[..., half:]
    return jnp.concatenate([x1 * cos - x2 * sin, x2 * cos + x1 * sin], axis=-1).astype(x.dtype)

def masked_softmax(s, mask):
    s = jnp.where(mask, s.astype(jnp.float32), -jnp.inf)
    m = jnp.max(s, axis=-1, keepdims=True)
    m = jnp.where(jnp.isfinite(m), m, 0.0)
    e = jnp.where(mask, jnp.exp(s - m), 0.0)
    den = jnp.sum(e, axis=-1, keepdims=True)
    return e / jnp.where(den > 0, den, 1.0)

def pad_rows(a):
    extra = (-a.shape[1]) % L_SEL
    return jnp.pad(a, ((0, 0), (0, extra)) + ((0, 0),) * (a.ndim - 2))

def mixer_projection(x, p, pos):
    bsz, t, _ = x.shape
    z = rms_norm(x, p['g_mix']) @ p['w_in']
    sizes = (SSM_WIDTH, Q_DIM, KV_DIM, KV_DIM, KV_DIM, KV_DIM, KV_DIM, KV_DIM, 3 * N_HEADS, 2 * D_MODEL)
    u, q, kc, vc, ks, vs, kw, vw, g_nsa, g_mrg = jnp.split(z, np.cumsum(sizes)[:-1].tolist(), axis=-1)
    heads = lambda a, n: a.reshape(bsz, t, n, HEAD_DIM)
    q = rope(heads(q, N_HEADS), pos).reshape(bsz, t, N_KV_HEADS, HEADS_PER_KV, HEAD_DIM)
    kc, ks, kw = rope(heads(kc, N_KV_HEADS), pos), rope(heads(ks, N_KV_HEADS), pos), rope(heads(kw, N_KV_HEADS), pos)
    vc, vs, vw = heads(vc, N_KV_HEADS), heads(vs, N_KV_HEADS), heads(vw, N_KV_HEADS)
    g_nsa = jax.nn.sigmoid(g_nsa.astype(jnp.float32)).astype(x.dtype).reshape(bsz, t, N_KV_HEADS, HEADS_PER_KV, 3)
    return u, q, kc, vc, ks, vs, kw, vw, g_nsa, g_mrg

def _complex_affine_combine(earlier, later):
    a1r, a1i, b1r, b1i = earlier
    a2r, a2i, b2r, b2i = later
    return (a2r * a1r - a2i * a1i, a2r * a1i + a2i * a1r,
            a2r * b1r - a2i * b1i + b2r, a2r * b1i + a2i * b1r + b2i)

def s5_branch(u, h0, p):
    f32 = jnp.float32
    bsz, t = u.shape[:2]
    uf = u.astype(f32).reshape(bsz, t, SSM_GROUPS, SSM_GROUP)
    a_re, a_im = p['ssm_a_re'].astype(f32), p['ssm_a_im'].astype(f32)
    dt = jnp.exp(p['ssm_log_dt'].astype(f32))[:, None]
    mag = jnp.exp(a_re * dt)
    lb_re, lb_im = mag * jnp.cos(a_im * dt), mag * jnp.sin(a_im * dt)
    den = a_re * a_re + a_im * a_im
    zr = lb_re - 1.0
    f_re = (zr * a_re + lb_im * a_im) / den
    f_im = (lb_im * a_re - zr * a_im) / den
    b_re, b_im = p['ssm_b_re'].astype(f32), p['ssm_b_im'].astype(f32)
    bb_re = f_re[..., None] * b_re - f_im[..., None] * b_im
    bb_im = f_re[..., None] * b_im + f_im[..., None] * b_re
    bu_re = jnp.einsum('btgc,gpc->btgp', uf, bb_re)
    bu_im = jnp.einsum('btgc,gpc->btgp', uf, bb_im)
    lam_re = jnp.broadcast_to(lb_re, bu_re.shape)
    lam_im = jnp.broadcast_to(lb_im, bu_re.shape)
    acc_re, acc_im, x_re, x_im = lax.associative_scan(
        _complex_affine_combine, (lam_re, lam_im, bu_re, bu_im), axis=1)
    h0r, h0i = h0[..., 0].astype(f32)[:, None], h0[..., 1].astype(f32)[:, None]
    x_re, x_im = x_re + acc_re * h0r - acc_im * h0i, x_im + acc_re * h0i + acc_im * h0r
    c_re, c_im = p['ssm_c_re'].astype(f32), p['ssm_c_im'].astype(f32)
    y = (jnp.einsum('gcp,btgp->btgc', c_re, x_re) - jnp.einsum('gcp,btgp->btgc', c_im, x_im)
         + p['ssm_d'].astype(f32) * uf)
    y = jax.nn.gelu(y.reshape(bsz, t, SSM_WIDTH)).astype(u.dtype)
    y_lin, y_gate = jnp.split(y @ p['w_glu'], 2, axis=-1)
    out = (y_lin * jax.nn.sigmoid(y_gate)) @ p['w_ssm_proj']
    h_last = jnp.stack([x_re[:, -1], x_im[:, -1]], axis=-1).astype(u.dtype)
    return out, h_last

def compress_rows(k, pe, w1, b1, w2):
    bsz, tk = k.shape[:2]
    halves = k.reshape(bsz, tk // L_STRIDE, L_STRIDE, N_KV_HEADS, HEAD_DIM)
    w1r = w1.reshape(2, L_STRIDE, HEAD_DIM, CMP_HIDDEN)
    lead = jnp.einsum('bnlgd,lde->bnge', halves, w1r[0])
    trail = jnp.einsum('bnlgd,lde->bnge', halves, w1r[1])
    pe_term = jnp.einsum('ld,lde->e', pe, w1.reshape(L_CMP, HEAD_DIM, CMP_HIDDEN))
    hidden = jax.nn.gelu(lead[:, :-1] + trail[:, 1:] + pe_term + b1)
    return hidden @ w2

def compress_kv(k_full, v_full, p):
    kc = compress_rows(k_full, p['cmp_pe_k'], p['cmp_w1_k'], p['cmp_b1_k'], p['cmp_w2_k'])
    vc = compress_rows(v_full, p['cmp_pe_v'], p['cmp_w1_v'], p['cmp_b1_v'], p['cmp_w2_v'])
    c_end = jnp.arange(kc.shape[1], dtype=jnp.int32) * L_STRIDE + (L_CMP - 1)
    return kc, vc, c_end

def nsa_attend(q, q_pos, kc, vc, c_end, ks, vs, kw, vw, kw_pos, gate):
    bsz, tq = q.shape[:2]
    scale = HEAD_DIM ** -0.5
    s_c = jnp.einsum('bqghd,bcgd->bghqc', q, kc).astype(jnp.float32) * scale
    p_c = masked_softmax(s_c, c_end[None, :] <= q_pos[:, None])
    o_c = jnp.einsum('bghqc,bcgd->bqghd', p_c.astype(vc.dtype), vc)
    imp = jnp.sum(p_c, axis=2)
    pad = ((0, 0), (0, 0), (0, 0))
    imp_half = jnp.pad(imp, pad + ((0, 1),)) + jnp.pad(imp, pad + ((1, 0),))
    n_sb = ks.shape[1] // L_SEL
    imp_sel = imp_half.reshape(bsz, N_KV_HEADS, tq, n_sb, L_SEL // L_STRIDE).sum(-1)
    sb = jnp.arange(n_sb, dtype=jnp.int32)[None, :]
    cur = (q_pos // L_SEL)[:, None]
    future = sb * L_SEL > q_pos[:, None]
    forced = (sb == 0) | (sb == cur) | (sb == cur - 1)
    score = jnp.where(future, -1.0, jnp.where(forced, FORCE_SCORE, imp_sel))
    _, idx = lax.top_k(score, min(N_SEL, n_sb))
    ks_b = ks.reshape(bsz, n_sb, L_SEL, N_KV_HEADS, HEAD_DIM).transpose(0, 3, 1, 2, 4)
    vs_b = vs.reshape(bsz, n_sb, L_SEL, N_KV_HEADS, HEAD_DIM).transpose(0, 3, 1, 2, 4)
    bi = jnp.arange(bsz)[:, None, None, None]
    gi = jnp.arange(N_KV_HEADS)[None, :, None, None]
    k_sel, v_sel = ks_b[bi, gi, idx], vs_b[bi, gi, idx]
    n_top = idx.shape[-1]
    tok_pos = idx[..., None] * L_SEL + jnp.arange(L_SEL, dtype=jnp.int32)
    mask_s = (tok_pos <= q_pos[None, None, :, None, None]).reshape(bsz, N_KV_HEADS, 1, tq, n_top * L_SEL)
    s_s = jnp.einsum('bqghd,bgqkld->bghqkl', q, k_sel).astype(jnp.float32) * scale
    p_s = masked_softmax(s_s.reshape(bsz, N_KV_HEADS, HEADS_PER_KV, tq, n_top * L_SEL), mask_s)
    p_s = p_s.reshape(bsz, N_KV_HEADS, HEADS_PER_KV, tq, n_top, L_SEL)
    o_s = jnp.einsum('bghqkl,bgqkld->bqghd', p_s.astype(vs.dtype), v_sel)
    s_w = jnp.einsum('bqghd,bkgd->bghqk', q, kw).astype(jnp.float32) * scale
    delta = q_pos[:, None] - kw_pos[None, :]
    mask_w = (delta >= 0) & (delta < WINDOW) & (kw_pos[None, :] >= 0)
    o_w = jnp.einsum('bghqk,bkgd->bqghd', masked_softmax(s_w, mask_w).astype(vw.dtype), vw)
    return gate[..., 0:1] * o_c + gate[..., 1:2] * o_s + gate[..., 2:3] * o_w

def hier_moe(h, p):
    n = h.shape[0]
    f32 = jnp.float32
    g_logits = (h @ p['w_router_group']).astype(f32) + p['b_router_group'].astype(f32)
    g_sel = jnp.argmax(g_logits, axis=-1).astype(jnp.int32)
    g_w = jnp.max(jax.nn.softmax(g_logits, axis=-1), axis=-1)
    e_logits = ((h @ p['w_router_expert']).astype(f32) + p['b_router_expert'].astype(f32)).reshape(
        n, N_EXPERT_GROUPS, EXPERTS_PER_GROUP)[jnp.arange(n), g_sel]
    top_v, top_i = lax.top_k(e_logits, TOP_K)
    w_assign = (jax.nn.softmax(top_v, axis=-1) * g_w[:, None]).reshape(-1)
    e_assign = (g_sel[:, None] * EXPERTS_PER_GROUP + top_i).reshape(-1).astype(jnp.int32)
    n_assign = n * TOP_K
    tok_assign = jnp.arange(n_assign, dtype=jnp.int32) // TOP_K
    order = jnp.argsort(e_assign)
    e_s, tok_s, w_s = e_assign[order], tok_assign[order], w_assign[order]
    counts = jnp.bincount(e_assign, length=N_EXPERTS)
    padded = (counts + EXPERT_BLOCK - 1) // EXPERT_BLOCK * EXPERT_BLOCK
    pad_end = jnp.cumsum(padded)
    pad_start = pad_end - padded
    start = jnp.cumsum(counts) - counts
    dest = pad_start[e_s] + jnp.arange(n_assign, dtype=jnp.int32) - start[e_s]
    n_blocks = -(-n_assign // EXPERT_BLOCK) + N_EXPERTS
    buf = jnp.zeros((n_blocks * EXPERT_BLOCK, D_MODEL), h.dtype).at[dest].set(h[tok_s])
    block_expert = jnp.minimum(
        jnp.searchsorted(pad_end, jnp.arange(n_blocks, dtype=jnp.int32) * EXPERT_BLOCK, side='right'),
        N_EXPERTS - 1)

    def expert_block(args):
        xb, e = args
        return (jax.nn.silu(xb @ p['w_exp_gate'][e]) * (xb @ p['w_exp_up'][e])) @ p['w_exp_down'][e]

    out = lax.map(expert_block, (buf.reshape(n_blocks, EXPERT_BLOCK, D_MODEL), block_expert))
    out = out.reshape(-1, D_MODEL)
    return jnp.zeros((n, D_MODEL), h.dtype).at[tok_s].add(out[dest] * w_s[:, None].astype(h.dtype))

def merge_and_ffn(x, ssm_out, attn_heads, g_mrg, p):
    bsz, t, _ = x.shape
    attn_out = attn_heads @ p['w_attn_proj']
    g_s, g_a = jnp.split(jax.nn.sigmoid(g_mrg), 2, axis=-1)
    x = x + (g_s * ssm_out + g_a * attn_out) @ p['w_out']
    h = rms_norm(x, p['g_ffn']).reshape(bsz * t, D_MODEL)
    return x + hier_moe(h, p).reshape(bsz, t, D_MODEL)

def gather_past(cache_kv, layer, page_table, slot):
    rows = cache_kv[layer, page_table, :, slot]
    return rows.reshape(page_table.shape[0], -1, N_KV_HEADS, HEAD_DIM)

def prompt_layer(x, p):
    bsz, t, _ = x.shape
    pos = jnp.arange(t, dtype=jnp.int32)
    u, q, kc, vc, ks, vs, kw, vw, g_nsa, g_mrg = mixer_projection(x, p, pos)
    ssm_out, ssm_state = s5_branch(u, jnp.zeros((bsz, SSM_GROUPS, SSM_STATE, 2), x.dtype), p)
    cmp_k, cmp_v, c_end = compress_kv(pad_rows(kc), pad_rows(vc), p)
    ks_full, vs_full = pad_rows(ks), pad_rows(vs)
    front = ((0, 0), (WINDOW, 0), (0, 0), (0, 0))
    kw_pad, vw_pad = jnp.pad(kw, front), jnp.pad(vw, front)

    def attend_block(i):
        start = i * Q_BLOCK
        sl = lambda a, n: lax.dynamic_slice_in_dim(a, start, n, axis=1)
        q_pos = start + jnp.arange(Q_BLOCK, dtype=jnp.int32)
        kw_pos = start - WINDOW + jnp.arange(WINDOW + Q_BLOCK, dtype=jnp.int32)
        return nsa_attend(sl(q, Q_BLOCK), q_pos, cmp_k, cmp_v, c_end, ks_full, vs_full,
                          sl(kw_pad, WINDOW + Q_BLOCK), sl(vw_pad, WINDOW + Q_BLOCK), kw_pos,
                          sl(g_nsa, Q_BLOCK))

    o = lax.map(attend_block, jnp.arange(t // Q_BLOCK, dtype=jnp.int32))
    o = jnp.moveaxis(o, 0, 1).reshape(bsz, t, Q_DIM)
    y = merge_and_ffn(x, ssm_out, o, g_mrg, p)
    kv_rows = jnp.stack([kc, vc, ks, vs], axis=2)
    win = jnp.stack([kw, vw], axis=2)[:, t - min(WINDOW, t):]
    return y, kv_rows, win, ssm_state

def sample_layer(x, cache_kv, layer, win_buf, ssm_h0, page_table, p):
    bsz, t, _ = x.shape
    pos = PAST_LEN + jnp.arange(t, dtype=jnp.int32)
    u, q, kc, vc, ks, vs, kw, vw, g_nsa, g_mrg = mixer_projection(x, p, pos)
    ssm_out, ssm_state = s5_branch(u, ssm_h0, p)
    full = lambda slot, new: pad_rows(jnp.concatenate([gather_past(cache_kv, layer, page_table, slot), new], axis=1))
    cmp_k, cmp_v, c_end = compress_kv(full(0, kc), full(1, vc), p)
    ks_full, vs_full = full(2, ks), full(3, vs)
    n_win = win_buf.shape[1]
    kw_all = jnp.concatenate([win_buf[:, :, 0], kw], axis=1)
    vw_all = jnp.concatenate([win_buf[:, :, 1], vw], axis=1)
    kw_pos = PAST_LEN - n_win + jnp.arange(n_win + t, dtype=jnp.int32)
    o = nsa_attend(q, pos, cmp_k, cmp_v, c_end, ks_full, vs_full, kw_all, vw_all, kw_pos, g_nsa)
    y = merge_and_ffn(x, ssm_out, o.reshape(bsz, t, Q_DIM), g_mrg, p)
    kv_rows = jnp.stack([kc, vc, ks, vs], axis=2)
    new_win = jnp.stack([kw_all, vw_all], axis=2)[:, t:]
    return y, kv_rows, new_win, ssm_state

def setup_inputs(seed: int = 0) -> dict:
    key = jax.random.key(seed)
    keys = iter(jax.random.split(key, 48))
    f32 = jnp.float32

    def normal(shape, scale):
        return scale * jax.random.normal(next(keys), shape, f32)

    n_pages = PAST_LEN // PAGE_SIZE
    n_used = DEC_BATCH * n_pages
    n_pool = n_used + n_used // 4
    win_buf = min(WINDOW, PAST_LEN)
    x_prompt = normal((BATCH, SEQ, D_MODEL), 1.0)
    x_sample = normal((DEC_BATCH, DEC_SEQ, D_MODEL), 1.0)
    cache_kv = normal((DEPTH, n_pool, PAGE_SIZE, N_KV_SLOTS, N_KV_HEADS, HEAD_DIM), 1.0)
    cache_win = normal((DEPTH, DEC_BATCH, win_buf, 2, N_KV_HEADS, HEAD_DIM), 1.0)
    state_ssm = normal((DEPTH, DEC_BATCH, SSM_GROUPS, SSM_STATE, 2), 0.1)
    page_table = jax.random.permutation(next(keys), n_pool)[:n_used].reshape(DEC_BATCH, n_pages).astype(jnp.int32)
    n_idx = jnp.arange(SSM_STATE, dtype=f32)
    ssm_a_re = -0.5 + normal((DEPTH, SSM_GROUPS, SSM_STATE), 0.01)
    ssm_a_im = jnp.pi * n_idx + normal((DEPTH, SSM_GROUPS, SSM_STATE), 0.01)
    ssm_log_dt = jax.random.uniform(next(keys), (DEPTH, SSM_GROUPS), f32, math.log(1e-3), math.log(1e-1))
    return {
        'x_prompt': x_prompt,
        'x_sample': x_sample,
        'cache_kv': cache_kv,
        'cache_win': cache_win,
        'state_ssm': state_ssm,
        'page_table': page_table,
        'g_mix': 1.0 + normal((DEPTH, D_MODEL), 0.01),
        'w_in': normal((DEPTH, D_MODEL, IN_DIM), D_MODEL ** -0.5),
        'ssm_a_re': ssm_a_re,
        'ssm_a_im': ssm_a_im,
        'ssm_log_dt': ssm_log_dt,
        'ssm_b_re': normal((DEPTH, SSM_GROUPS, SSM_STATE, SSM_GROUP), (2 * SSM_GROUP) ** -0.5),
        'ssm_b_im': normal((DEPTH, SSM_GROUPS, SSM_STATE, SSM_GROUP), (2 * SSM_GROUP) ** -0.5),
        'ssm_c_re': normal((DEPTH, SSM_GROUPS, SSM_GROUP, SSM_STATE), SSM_STATE ** -0.5),
        'ssm_c_im': normal((DEPTH, SSM_GROUPS, SSM_GROUP, SSM_STATE), SSM_STATE ** -0.5),
        'ssm_d': normal((DEPTH, SSM_GROUPS, SSM_GROUP), 1.0),
        'w_glu': normal((DEPTH, SSM_WIDTH, 2 * SSM_WIDTH), SSM_WIDTH ** -0.5),
        'w_ssm_proj': normal((DEPTH, SSM_WIDTH, D_MODEL), SSM_WIDTH ** -0.5),
        'cmp_pe_k': normal((DEPTH, L_CMP, HEAD_DIM), 0.02),
        'cmp_w1_k': normal((DEPTH, L_CMP * HEAD_DIM, CMP_HIDDEN), (L_CMP * HEAD_DIM) ** -0.5),
        'cmp_b1_k': normal((DEPTH, CMP_HIDDEN), 0.01),
        'cmp_w2_k': normal((DEPTH, CMP_HIDDEN, HEAD_DIM), CMP_HIDDEN ** -0.5),
        'cmp_pe_v': normal((DEPTH, L_CMP, HEAD_DIM), 0.02),
        'cmp_w1_v': normal((DEPTH, L_CMP * HEAD_DIM, CMP_HIDDEN), (L_CMP * HEAD_DIM) ** -0.5),
        'cmp_b1_v': normal((DEPTH, CMP_HIDDEN), 0.01),
        'cmp_w2_v': normal((DEPTH, CMP_HIDDEN, HEAD_DIM), CMP_HIDDEN ** -0.5),
        'w_attn_proj': normal((DEPTH, Q_DIM, D_MODEL), Q_DIM ** -0.5),
        'w_out': normal((DEPTH, D_MODEL, D_MODEL), D_MODEL ** -0.5),
        'g_ffn': 1.0 + normal((DEPTH, D_MODEL), 0.01),
        'w_router_group': normal((DEPTH, D_MODEL, N_EXPERT_GROUPS), D_MODEL ** -0.5),
        'b_router_group': normal((DEPTH, N_EXPERT_GROUPS), 0.01),
        'w_router_expert': normal((DEPTH, D_MODEL, N_EXPERTS), D_MODEL ** -0.5),
        'b_router_expert': normal((DEPTH, N_EXPERTS), 0.01),
        'w_exp_gate': normal((DEPTH, N_EXPERTS, D_MODEL, D_EXPERT), D_MODEL ** -0.5),
        'w_exp_up': normal((DEPTH, N_EXPERTS, D_MODEL, D_EXPERT), D_MODEL ** -0.5),
        'w_exp_down': normal((DEPTH, N_EXPERTS, D_EXPERT, D_MODEL), D_EXPERT ** -0.5),
        'g_final': 1.0 + normal((D_MODEL,), 0.01),
    }

def reference(x_prompt, x_sample, cache_kv, cache_win, state_ssm, page_table,
              g_mix, w_in, ssm_a_re, ssm_a_im, ssm_log_dt, ssm_b_re, ssm_b_im, ssm_c_re, ssm_c_im,
              ssm_d, w_glu, w_ssm_proj, cmp_pe_k, cmp_w1_k, cmp_b1_k, cmp_w2_k,
              cmp_pe_v, cmp_w1_v, cmp_b1_v, cmp_w2_v, w_attn_proj, w_out, g_ffn,
              w_router_group, b_router_group, w_router_expert, b_router_expert,
              w_exp_gate, w_exp_up, w_exp_down, g_final):
    xp, xs = x_prompt, x_sample
    kv_p, kv_s, win_p, win_s, ssm_p, ssm_s = [], [], [], [], [], []
    for l in range(DEPTH):
        p = {
            'g_mix': g_mix[l], 'w_in': w_in[l],
            'ssm_a_re': ssm_a_re[l], 'ssm_a_im': ssm_a_im[l], 'ssm_log_dt': ssm_log_dt[l],
            'ssm_b_re': ssm_b_re[l], 'ssm_b_im': ssm_b_im[l], 'ssm_c_re': ssm_c_re[l], 'ssm_c_im': ssm_c_im[l],
            'ssm_d': ssm_d[l], 'w_glu': w_glu[l], 'w_ssm_proj': w_ssm_proj[l],
            'cmp_pe_k': cmp_pe_k[l], 'cmp_w1_k': cmp_w1_k[l], 'cmp_b1_k': cmp_b1_k[l], 'cmp_w2_k': cmp_w2_k[l],
            'cmp_pe_v': cmp_pe_v[l], 'cmp_w1_v': cmp_w1_v[l], 'cmp_b1_v': cmp_b1_v[l], 'cmp_w2_v': cmp_w2_v[l],
            'w_attn_proj': w_attn_proj[l], 'w_out': w_out[l], 'g_ffn': g_ffn[l],
            'w_router_group': w_router_group[l], 'b_router_group': b_router_group[l],
            'w_router_expert': w_router_expert[l], 'b_router_expert': b_router_expert[l],
            'w_exp_gate': w_exp_gate[l], 'w_exp_up': w_exp_up[l], 'w_exp_down': w_exp_down[l],
        }
        xp, kv_rows_p, win_rows_p, h_p = prompt_layer(xp, p)
        xs, kv_rows_s, win_rows_s, h_s = sample_layer(xs, cache_kv, l, cache_win[l], state_ssm[l], page_table, p)
        kv_p.append(kv_rows_p)
        kv_s.append(kv_rows_s)
        win_p.append(win_rows_p)
        win_s.append(win_rows_s)
        ssm_p.append(h_p)
        ssm_s.append(h_s)
    y_prompt = rms_norm(xp, g_final)
    y_sample = rms_norm(xs, g_final)
    kv_prompt, kv_sample = jnp.stack(kv_p), jnp.stack(kv_s)
    win_prompt, win_sample = jnp.stack(win_p), jnp.stack(win_s)
    ssm_prompt, ssm_sample = jnp.stack(ssm_p), jnp.stack(ssm_s)
    return (y_prompt, y_sample, kv_prompt, kv_sample, win_prompt, win_sample, ssm_prompt, ssm_sample)


_drawn_inputs = setup_inputs


def setup_inputs(seed=0):
    import zlib

    import numpy as np

    out = dict(_drawn_inputs(seed))
    spreads = {}
    factors = {'g_mix': 5.673,
     'ssm_a_re': 15.489,
     'cmp_pe_k': 8.0,
     'cmp_b1_k': 34.863,
     'cmp_pe_v': 27.923,
     'cmp_b1_v': 64.0,
     'b_router_group': 29.018,
     'g_final': 28.521,
     'ssm_c_re': 3.268,
     'ssm_c_im': 3.344,
     'g_ffn': 8.0,
     'b_router_expert': 8.0}
    for name, (base, spread) in spreads.items():
        noise = np.random.default_rng([zlib.crc32(name.encode()), seed]).standard_normal(out[name].shape)
        drawn = base * np.exp(spread * noise) if base else spread * noise
        out[name] = jnp.asarray(drawn.astype(out[name].dtype))
    for name, factor in factors.items():
        out[name] = (out[name] * factor).astype(out[name].dtype)
    return out
```

```python
from contextlib import ExitStack

import numpy as np

import concourse.bass as bass
from concourse import mybir

F32 = mybir.dt.float32
I32 = mybir.dt.int32
U32 = mybir.dt.uint32
ALU = mybir.AluOpType
ACT = mybir.ActivationFunctionType
AX = mybir.AxisListType.X

P = 128
D = 1024
KD = D // P
SEQ = 512
NB, NT = 8, 8
TOK = SEQ + NB * NT
HALF = TOK // 2
TILES = 5
ROWS = [P, P, P, P, NB * NT]
PAST = 1024
PAGE = 128
PAGES = PAST // PAGE
POOL = 80
SW = 512
GROUPS = 32
ST = 16
CH = 8
PCH = SEQ // CH
NCH = PCH + NB
HD = 64
HG = 4
QKV = 512 + 768
ZW = SW + QKV + 24
ZQ, ZK, ZG = SW, SW + 512, SW + QKV
CHUNKS = [(0, 512), (512, 512), (1024, 512), (1536, 280)]
N_EXP = 32
DE = 512
KE = DE // P
BLOCKS = 42
BIG = 1 << 20
NEG = -1.0e30
EPS = 1e-6
SCALE = HD ** -0.5
TWO_PI = 2 * np.pi
GELU_A = 0.044715
GELU_B = float(np.sqrt(2 / np.pi))

CONST = {
    "ident": P, "ones": P, "tri": P, "causal": P, "same": P, "cos": TILES * 32, "sin": TILES * 32,
    "cmask": 4 * 32, "newmask": 4 * 64, "winmask": 8, "expand": 4 * P, "headpick": 8, "eye7": 16,
    "blk17": 17, "force17": 17, "desc4": 4, "desc32": 32, "valid": TILES, "blkno": BLOCKS,
}
COFF, _o = {}, 0
for _n, _w in CONST.items():
    COFF[_n] = _o
    _o += _w
CW = _o


def constants():
    r = np.arange(P)
    c = {n: np.zeros((P, w), np.float32) for n, w in CONST.items()}
    c["ident"][:] = np.eye(P)
    c["ones"][:] = 1
    c["tri"][:] = r[:, None] < r[None, :]
    c["causal"][:] = np.where(r[None, :] <= r[:, None], 0, NEG)
    b2, g, hg, t = r // 64, r // 32 % 2, r // 8 % 4, r % 8
    c["same"][:] = (b2[:, None] == b2) & (g[:, None] == g) & (t[:, None] == t)
    pos = np.concatenate([np.arange(SEQ), PAST + np.arange(64) % 8, np.zeros(64)]).reshape(TILES, P)
    inv = np.float32(10000.0) ** (-np.arange(32, dtype=np.float32) / np.float32(32))
    ang = (pos.astype(np.float32)[:, :, None] * inv.astype(np.float32)).astype(np.float32)
    c["cos"][:] = np.cos(ang.astype(np.float64)).transpose(1, 0, 2).reshape(P, -1)
    c["sin"][:] = np.sin(ang.astype(np.float64)).transpose(1, 0, 2).reshape(P, -1)
    q = np.arange(4)[None, :, None] * P + r[:, None, None]
    j = np.arange(32)
    c["cmask"][:] = np.where((j * 16 + 31 <= q) & (j < 31), 0, NEG).reshape(P, -1)
    s = np.arange(64)
    bp = np.arange(4)[None, :, None]
    ok = (s // 8 == 2 * bp + b2[:, None, None]) & (s % 8 <= t[:, None, None])
    c["newmask"][:] = np.where(ok, 0, NEG).reshape(P, -1)
    c["winmask"][:] = np.where(np.arange(8)[None, :] > t[:, None], 0, NEG)
    e = (np.arange(64)[:, None, None] // 8 == 2 * bp + b2[None, None, :]) & (np.arange(64)[:, None, None] % 8 == t)
    c["expand"][:64] = e.reshape(64, -1)
    c["headpick"][:] = (g * 4 + hg)[:, None] == np.arange(8)
    c["eye7"][:] = r[:, None] == 112 + np.arange(16)
    c["blk17"][:] = 1 + np.arange(17)
    c["force17"][:] = np.isin(np.arange(17), [0, 15, 16])
    c["desc4"][:] = 4 - np.arange(4)
    c["desc32"][:] = 32 - np.arange(32)
    c["valid"][:] = np.arange(TILES) * P + r[:, None] < TOK
    c["blkno"][:] = np.arange(BLOCKS)
    return np.concatenate([c[n] for n in CONST], 1)


class Steps:

    def __init__(self, sem):
        self.sem, self.n = sem, 0

    def on(self, eng):
        def link(ins):
            self.n += 1
            ins.then_inc(self.sem, 1)
            eng.wait_ge(self.sem, self.n)
        return link


class Core:
    pass


class Region:

    def __init__(self, arena, start, end):
        self.arena, self.pos, self.end = arena, start, end

    def take(self, shape, dt=F32):
        n = int(np.prod(shape[1:]))
        ap = self.arena[0:shape[0], self.pos:self.pos + n]
        self.pos += n
        assert self.pos <= self.end, (self.pos, self.end)
        if dt is not F32:
            ap = ap.bitcast(dt)
        names = "abcdef"[:len(shape) - 1]
        if len(names) > 1:
            ap = ap.rearrange(f"p ({' '.join(names)}) -> p {' '.join(names)}", **dict(zip(names, shape[1:])))
        return ap


AT_Z4 = 4992
AT_Z = AT_Z4 + ZW
AT_SSM = AT_Z + TILES * ZW
AT_KT = AT_SSM + GROUPS * NCH
AT_XM = AT_KT + 2 * 4096
AT_AT = AT_XM + 2 * ST * NCH
AT_STATE = AT_AT + 4 * TOK
AT_LOCAL = AT_STATE + (NCH + 1) * 2 * ST + NCH * 2 * ST
AT_END = 53100


def project(nc, c):
    with ExitStack() as ctx:
        region = Region(c.arena, AT_SSM, AT_END)
        def sem(name):
            return c.sem("project_" + name)

        xT = region.take([P, KD, TOK])
        gcol = region.take([P, KD])
        w = region.take([P, 3, KD, 512])
        x = region.take([P, TILES, D])
        sg = region.take([P, 4, TOK])
        junk = region.take([P, D])
        ss = region.take([P, TILES])
        rinv = region.take([P, TILES])
        diag = region.take([P, TILES, P])
        rinv_row = region.take([P, TOK])
        rt = region.take([P, 4, 512])

        consts_in, x_in, xT_in = sem("consts_in"), sem("x_in"), sem("xT_in")
        w_in = [sem(f"w_in{i}") for i in range(3)]
        xg_ready, square_done, diag_ready, row_ps, row_ready = (
            sem("xg_ready"), sem("square_done"), sem("diag_ready"), sem("row_ps"), sem("row_ready"))
        rinv_ready, tail_zero = sem("rinv_ready"), sem("tail_zero")
        tok_ps, tok_out, chan_ps, chan_scaled, chan_tanh = (
            sem("tok_ps"), sem("tok_out"), sem("chan_ps"), sem("chan_scaled"), sem("chan_tanh"))
        gates_ready, roped, stored = sem("gates_tanh"), sem("roped"), sem("stored")
        gate_ready, mean_ready, root_done = sem("gate_ready"), sem("mean_ready"), sem("root_done")
        gate_stored = [sem(f"gate_stored{i}") for i in range(4)]
        NTU = 4 * TILES

        block = ctx.enter_context(nc.Block())

        @block.sync
        def _(sp):
            sp.dma_start(xT[:], c.d["xT"]).then_inc(xT_in, 16)
            sp.dma_start(gcol[:], c.d["g_mix"]).then_inc(xT_in, 16)
            for n in range(8):
                if 3 <= n < 7:
                    sp.wait_ge(tok_ps, TILES * (n - 2))
                elif n == 7:
                    sp.wait_ge(chan_ps, 8)
                if n < 4:
                    width = CHUNKS[n][1]
                    src = c.d["w_tok"][n] if n < 3 else c.d["w_tail"]
                    sp.dma_start(w[:, n % 3, :, 0:width], src).then_inc(w_in[n % 3], 16)
                else:
                    sp.dma_start(w[:, n % 3], c.d["w_chan"][n - 4]).then_inc(w_in[n % 3], 16)
                if n == 0:
                    sp.dma_start(c.K[:], c.d["consts"]).then_inc(consts_in, 16)
                    for dst, name in ((c.w1, "cmp_w1"), (c.w2, "cmp_w2"), (c.pe, "cmp_pe"), (c.b1, "cmp_b1")):
                        sp.dma_start(dst[:], c.d[name]).then_inc(c.w1_in, 16)
                    sp.dma_start(x[:, 0:4, :], c.d["x"][0:SEQ].rearrange("(i p) d -> p i d", p=P)).then_inc(x_in, 16)
                    sp.dma_start(x[0:64, 4, :], c.d["x"][SEQ:TOK]).then_inc(x_in, 16)
            sp.wait_ge(tok_out, TILES)
            sp.dma_start(c.d["u"][0:SEQ].rearrange("(i p) d -> p i d", p=P), c.z[:, 0:4, 0:SW]).then_inc(stored, 16)
            sp.dma_start(c.d["u"][SEQ:TOK], c.z[0:64, 4, 0:SW]).then_inc(stored, 16)
            sp.wait_ge(roped, TILES)
            sp.wait_ge(tok_out, NTU)
            kv = c.z[:, :, ZK:ZK + 512]
            win = c.z[:, :, ZK + 512:ZK + 768]
            sp.dma_start(c.o["kv"][0:SEQ].rearrange("(i p) d -> p i d", p=P), kv[:, 0:4]).then_inc(stored, 16)
            sp.dma_start(c.o["kv"][SEQ:TOK], kv[0:64, 4]).then_inc(stored, 16)
            sp.dma_start(c.o["win_p"].rearrange("(i p) d -> p i d", p=P), win[:, 0:4]).then_inc(stored, 16)
            for b in range(NB):
                sp.dma_start(c.o["win_s"][b, SEQ - NT:SEQ], win[b * NT:(b + 1) * NT, 4]).then_inc(stored, 16)
            sp.dma_start(c.o["win_s"][:, 0:SEQ - NT], c.d["win_rows"][:, NT:SEQ]).then_inc(stored, 16)
            for m in range(16):
                sp.wait_ge(gate_ready, m + 1)
                sp.dma_start(c.d["sig"][m], sg[:, m % 4]).then_inc(gate_stored[m % 4], 16)
            for i in range(4):
                sp.wait_ge(gate_stored[i], 64)
            sp.wait_ge(stored, 16 * (5 + NB + 1))

        @block.scalar
        def _(act):
            act.wait_ge(x_in, 32)
            act.wait_ge(tail_zero, 1)
            for i in range(TILES):
                if i:
                    act.wait_ge(square_done, i)
                act.activation(junk[:], x[:, i, :], ACT.Square, accum_out=ss[:, i:i + 1]).then_inc(square_done, 1)
            act.wait_ge(mean_ready, 1)
            act.activation(ss[:], ss[:], ACT.Sqrt).then_inc(root_done, 1)
            act.wait_ge(rinv_ready, 1)
            for n in range(NTU):
                j, i = n // TILES, n % TILES
                r, (at, width) = ROWS[i], CHUNKS[j]
                act.wait_ge(tok_ps, n + 1)
                act.activation(c.z[0:r, i, at:at + width], c.ps[0:r, n % 4, 0:width], ACT.Copy,
                               scale=rinv[0:r, i:i + 1]).then_inc(tok_out, 1)
            act.wait_ge(tok_out, NTU)
            act.activation(c.gate[:], c.z[:, :, ZG:ZW], ACT.Tanh, scale=0.5).then_inc(gates_ready, 1)
            for m in range(16):
                act.wait_ge(chan_scaled, 2 * m + 2)
                act.activation(sg[:, m % 4], sg[:, m % 4], ACT.Tanh, scale=0.5).then_inc(chan_tanh, 1)

        @block.tensor
        def _(pe):
            pe.wait_ge(xg_ready, KD)
            for n in range(NTU):
                j, i = n // TILES, n % TILES
                r, width = ROWS[i], CHUNKS[j][1]
                if i == 0:
                    pe.wait_ge(w_in[j % 3], 16 * (j // 3 + 1))
                if n >= 4:
                    pe.wait_ge(tok_out, n - 3)
                for k in range(KD):
                    mm = pe.matmul(c.ps[0:r, n % 4, 0:width], xT[:, k, i * P:i * P + r], w[:, j % 3, k, 0:width],
                                   start=k == 0, stop=k == KD - 1)
                mm.then_inc(tok_ps, 1)
            pe.wait_ge(diag_ready, 1)
            pe.wait_ge(consts_in, 16)
            for i in range(TILES):
                r = ROWS[i]
                mm = pe.matmul(c.ps[:, 4 + i // 4, i % 4 * P:i % 4 * P + r], c.k("ones")[0:r], diag[0:r, i, 0:r],
                               start=True, stop=True)
            mm.then_inc(row_ps, 1)
            for m in range(16):
                n = 4 + m // 4
                if m % 4 == 0:
                    pe.wait_ge(w_in[n % 3], 16 * (n // 3 + 1))
                for h in range(2):
                    v = 2 * m + h
                    if v >= 4:
                        pe.wait_ge(chan_scaled, v - 3)
                    else:
                        pe.wait_ge(tok_out, NTU)
                    for k in range(KD):
                        mm = pe.matmul(c.ps[:, v % 4, 0:HALF], w[:, n % 3, k, m % 4 * P:(m % 4 + 1) * P],
                                       xT[:, k, h * HALF:(h + 1) * HALF], start=k == 0, stop=k == KD - 1)
                    mm.then_inc(chan_ps, 1)

        @block.vector
        def _(dve):
            link = c.vsteps.on(dve)

            def finish_gate(m):
                dve.wait_ge(chan_tanh, m + 1)
                dve.tensor_scalar(sg[:, m % 4], sg[:, m % 4], 0.5, 0.5, ALU.mult, ALU.add).then_inc(gate_ready, 1)

            dve.memset(x[64:P, 4, :], 0.0).then_inc(tail_zero, 1)
            dve.memset(c.z[64:P, 4, :], 0.0)
            dve.wait_ge(xT_in, 32)
            for k in range(KD):
                dve.tensor_scalar(xT[:, k], xT[:, k], gcol[:, k:k + 1], None, ALU.mult).then_inc(xg_ready, 1)
            dve.wait_ge(square_done, TILES)
            dve.tensor_scalar(ss[:], ss[:], 1.0 / D, EPS, ALU.mult, ALU.add).then_inc(mean_ready, 1)
            dve.wait_ge(root_done, 1)
            dve.reciprocal(rinv[:], ss[:]).then_inc(rinv_ready, 1)
            dve.wait_ge(rinv_ready, 1)
            dve.wait_ge(consts_in, 16)
            for i in range(TILES):
                ins = dve.tensor_scalar(diag[:, i], c.k("ident"), rinv[:, i:i + 1], None, ALU.mult)
            ins.then_inc(diag_ready, 1)
            dve.wait_ge(row_ps, 1)
            link(dve.tensor_copy(rinv_row[:, 0:512], c.ps[:, 4, :]))
            link(dve.tensor_copy(rinv_row[:, 512:TOK], c.ps[:, 5, 0:64]))
            dve.wait_ge(gates_ready, 1)
            link(dve.tensor_scalar(c.gate[:], c.gate[:], 0.5, 0.5, ALU.mult, ALU.add))
            for m in range(16):
                for h in range(2):
                    v = 2 * m + h
                    dve.wait_ge(chan_ps, v + 1)
                    if m >= 4:
                        dve.wait_ge(gate_stored[m % 4], 16 * (m // 4))
                    dve.tensor_tensor(sg[:, m % 4, h * HALF:(h + 1) * HALF], c.ps[:, v % 4, 0:HALF],
                                      rinv_row[:, h * HALF:(h + 1) * HALF], ALU.mult).then_inc(chan_scaled, 1)
                if m >= 1:
                    finish_gate(m - 1)
            finish_gate(15)

        @block.gpsimd
        def _(pool):
            link = c.gsteps.on(pool)
            pool.wait_ge(consts_in, 16)
            for i in range(TILES):
                pool.wait_ge(tok_out, 3 * TILES + i + 1)
                co = c.k("cos")[:, i * 32:(i + 1) * 32]
                si = c.k("sin")[:, i * 32:(i + 1) * 32]
                q = c.z[:, i, ZQ:ZQ + 512].rearrange("p (h f d) -> p h f d", f=2, d=32)
                kk = c.z[:, i, ZK:ZK + 768].rearrange("p (s v g f d) -> p s v g f d", s=3, v=2, g=2, f=2)
                parts = [(q[:, :, 0], q[:, :, 1], 8)]
                parts += [(kk[:, s, 0, :, 0], kk[:, s, 0, :, 1], 2) for s in range(3)]
                for lo, hi, n in parts:
                    cb = co.unsqueeze(1).broadcast_to([P, n, 32])
                    sb_ = si.unsqueeze(1).broadcast_to([P, n, 32])
                    t = [rt[:, a, 0:n * 32].rearrange("p (h d) -> p h d", d=32) for a in range(4)]
                    pool.tensor_tensor(t[0], lo, cb, ALU.mult)
                    pool.tensor_tensor(t[1], hi, sb_, ALU.mult)
                    pool.tensor_tensor(t[2], hi, cb, ALU.mult)
                    link(pool.tensor_tensor(t[3], lo, sb_, ALU.mult))
                    pool.tensor_tensor(lo, t[0], t[1], ALU.subtract)
                    link(pool.tensor_tensor(hi, t[2], t[3], ALU.add))
                pool.engine_nop().then_inc(roped, 1)


def ssm_build(nc, c):
    with ExitStack() as ctx:
        region = Region(c.arena, AT_LOCAL, AT_END)
        def sem(name):
            return c.sem("ssm_build_" + name)

        raw = region.take([P, 3, ST])
        b = region.take([P, 2, ST, 16])
        cc = region.take([P, 2, ST, 16])
        dd = region.take([P, GROUPS, 16])
        v = region.take([P, 14, ST])
        vi = region.take([P, ST], I32)
        pw = region.take([P, 2, 9, ST])
        tw = region.take([P, 4, 4, ST])
        bb = region.take([P, 2, ST, 16])
        t4 = region.take([P, 2, 1024])
        u_rows = Region(c.arena, region.pos, AT_END).take([NCH, CH, GROUPS, 16])
        Z = region.take([P, 2, ST, CH, 16])
        ch = Region(c.arena, region.pos, AT_END).take([NCH, GROUPS, CH * 16])
        wt = region.take([P, 2, ST, P])
        mt = region.take([P, GROUPS * 16])

        par_in, u_in, u_grouped = sem("par_in"), sem("u_in"), sem("u_grouped")
        dt_exp, mag_exp, sin_ready, sin_done, z_ready = (
            sem("dt_exp"), sem("mag_exp"), sem("sin_ready"), sem("sin_done"), sem("z_ready"))
        tr_ps, tr_out, mt_ps, mt_ready, kt_zero, kt_in, st_ps, st_out, h0_in = (
            sem("tr_ps"), sem("tr_out"), sem("mt_ps"), sem("mt_ready"), sem("kt_zero"), sem("kt_in"),
            sem("st_ps"), sem("st_out"), sem("h0_in"))
        UB = 4
        NU = GROUPS // UB
        NZ = 2 * ST // 4

        block = ctx.enter_context(nc.Block())

        @block.sync
        def _(sp):
            sp.dma_start(raw[:], c.d["ssm_par"]).then_inc(par_in, 16)
            sp.dma_start(b[:], c.d["ssm_b"]).then_inc(par_in, 16)
            sp.dma_start(cc[:], c.d["ssm_c"]).then_inc(par_in, 16)
            sp.dma_start(dd[:], c.d["ssm_d"]).then_inc(par_in, 16)
            sp.dma_start(u_rows.rearrange("k s g e -> k (s g e)"), c.d["u"].rearrange("(k s) d -> k (s d)", s=CH)).then_inc(u_in, 16)
            sp.dma_start(c.X[:, PCH + 1:PCH + 1 + NB], c.d["state"]).then_inc(h0_in, 16)
            sp.wait_ge(mt_ready, 2)
            sp.wait_ge(kt_zero, 1)
            for t in range(CH):
                sp.dma_start(c.KT[0:16 * (t + 1), t, :], mt[16 * (CH - 1 - t):P, :]).then_inc(kt_in, 16)
            sp.wait_ge(kt_in, 16 * CH)
            sp.wait_ge(h0_in, 16)

        @block.scalar
        def _(act):
            act.wait_ge(par_in, 64)
            act.activation(v[:, 0], raw[:, 2], ACT.Exp).then_inc(dt_exp, 1)
            act.wait_ge(mag_exp, 1)
            act.activation(v[:, 2], v[:, 1], ACT.Exp).then_inc(dt_exp, 1)
            act.wait_ge(sin_ready, 1)
            act.activation(v[:, 7:9], v[:, 5:7], ACT.Sin).then_inc(sin_done, 1)
            for n in range(NU + NZ):
                act.wait_ge(tr_ps, n + 1)
                if n < NU:
                    act.activation(c.U[:, UB * n:UB * (n + 1)],
                                   c.ps[:, n % 2, 0:UB * NCH].rearrange("p (g k) -> p g k", g=UB),
                                   ACT.Copy).then_inc(tr_out, 1)
                else:
                    m = n - NU
                    dst = wt[:].rearrange("p r s q -> p (r s q)")[:, 512 * m:512 * (m + 1)]
                    act.activation(dst, c.ps[:, n % 2, :], ACT.Copy).then_inc(tr_out, 1)
            for tl in range(ST):
                act.wait_ge(st_ps, tl + 1)
                src = c.ps[:, 4 + tl % 2, 0:2 * NCH].rearrange("p (r k) -> p k r", r=2)
                act.activation(c.S[:, :, :, tl], src, ACT.Copy).then_inc(st_out, 1)

        @block.tensor
        def _(pe):
            pe.wait_ge(u_grouped, 2)
            for n in range(NU):
                if n >= 2:
                    pe.wait_ge(tr_out, n - 1)
                for a in range(UB):
                    g = UB * n + a
                    mm = pe.transpose(c.ps[:, n % 2, a * NCH:(a + 1) * NCH], ch[:, g], c.k("ident")[0:NCH, 0:NCH])
                mm.then_inc(tr_ps, 1)
            pe.wait_ge(z_ready, 1)
            zf = Z[:].rearrange("p r s k e -> p (r s) (k e)")
            for n in range(NU, NU + NZ):
                pe.wait_ge(tr_out, n - 1)
                for a in range(4):
                    mm = pe.transpose(c.ps[:, n % 2, a * P:(a + 1) * P], zf[:, 4 * (n - NU) + a], c.k("ident"))
                mm.then_inc(tr_ps, 1)
            for g in range(GROUPS):
                lo = HD * (g % 2)
                for r in range(2):
                    mm = pe.matmul(c.ps[:, 2 + g % 2, g // 2 * 16:(g // 2 + 1) * 16], zf[lo:lo + HD, r * ST + g // 2],
                                   cc[lo:lo + HD, r, g // 2], start=r == 0, stop=r == 1)
            mm.then_inc(mt_ps, 1)
            pe.wait_ge(tr_out, NU + NZ)
            for tl in range(ST):
                if tl >= 2:
                    pe.wait_ge(st_out, tl - 1)
                for r in range(2):
                    for h in range(2):
                        mm = pe.matmul(c.ps[HD * h:HD * (h + 1), 4 + tl % 2, r * NCH:(r + 1) * NCH],
                                       wt[:, r, tl, HD * h:HD * (h + 1)], c.U[:, 2 * tl + h],
                                       start=True, stop=True)
                mm.then_inc(st_ps, 1)

        @block.gpsimd
        def _(pool):
            pool.memset(c.KT[:], 0.0).then_inc(kt_zero, 1)
            pool.memset(c.X[:, 0:1], 0.0)

        @block.vector
        def _(dve):
            link = c.vsteps.on(dve)

            def mul(o, a, bb_):
                return dve.tensor_tensor(o, a, bb_, ALU.mult)

            def complex_mul(o_re, o_im, a, b_, tmp):
                mul(tmp[0], a[0], b_[0])
                mul(tmp[1], a[1], b_[1])
                mul(tmp[2], a[0], b_[1])
                link(mul(tmp[3], a[1], b_[0]))
                dve.tensor_tensor(o_re, tmp[0], tmp[1], ALU.subtract)
                link(dve.tensor_tensor(o_im, tmp[2], tmp[3], ALU.add))

            a_re, a_im = raw[:, 0], raw[:, 1]
            dve.wait_ge(u_in, 16)
            for a in range(2):
                half = slice(a * GROUPS // 2, (a + 1) * GROUPS // 2)
                dve.tensor_copy(ch[:, half].rearrange("k g (s e) -> k s g e", s=CH), u_rows[:, :, half]).then_inc(u_grouped, 1)
            dve.wait_ge(u_grouped, 2)
            dve.wait_ge(par_in, 64)
            link(dve.tensor_scalar(cc[:, 1], cc[:, 1], -1.0, None, ALU.mult))
            dve.wait_ge(dt_exp, 1)
            link(mul(v[:, 1], a_re, v[:, 0]))
            dve.engine_nop().then_inc(mag_exp, 1)
            link(mul(v[:, 3], a_im, v[:, 0]))
            link(dve.tensor_scalar(v[:, 4], v[:, 3], 1.0 / TWO_PI, None, ALU.mult))
            link(dve.tensor_copy(vi[:], v[:, 4]))
            link(dve.tensor_copy(v[:, 4], vi[:]))
            hi = 6.28125
            link(dve.scalar_tensor_tensor(v[:, 3], v[:, 4], -hi, v[:, 3], ALU.mult, ALU.add))
            link(dve.scalar_tensor_tensor(v[:, 3], v[:, 4], -(TWO_PI - hi), v[:, 3], ALU.mult, ALU.add))
            link(dve.tensor_scalar(v[:, 4], v[:, 3], float(np.pi), -TWO_PI, ALU.is_gt, ALU.mult))
            link(dve.tensor_tensor(v[:, 3], v[:, 3], v[:, 4], ALU.add))
            link(dve.tensor_scalar(v[:, 4], v[:, 3], float(-np.pi), TWO_PI, ALU.is_lt, ALU.mult))
            link(dve.tensor_tensor(v[:, 3], v[:, 3], v[:, 4], ALU.add))
            link(dve.tensor_scalar(v[:, 5], v[:, 3], 0.5, None, ALU.mult))
            link(dve.tensor_scalar(v[:, 4], v[:, 5], -1.0, None, ALU.mult))
            link(dve.tensor_tensor(v[:, 4], v[:, 4], v[:, 5], ALU.max))
            dve.tensor_scalar(v[:, 6], v[:, 4], -1.0, float(np.pi / 2), ALU.mult, ALU.add).then_inc(sin_ready, 1)
            dve.wait_ge(sin_done, 1)
            dve.wait_ge(dt_exp, 2)
            link(mul(v[:, 9], v[:, 7], v[:, 8]))
            link(mul(v[:, 10], v[:, 7], v[:, 7]))
            link(dve.tensor_scalar(v[:, 9], v[:, 9], 2.0, None, ALU.mult))
            link(dve.tensor_scalar(v[:, 10], v[:, 10], -2.0, 1.0, ALU.mult, ALU.add))
            mul(pw[:, 0, 1], v[:, 2], v[:, 10])
            link(mul(pw[:, 1, 1], v[:, 2], v[:, 9]))
            dve.memset(pw[:, 0, 0], 1.0)
            dve.memset(pw[:, 1, 0], 0.0)
            for n in (1, 2, 4):
                a = [pw[:, r, 1:1 + n] for r in range(2)]
                m = [pw[:, r, n:n + 1].broadcast_to([P, n, ST]) for r in range(2)]
                complex_mul(pw[:, 0, n + 1:2 * n + 1], pw[:, 1, n + 1:2 * n + 1], a, m,
                            [tw[:, q, 0:n] for q in range(4)])
            link(mul(v[:, 4], a_re, a_re))
            link(mul(v[:, 5], a_im, a_im))
            link(dve.tensor_tensor(v[:, 4], v[:, 4], v[:, 5], ALU.add))
            link(dve.reciprocal(v[:, 4], v[:, 4]))
            link(dve.tensor_scalar(v[:, 5], pw[:, 0, 1], -1.0, None, ALU.add))
            mul(v[:, 6], v[:, 5], a_re)
            mul(v[:, 7], pw[:, 1, 1], a_im)
            mul(v[:, 8], pw[:, 1, 1], a_re)
            link(mul(v[:, 9], v[:, 5], a_im))
            dve.tensor_tensor(v[:, 10], v[:, 6], v[:, 7], ALU.add)
            link(dve.tensor_tensor(v[:, 11], v[:, 8], v[:, 9], ALU.subtract))
            mul(v[:, 12], v[:, 10], v[:, 4])
            link(mul(v[:, 13], v[:, 11], v[:, 4]))
            f = [v[:, 12 + r].unsqueeze(2).broadcast_to([P, ST, 16]) for r in range(2)]
            tb = [t4[:, 0, q * 256:(q + 1) * 256].rearrange("p (s e) -> p s e", s=ST) for q in range(4)]
            complex_mul(bb[:, 0], bb[:, 1], f, [b[:, 0], b[:, 1]], tb)

            def powers(r, t, first, step):
                return pw[:, r, first + step * t].unsqueeze(2).broadcast_to([P, ST, 16])

            tt = [t4[:, 1, q * 256:(q + 1) * 256].rearrange("p (s e) -> p s e", s=ST) for q in range(4)]
            for s in range(CH):
                complex_mul(Z[:, 0, :, s], Z[:, 1, :, s], [powers(r, s, CH - 1, -1) for r in range(2)],
                            [bb[:, 0], bb[:, 1]], tt if s % 2 else tb)
            dve.engine_nop().then_inc(z_ready, 1)
            for t in range(CH):
                p_re, p_im = powers(0, t, 1, 1), powers(1, t, 1, 1)
                q4 = tt if t % 2 else tb
                mul(q4[0], cc[:, 0], p_re)
                mul(q4[1], cc[:, 1], p_im)
                mul(q4[2], cc[:, 1], p_re)
                link(mul(q4[3], cc[:, 0], p_im))
                dve.tensor_tensor(c.C[:, 0, :, t], q4[0], q4[1], ALU.add)
                link(dve.tensor_tensor(c.C[:, 1, :, t], q4[2], q4[3], ALU.subtract))
            dve.tensor_copy(c.A8[:, 0, 0], pw[:, 0, 8])
            dve.tensor_copy(c.A8[:, 0, 1], pw[:, 0, 8])
            dve.tensor_scalar(c.A8[:, 1, 0], pw[:, 1, 8], -1.0, None, ALU.mult)
            dve.tensor_copy(c.A8[:, 1, 1], pw[:, 1, 8])
            e7 = c.k("eye7").unsqueeze(1).broadcast_to([P, GROUPS, 16])
            link(mul(dd[:], dd[:], e7))
            dve.wait_ge(mt_ps, 1)
            for h in range(2):
                dve.tensor_tensor(mt[:].rearrange("p (s h e) -> p s h e", h=2, e=16)[:, :, h],
                                  c.ps[:, 2 + h, 0:ST * 16].rearrange("p (s e) -> p s e", e=16),
                                  dd[:].rearrange("p (s h) e -> p s h e", h=2)[:, :, h], ALU.add).then_inc(mt_ready, 1)


def prompt(nc, c):
    with ExitStack() as ctx:
        region = Region(c.arena, AT_LOCAL, AT_END)
        def sem(name):
            return c.sem("prompt_" + name)

        kT = region.take([P, 2, SEQ])
        qT = region.take([P, HG, SEQ])
        rows = region.take([32, 2, 2, 16 * HD])
        hT = region.take([P, 32, 32])
        trail = region.take([HD, 4, 32])
        hid = region.take([HD, 4, 32])
        gt = region.take([HD, 2, 4, 32])
        kc = region.take([P, 32])
        vc = region.take([32, P])
        pr = region.take([P, 4, 512])
        pt = region.take([P, 2, 512])
        st = region.take([P, 8, 4])
        at = region.take([P, 4, 512])
        sc = region.take([P, 2, 2, ST])

        rows_in, tr_ps, tr_out, cmp_ps, trail_out, hid_add, hid_scaled, hid_tanh, hid_ready, kc_ps, kc_out = (
            sem("rows_in"), sem("tr_ps"), sem("tr_out"), sem("cmp_ps"), sem("trail_out"), sem("hid_add"),
            sem("hid_scaled"), sem("hid_tanh"), sem("hid_ready"), sem("kc_ps"), sem("kc_out"))
        score_ps, bias_ready, exp_done, pt_ps, pt_out, pv_ps, unit_out, at_ps, at_out, scanned, pe_ps = (
            sem("score_ps"), sem("bias_ready"), sem("exp_done"), sem("pt_ps"), sem("pt_out"), sem("pv_ps"),
            sem("unit_out"), sem("at_ps"), sem("at_out"), sem("scanned"), sem("pe_ps"))

        work = [([c.z[:, i, ZK + 256 * (1 + s):ZK + 256 * (1 + s) + P] for i in range(4)], kT[:, s, :])
                for s in range(2)]
        for h in range(HG):
            work.append(([c.z[:, i, ZQ + h * P:ZQ + (h + 1) * P]
                          for i in range(4)], qT[:, h, :]))
        units = [(i, g, h, s) for i in range(4) for g in range(2) for h in range(HG) for s in range(3)]
        N = len(units)
        LAG = 3

        block = ctx.enter_context(nc.Block())

        @block.sync
        def _(sp):
            src = c.o["kv"][0:SEQ].rearrange("(n l) (s g d) -> n s g l d", l=16, s=4, g=2)
            for s in range(2):
                for g in range(2):
                    sp.dma_start(rows[:, s, g].rearrange("n (l d) -> n l d", l=16), src[:, s, g]).then_inc(rows_in, 16)
            sp.wait_ge(rows_in, 64)

        @block.tensor
        def _(pe):
            for n, (srcs, _) in enumerate(work):
                if n >= 2:
                    pe.wait_ge(tr_out, n - 1)
                for a, src in enumerate(srcs):
                    mm = pe.transpose(c.ps[:, n % 2, a * P:(a + 1) * P], src, c.k("ident"))
                mm.then_inc(tr_ps, 1)
            pe.wait_ge(rows_in, 64)
            for n in range(2):
                pe.wait_ge(tr_out, len(work) + n - 1)
                for g in range(2):
                    for j in range(8):
                        a = g * 8 + j
                        mm = pe.transpose(c.ps[:, n % 2, a * 32:(a + 1) * 32], rows[:, n, g, j * P:(j + 1) * P], c.k("ident")[0:32, 0:32])
                mm.then_inc(tr_ps, 1)
            pe.wait_ge(tr_out, len(work) + 2)
            pe.wait_ge(c.w1_in, 16 * 4)
            for s in range(2):
                for g in range(2):
                    for j in range(8):
                        mm = pe.matmul(c.ps[:, 2, (s * 2 + g) * 32:(s * 2 + g + 1) * 32], c.w1[:, s, j],
                                       hT[:, s * 16 + g * 8 + j], start=j == 0, stop=j == 7)
            mm.then_inc(cmp_ps, 1)
            for s in range(2):
                for a in range(16):
                    mm = pe.matmul(c.ps[0:HD, 3, 64 + s:65 + s], c.w1[:, s, a % 8, a // 8 * HD:(a // 8 + 1) * HD],
                                   c.pe[:, s, a:a + 1], start=a == 0, stop=a == 15)
            mm.then_inc(pe_ps, 1)
            pe.wait_ge(hid_ready, 1)
            for g in range(2):
                pe.matmul(c.ps[HD * g:HD * (g + 1), 3, 0:32], c.w2[:, 0], hid[:, g], start=True, stop=True)
                mm = pe.matmul(c.ps[0:32, 4, g * HD:(g + 1) * HD], hid[:, 2 + g], c.w2[:, 1], start=True, stop=True)
            mm.then_inc(kc_ps, 1)
            pe.wait_ge(kc_out, 2)
            for step in range(N + LAG + 1):
                if step < N:
                    i, g, h, s = units[step]
                    lo, n = HD * g, 32 if s == 0 else (i + 1) * P
                    if step >= 4:
                        pe.wait_ge(exp_done, step - 3)
                    k = kc[lo:lo + HD, :] if s == 0 else kT[lo:lo + HD, s - 1, 0:n]
                    pe.matmul(c.ps[:, step % 4, 0:n], qT[lo:lo + HD, h, i * P:(i + 1) * P], k,
                              start=True, stop=True).then_inc(score_ps, 1)
                u = step - LAG
                if 0 <= u < N:
                    i, g, h, s = units[u]
                    pe.wait_ge(exp_done, u + 1)
                    if u >= 2:
                        pe.wait_ge(pt_out, u - 1)
                    if s == 0:
                        mm = pe.transpose(c.ps[0:32, 4 + u % 2, 0:P], pr[:, u % 4, 0:32], c.k("ident"))
                    else:
                        for a in range(i + 1):
                            mm = pe.transpose(c.ps[:, 4 + u % 2, a * P:(a + 1) * P], pr[:, u % 4, a * P:(a + 1) * P],
                                              c.k("ident"))
                    mm.then_inc(pt_ps, 1)
                u = step - LAG - 1
                if 0 <= u < N:
                    i, g, h, s = units[u]
                    pe.wait_ge(pt_out, u + 1)
                    if u >= 2:
                        pe.wait_ge(unit_out, u - 1)
                    if s == 0:
                        mm = pe.matmul(c.ps[:, 6 + u % 2, 0:HD], pt[0:31, u % 2, 0:P], vc[0:31, g * HD:(g + 1) * HD],
                                       start=True, stop=True)
                    else:
                        col = ZK + 256 * s + P + g * HD
                        for a in range(i + 1):
                            mm = pe.matmul(c.ps[:, 6 + u % 2, 0:HD], pt[:, u % 2, a * P:(a + 1) * P],
                                           c.z[:, a, col:col + HD], start=a == 0, stop=a == i)
                    mm.then_inc(pv_ps, 1)
            for n in range(4):
                if n == 0:
                    pe.wait_ge(unit_out, N)
                if n >= 2:
                    pe.wait_ge(at_out, n - 1)
                for i in range(4):
                    mm = pe.transpose(c.ps[:, n % 2, i * P:(i + 1) * P], at[:, i, n * P:(n + 1) * P], c.k("ident"))
                mm.then_inc(at_ps, 1)

        @block.scalar
        def _(act):
            for n, (_, dst) in enumerate(work):
                act.wait_ge(tr_ps, n + 1)
                act.activation(dst, c.ps[:, n % 2, :], ACT.Copy).then_inc(tr_out, 1)
            for n in range(2):
                act.wait_ge(tr_ps, len(work) + n + 1)
                act.activation(hT[:, n * 16:(n + 1) * 16], c.ps[:, n % 2, :].rearrange("p (a n) -> p a n", n=32),
                               ACT.Copy).then_inc(tr_out, 1)
            act.wait_ge(cmp_ps, 1)
            for s in range(2):
                act.activation(trail[:, 2 * s:2 * s + 2], c.ps[HD:P, 2, s * 64:(s + 1) * 64].rearrange("p (g n) -> p g n", g=2),
                               ACT.Copy).then_inc(trail_out, 1)
            act.wait_ge(hid_scaled, 1)
            act.activation(gt[:, 1, :, 0:31], gt[:, 0, :, 0:31], ACT.Tanh, scale=GELU_B).then_inc(hid_tanh, 1)
            act.wait_ge(kc_ps, 1)
            act.activation(kc[:], c.ps[:, 3, 0:32], ACT.Copy).then_inc(kc_out, 1)
            act.activation(vc[:], c.ps[0:32, 4, 0:P], ACT.Copy).then_inc(kc_out, 1)
            for step in range(N + LAG):
                if step < N:
                    i, g, h, s = units[step]
                    n = 32 if s == 0 else (i + 1) * P
                    act.wait_ge(bias_ready, step + 1)
                    if step >= 4:
                        act.wait_ge(pt_ps, step - 3)
                    if step >= 8:
                        act.wait_ge(unit_out, step - 7)
                    act.activation(pr[:, step % 4, 0:n], c.ps[:, step % 4, 0:n], ACT.Exp, bias=st[:, step % 8, 1:2],
                                   scale=SCALE, accum_out=st[:, step % 8, 2:3]).then_inc(exp_done, 1)
                u = step - LAG
                if u >= 0:
                    i, g, h, s = units[u]
                    act.wait_ge(pt_ps, u + 1)
                    if u >= 2:
                        act.wait_ge(pv_ps, u - 1)
                    r, n = (32, P) if s == 0 else (P, (i + 1) * P)
                    act.activation(pt[0:r, u % 2, 0:n], c.ps[0:r, 4 + u % 2, 0:n], ACT.Copy).then_inc(pt_out, 1)
            for n in range(4):
                act.wait_ge(at_ps, n + 1)
                act.activation(c.aT[:, n, 0:SEQ], c.ps[:, n % 2, :], ACT.Copy).then_inc(at_out, 1)

        @block.vector
        def _(dve):
            link = c.vsteps.on(dve)
            dve.tensor_copy(c.z4[:], c.z[:, 4])
            dve.wait_ge(pe_ps, 1)
            link(dve.tensor_tensor(c.b1[:], c.b1[:], c.ps[0:HD, 3, 64:66], ALU.add))
            dve.wait_ge(trail_out, 2)
            link(dve.memset(hid[:], 0.0))
            gelu_hidden(dve, link, c.b1, hid[:, :, 0:31],
                        c.ps[0:HD, 2, 0:P].rearrange("p (a n) -> p a n", a=4)[:, :, 0:31],
                        trail[:, :, 1:32], gt[:, :, :, 0:31], lambda ins: ins.then_inc(hid_scaled, 1),
                        lambda: dve.wait_ge(hid_tanh, 1))
            dve.engine_nop().then_inc(hid_ready, 1)
            for step in range(N + LAG + 1):
                if step < N:
                    i, g, h, s = units[step]
                    n = 32 if s == 0 else (i + 1) * P
                    dve.wait_ge(score_ps, step + 1)
                    S = c.ps[:, step % 4]
                    if s == 0:
                        link(dve.tensor_tensor(S[:, 0:32], S[:, 0:32], c.k("cmask")[:, i * 32:(i + 1) * 32], ALU.add))
                    else:
                        link(dve.tensor_tensor(S[:, i * P:n], S[:, i * P:n], c.k("causal"), ALU.add))
                    if step >= 4:
                        dve.wait_ge(exp_done, step - 3)
                    link(dve.tensor_reduce(st[:, step % 8, 0:1], S[:, 0:n], AX, ALU.max))
                    dve.tensor_scalar(st[:, step % 8, 1:2], st[:, step % 8, 0:1], -1.0e25, -SCALE, ALU.max,
                                      ALU.mult).then_inc(bias_ready, 1)
                u = step - LAG - 1
                if 0 <= u < N:
                    i, g, h, s = units[u]
                    head = g * HG + h
                    dve.wait_ge(exp_done, u + 1)
                    link(dve.tensor_scalar(st[:, u % 8, 3:4], st[:, u % 8, 2:3], 1.0e-30, None, ALU.max))
                    link(dve.reciprocal(st[:, u % 8, 3:4], st[:, u % 8, 3:4]))
                    link(dve.tensor_tensor(st[:, u % 8, 3:4], st[:, u % 8, 3:4], c.gate[:, i, head * 3 + s:head * 3 + s + 1],
                                           ALU.mult))
                    dve.wait_ge(pv_ps, u + 1)
                    o = at[:, i, head * HD:(head + 1) * HD]
                    if s == 0:
                        dve.tensor_scalar(o, c.ps[:, 6 + u % 2, 0:HD], st[:, u % 8, 3:4], None,
                                          ALU.mult).then_inc(unit_out, 1)
                    else:
                        dve.wait_ge(unit_out, u)
                        dve.scalar_tensor_tensor(o, c.ps[:, 6 + u % 2, 0:HD], st[:, u % 8, 3:4], o, ALU.mult,
                                                 ALU.add).then_inc(unit_out, 1)

        @block.gpsimd
        def _(pool):
            link = c.gsteps.on(pool)
            for k in range(PCH):
                x = c.X[:, k]
                pool.tensor_tensor(sc[:, 0], c.A8[:, 0], x, ALU.mult)
                link(pool.tensor_tensor(sc[:, 1], c.A8[:, 1], x[:, ::-1], ALU.mult))
                link(pool.tensor_tensor(sc[:, 0], sc[:, 0], c.S[:, k], ALU.add))
                link(pool.tensor_tensor(c.X[:, k + 1], sc[:, 0], sc[:, 1], ALU.add))
            pool.tensor_copy(c.XM[:, :, :, 0:PCH], c.X[:, 0:PCH].rearrange("p k r s -> p r s k"))
            pool.tensor_copy(c.XM[:, :, :, PCH:NCH], c.X[:, PCH + 1:PCH + 1 + NB].rearrange("p k r s -> p r s k"))
            pool.tensor_copy(c.fin[:, 0], c.X[:, PCH])
            for b in range(NB):
                x = c.X[:, PCH + 1 + b]
                pool.tensor_tensor(sc[:, 0], c.A8[:, 0], x, ALU.mult)
                link(pool.tensor_tensor(sc[:, 1], c.A8[:, 1], x[:, ::-1], ALU.mult))
                link(pool.tensor_tensor(sc[:, 0], sc[:, 0], c.S[:, PCH + b], ALU.add))
                link(pool.tensor_tensor(c.fin[:, 1 + b], sc[:, 0], sc[:, 1], ALU.add))
            pool.dma_start(c.o["ssm"], c.fin[:].rearrange("p k r s -> p (k r s)")).then_inc(scanned, 16)
            pool.wait_ge(scanned, 16)


def gelu_hidden(dve, link, bias, out, lead, trail, tmp, scaled, wait_tanh):
    n = out.shape[1] // 2
    for s in range(2):
        link(dve.scalar_tensor_tensor(out[:, s * n:(s + 1) * n], lead[:, s * n:(s + 1) * n], bias[:, s:s + 1],
                                      trail[:, s * n:(s + 1) * n], ALU.add, ALU.add))
    gelu_tail(dve, link, out, out, tmp[:, 0], tmp[:, 1], scaled, wait_tanh)


def gelu_tail(dve, link, out, x, t, e, scaled, wait_tanh):
    link(dve.tensor_tensor(t, x, x, ALU.mult))
    link(dve.tensor_scalar(t, t, GELU_A, 1.0, ALU.mult, ALU.add))
    scaled(dve.tensor_tensor(t, t, x, ALU.mult))
    wait_tanh()
    link(dve.tensor_scalar(e, e, 0.5, 0.5, ALU.mult, ALU.add))
    link(dve.tensor_tensor(out, x, e, ALU.mult))


def sample(nc, c):
    with ExitStack() as ctx:
        region = Region(c.arena, AT_STATE, AT_END)
        def sem(name):
            return c.sem("sample_" + name)

        NP = NB // 2
        pgt = region.take([1, NB * PAGES], I32)
        pg = [Region(c.arena, AT_Z, AT_SSM).take([P, 2 * PAGES, 4, P]), region.take([P, 2 * PAGES, 4, P])]
        wk = region.take([P, 2, 2, SEQ])
        wv = region.take([P, 2, 2, 4, P])
        qs = region.take([P, HG, 64])
        kn = region.take([P, 2, 64])
        qb = region.take([P, NB, 2, HG, NT])
        trail = region.take([HD, 4, P])
        hid = region.take([HD, 4, P])
        gt = region.take([HD, 2, 4, P])
        kc = region.take([P, P])
        vc = region.take([63, 2, P])
        S = region.take([P, 1088 + 576])
        pc = region.take([P, 64])
        imp = region.take([P, 70])
        half = region.take([P, 68])
        b17 = region.take([P, 6, 17])
        s1 = region.take([P, 16])
        gb = region.take([P, 3, 8])
        gsel = region.take([P, 3])
        pt = region.take([P, 16 * P])
        o = region.take([P, 2 * HD])

        imp_out = sem("imp_out")
        table_in, small_ps, small_out, qb_zero = (
            sem("table_in"), sem("small_ps"), sem("small_out"), sem("qb_zero"))
        pages_in = [sem(f"pages_in{i}") for i in range(2)]
        cmp_ps, trail_out, hid_scaled, hid_tanh, hid_ready, kc_ps, kc_out = (
            sem("s_cmp_ps"), sem("s_trail_out"), sem("s_hid_scaled"), sem("s_hid_tanh"), sem("s_hid_ready"),
            sem("s_kc_ps"), sem("s_kc_out"))
        wide_ps, sc_ps, bias_c, exp_c, pc_ready, imp_ps, pct_ps, pct_out = (
            sem("wide_ps"), sem("sc_ps"), sem("bias_c"), sem("exp_c"), sem("pc_ready"),
            sem("imp_ps"), sem("pct_ps"), sem("pct_out"))
        bias_w, exp_w, pt_ps, pt_out, pv_ps, o_ready, ot_ps, ot_out = (
            sem("bias_w"), sem("exp_w"), sem("s_pt_ps"), sem("s_pt_out"), sem("s_pv_ps"), sem("o_ready"),
            sem("ot_ps"), sem("ot_out"))
        KT = [(0, a, P) for a in range(PAGES)] + [(0, PAGES, 64)] + [(1, a, P) for a in range(4)] + [(1, 4, 64)]
        OFF = [a * P for a in range(PAGES)] + [PAST] + [1088 + a * P for a in range(4)] + [1088 + SEQ]
        GROUPED = [list(range(a, min(a + 4, len(KT)))) for a in range(0, len(KT), 4)]

        block = ctx.enter_context(nc.Block())

        @block.sync
        def _(sp):
            sp.dma_start(pgt[:], c.d["page_table"]).then_inc(table_in, 16)
            sp.wait_ge(table_in, 16)
            for p in range(NP):
                if p >= 2:
                    sp.wait_ge(ot_out, 4 * (p - 1))
                for a in range(2 * PAGES):
                    v = sp.value_load(pgt[0:1, 2 * PAGES * p + a:2 * PAGES * p + a + 1], min_val=0, max_val=POOL - 1)
                    sp.dma_start(pg[p % 2][:, a], c.d["cache"][bass.ds(v, 1)].rearrange("o p s e -> (o p) s e")).then_inc(pages_in[p % 2], 16)
                sp.dma_start(wk[:, p % 2], c.d["win_kT"][:, 2 * p:2 * p + 2]).then_inc(pages_in[p % 2], 16)
                sp.dma_start(wv[:, p % 2], c.d["win_v"][:, 2 * p:2 * p + 2]).then_inc(pages_in[p % 2], 16)

        @block.tensor
        def _(pe):
            z4 = c.z4[0:64]
            idn = c.k("ident")[0:64, 0:64]
            for h in range(HG):
                pe.transpose(c.ps[:, 0, h * 64:(h + 1) * 64],
                             z4[:, ZQ + h * P:ZQ + (h + 1) * P], idn)
            for s in range(2):
                pe.transpose(c.ps[:, 0, 256 + s * 64:320 + s * 64], z4[:, ZK + 256 * (s + 1):ZK + 256 * (s + 1) + P], idn)
            for p in range(NP):
                mm = pe.matmul(c.ps[:, 1, p * 24:(p + 1) * 24], c.k("expand")[0:64, p * P:(p + 1) * P], c.gate[0:64, 4],
                               start=True, stop=True)
            mm.then_inc(small_ps, 1)
            pe.wait_ge(small_out, 3)
            pe.wait_ge(qb_zero, 9)
            for p in range(NP):
                b = p % 2
                pe.wait_ge(pages_in[b], 16 * (2 * PAGES + 2) * (p // 2 + 1))
                if p:
                    pe.wait_ge(ot_out, 4 * p)
                for s in range(2):
                    for g in range(2):
                        for j in range(8):
                            mov = pg[b][:, :, s].rearrange("p a (g j n) -> p a g j n", g=2, j=8)[:, :, g, j]
                            mm = pe.matmul(c.ps[:, 5, (s * 2 + g) * P:(s * 2 + g + 1) * P], c.w1[:, s, j], mov,
                                           start=j == 0, stop=j == 7)
                mm.then_inc(cmp_ps, 1)
                for e in range(2):
                    row = slice(HD * e, HD * (e + 1))
                    q = qb[:, 2 * p + e].rearrange("p g h t -> p (g h t)")
                    for a in range(2):
                        pe.matmul(c.ps[row, a, :], q, pg[b][:, e * PAGES + 4 * a:e * PAGES + 4 * a + 4, 2], start=True, stop=True)
                    pe.matmul(c.ps[row, 2, 0:64], q, kn[:, 0], start=True, stop=True)
                    pe.matmul(c.ps[row, 3, :], q, wk[:, b, e], start=True, stop=True)
                    mm = pe.matmul(c.ps[row, 4, 0:64], q, kn[:, 1], start=True, stop=True)
                mm.then_inc(wide_ps, 1)
                pe.wait_ge(hid_ready, p + 1)
                for g in range(2):
                    pe.matmul(c.ps[HD * g:HD * (g + 1), 6, 0:P], c.w2[:, 0], hid[:, g], start=True, stop=True)
                    for e in range(2):
                        mm = pe.matmul(c.ps[0:63, 7, e * P + g * HD:e * P + (g + 1) * HD], hid[:, 2 + g, e * 64:e * 64 + 63],
                                       c.w2[:, 1], start=True, stop=True)
                mm.then_inc(kc_ps, 1)
                pe.wait_ge(kc_out, 2 * p + 2)
                for e in range(2):
                    mm = pe.matmul(c.ps[HD * e:HD * (e + 1), 5, 0:63], qb[:, 2 * p + e].rearrange("p g h t -> p (g h t)"),
                                   kc[:, e * 64:e * 64 + 63], start=True, stop=True)
                mm.then_inc(sc_ps, 1)
                pe.wait_ge(pc_ready, p + 1)
                pe.matmul(c.ps[:, 7, 256:319], c.k("same"), pc[:, 0:63], start=True, stop=True).then_inc(imp_ps, 1)
                pe.transpose(c.ps[0:63, 6, 0:P], pc[:, 0:63], c.k("ident")).then_inc(pct_ps, 1)
                pe.wait_ge(pct_out, p + 1)
                pe.wait_ge(imp_out, p + 1)
                for e in range(2):
                    for g in range(2):
                        lo = 64 * e + 32 * g
                        mm = pe.matmul(c.ps[lo:lo + 32, 7, 0:HD], pt[0:63, lo:lo + 32], vc[0:63, e, g * HD:(g + 1) * HD],
                                       start=True, stop=True, tile_position=(0, lo))
                mm.then_inc(pv_ps, 1)
                for n, tiles in enumerate(GROUPED):
                    m = len(GROUPED) * p + n
                    pe.wait_ge(exp_w, 2 * p + 1 + max(KT[t][0] for t in tiles))
                    if m >= 2:
                        pe.wait_ge(pt_out, m - 1)
                    for a, t in enumerate(tiles):
                        r = KT[t][2]
                        mm = pe.transpose(c.ps[0:r, m % 2, a * P:(a + 1) * P], S[:, OFF[t]:OFF[t] + r], c.k("ident"))
                    mm.then_inc(pt_ps, 1)
                pe.wait_ge(pt_out, len(GROUPED) * (p + 1))
                for w in range(2):
                    tiles = [t for t in range(len(KT)) if KT[t][0] == w]
                    for e in range(2):
                        for g in range(2):
                            lo = 64 * e + 32 * g
                            for t in tiles:
                                a, r = KT[t][1], KT[t][2]
                                if r == 64:
                                    v = c.z4[0:64, ZK + 256 * (w + 1) + P + g * HD:ZK + 256 * (w + 1) + P + (g + 1) * HD]
                                elif w == 0:
                                    v = pg[b][:, e * PAGES + a, 3, g * HD:(g + 1) * HD]
                                else:
                                    v = wv[:, b, e, a, g * HD:(g + 1) * HD]
                                mm = pe.matmul(c.ps[lo:lo + 32, 3 + w, 0:HD], pt[0:r, t * P + lo:t * P + lo + 32], v,
                                               start=t == tiles[0], stop=t == tiles[-1], tile_position=(0, lo))
                    mm.then_inc(pv_ps, 1)
                pe.wait_ge(o_ready, p + 1)
                pe.transpose(c.ps[:, 2, 0:P], o[:], c.k("ident")).then_inc(ot_ps, 1)

        @block.scalar
        def _(act):
            act.wait_ge(small_ps, 1)
            act.activation(qs[:], c.ps[:, 0, 0:256].rearrange("p (h t) -> p h t", h=HG), ACT.Copy).then_inc(small_out, 1)
            act.activation(kn[:], c.ps[:, 0, 256:384].rearrange("p (s t) -> p s t", s=2), ACT.Copy).then_inc(small_out, 1)
            act.activation(c.gs[:], c.ps[:, 1, 0:96].rearrange("p (a e) -> p a e", a=4), ACT.Copy).then_inc(small_out, 1)
            act.wait_ge(small_out, 1)
            act.wait_ge(qb_zero, 1)
            for g in range(2):
                r = slice(HD * g, HD * (g + 1))
                for h in range(HG):
                    act.activation(qb[r, :, g, h], qs[r, h].rearrange("p (b t) -> p b t", b=NB), ACT.Copy).then_inc(qb_zero, 1)
            for p in range(NP):
                act.wait_ge(cmp_ps, p + 1)
                if p:
                    act.wait_ge(hid_ready, p)
                for s in range(2):
                    act.activation(trail[:, 2 * s:2 * s + 2], c.ps[HD:P, 5, s * 256:(s + 1) * 256].rearrange("p (g n) -> p g n", g=2),
                                   ACT.Copy).then_inc(trail_out, 1)
                act.wait_ge(hid_scaled, p + 1)
                g4 = gt[:].rearrange("p r a (b n) -> p r (a b) n", b=2)[:, :, :, 0:63]
                act.activation(g4[:, 1], g4[:, 0], ACT.Tanh, scale=GELU_B).then_inc(hid_tanh, 1)
                act.wait_ge(kc_ps, p + 1)
                act.activation(kc[:], c.ps[:, 6, 0:P], ACT.Copy).then_inc(kc_out, 1)
                act.activation(vc[:], c.ps[0:63, 7, 0:2 * P].rearrange("p (e n) -> p e n", e=2), ACT.Copy).then_inc(kc_out, 1)
                act.wait_ge(bias_c, p + 1)
                act.activation(pc[:, 0:63], c.ps[:, 5, 0:63], ACT.Exp, bias=s1[:, 1:2], scale=SCALE,
                               accum_out=s1[:, 2:3]).then_inc(exp_c, 1)
                act.wait_ge(pct_ps, p + 1)
                act.activation(pt[0:63, 0:P], c.ps[0:63, 6, 0:P], ACT.Copy).then_inc(pct_out, 1)
                for w in range(2):
                    act.wait_ge(bias_w, 2 * p + w + 1)
                    s = S[:, 1088 * w:1088 + 576 * w]
                    act.activation(s, s, ACT.Exp, bias=s1[:, 4 + 3 * w:5 + 3 * w], scale=SCALE,
                                   accum_out=s1[:, 5 + 3 * w:6 + 3 * w]).then_inc(exp_w, 1)
                act.wait_ge(pv_ps, 3 * p + 1)
                for n, tiles in enumerate(GROUPED):
                    m = len(GROUPED) * p + n
                    act.wait_ge(pt_ps, m + 1)
                    full = [t for t in tiles if KT[t][2] == P]
                    for t0, t1, r in ([(tiles[0], tiles[-1] + 1, P)] if len(full) == len(tiles) else
                                      [(t, t + 1, KT[t][2]) for t in tiles]):
                        a = t0 - tiles[0]
                        ins = act.activation(pt[0:r, t0 * P:t1 * P], c.ps[0:r, m % 2, a * P:(a + t1 - t0) * P], ACT.Copy)
                    ins.then_inc(pt_out, 1)
                act.wait_ge(ot_ps, p + 1)
                for h2 in range(2):
                    src = c.ps[HD * h2:HD * (h2 + 1), 2, 0:P].rearrange("p (b n f t) -> p b n f t", b=2, n=4, f=2)[:, :, :, h2]
                    dst = c.aT[HD * h2:HD * (h2 + 1), :, SEQ + 16 * p:SEQ + 16 * (p + 1)].rearrange("p n (b t) -> p b n t", b=2)
                    for e in range(2):
                        act.activation(dst[:, e], src[:, e], ACT.Copy).then_inc(ot_out, 1)

        @block.vector
        def _(dve):
            link = c.vsteps.on(dve)
            dve.memset(s1[:], 0.0)
            dve.memset(hid[:], 0.0)
            dve.memset(imp[:], 0.0)
            dve.memset(qb[:], 0.0).then_inc(qb_zero, 1)
            dve.wait_ge(small_out, 3)
            for p in range(NP):
                dve.wait_ge(trail_out, 2 * p + 2)
                if p:
                    dve.wait_ge(kc_ps, p)
                    dve.wait_ge(ot_out, 4 * p)

                def v3(ap):
                    return ap.rearrange("p a (b n) -> p (a b) n", b=2)
                gelu_hidden(dve, link, c.b1, v3(hid[:])[:, :, 0:63],
                            c.ps[0:HD, 5, :].rearrange("p (a n) -> p a n", n=64)[:, :, 0:63],
                            v3(trail[:])[:, :, 1:64],
                            gt[:].rearrange("p r a (b n) -> p r (a b) n", b=2)[:, :, :, 0:63],
                            lambda ins: ins.then_inc(hid_scaled, 1), lambda: dve.wait_ge(hid_tanh, p + 1))
                dve.engine_nop().then_inc(hid_ready, 1)
                g3 = c.gs[:, p].rearrange("p (h r) -> p r h", r=3)
                link(dve.tensor_tensor(gb[:], g3, c.k("headpick").unsqueeze(1).broadcast_to([P, 3, 8]), ALU.mult))
                link(dve.tensor_reduce(gsel[:], gb[:], AX, ALU.add))
                dve.wait_ge(sc_ps, p + 1)
                link(dve.tensor_reduce(s1[:, 0:1], c.ps[:, 5, 0:63], AX, ALU.max))
                dve.tensor_scalar(s1[:, 1:2], s1[:, 0:1], -SCALE, None, ALU.mult).then_inc(bias_c, 1)
                dve.wait_ge(exp_c, p + 1)
                link(dve.reciprocal(s1[:, 3:4], s1[:, 2:3]))
                dve.tensor_scalar(pc[:, 0:63], pc[:, 0:63], s1[:, 3:4], None, ALU.mult).then_inc(pc_ready, 1)
                dve.wait_ge(wide_ps, p + 1)
                W = S[:, 1088:1088 + 576]
                dve.tensor_tensor(W[:, 0:8], c.ps[:, 3, 0:8], c.k("winmask"), ALU.add)
                dve.tensor_copy(W[:, 8:SEQ], c.ps[:, 3, 8:SEQ])
                nm = c.k("newmask")[:, 64 * p:64 * (p + 1)]
                link(dve.tensor_tensor(W[:, SEQ:SEQ + 64], c.ps[:, 4, 0:64], nm, ALU.add))
                link(dve.tensor_reduce(s1[:, 6:7], W, AX, ALU.max))
                link(dve.tensor_scalar(s1[:, 7:8], s1[:, 6:7], -SCALE, None, ALU.mult))
                dve.wait_ge(imp_ps, p + 1)
                dve.tensor_copy(imp[:, 1:64], c.ps[:, 7, 256:319]).then_inc(imp_out, 1)
                dve.wait_ge(imp_out, p + 1)
                link(dve.tensor_tensor(half[:], imp[:, 1:69], imp[:, 0:68], ALU.add))
                link(dve.tensor_reduce(b17[:, 0], half[:].rearrange("p (b n) -> p b n", n=4), AX, ALU.add))
                fo = c.k("force17")
                link(dve.tensor_scalar(b17[:, 1], fo, -1.0, 1.0, ALU.mult, ALU.add))
                link(dve.tensor_tensor(b17[:, 1], b17[:, 1], b17[:, 0], ALU.mult))
                link(dve.scalar_tensor_tensor(b17[:, 1], fo, 1.0e4, b17[:, 1], ALU.mult, ALU.add))
                link(dve.tensor_reduce(s1[:, 12:13], b17[:, 1], AX, ALU.min))
                link(dve.tensor_scalar(b17[:, 2], b17[:, 1], s1[:, 12:13], None, ALU.is_equal))
                link(dve.tensor_tensor(b17[:, 2], b17[:, 2], c.k("blk17"), ALU.mult))
                link(dve.tensor_reduce(s1[:, 13:14], b17[:, 2], AX, ALU.max))
                link(dve.tensor_scalar(b17[:, 3], b17[:, 2], s1[:, 13:14], NEG, ALU.is_equal, ALU.mult))
                for a in range(2):
                    link(dve.tensor_tensor(S[:, 512 * a:512 * (a + 1)].rearrange("p (b n) -> p b n", n=64),
                                           c.ps[:, a, :].rearrange("p (b n) -> p b n", n=64),
                                           b17[:, 3, 8 * a:8 * a + 8].unsqueeze(2).broadcast_to([P, 8, 64]), ALU.add))
                link(dve.tensor_tensor(S[:, PAST:PAST + 64], c.ps[:, 2, 0:64], nm, ALU.add))
                link(dve.tensor_reduce(s1[:, 14:15], S[:, 0:1088], AX, ALU.max))
                dve.tensor_scalar(s1[:, 4:5], s1[:, 14:15], -SCALE, None, ALU.mult).then_inc(bias_w, 1)
                dve.engine_nop().then_inc(bias_w, 1)
                dve.wait_ge(exp_w, 2 * p + 2)
                link(dve.reciprocal(s1[:, 9:10], s1[:, 5:6]))
                link(dve.reciprocal(s1[:, 10:11], s1[:, 8:9]))
                link(dve.tensor_tensor(s1[:, 9:11], s1[:, 9:11], gsel[:, 1:3], ALU.mult))
                dve.wait_ge(pv_ps, 3 * p + 3)
                link(dve.tensor_scalar(o[:, 0:HD], c.ps[:, 7, 0:HD], gsel[:, 0:1], None, ALU.mult))
                link(dve.scalar_tensor_tensor(o[:, 0:HD], c.ps[:, 3, 0:HD], s1[:, 9:10], o[:, 0:HD], ALU.mult, ALU.add))
                link(dve.scalar_tensor_tensor(o[:, 0:HD], c.ps[:, 4, 0:HD], s1[:, 10:11], o[:, 0:HD], ALU.mult, ALU.add))
                dve.tensor_copy(o[:, HD:2 * HD], o[:, 0:HD]).then_inc(o_ready, 1)


def merge(nc, c):
    with ExitStack() as ctx:
        def sem(name):
            return c.sem("merge_" + name)

        region = Region(c.arena, AT_STATE, AT_END)
        sig = Region(c.arena, AT_Z4, AT_SSM).take([P, 16, TOK])
        w_out = Region(c.arena, AT_KT, AT_XM).take([P, KD, D])
        late = Region(c.arena, region.pos, region.pos + 8192)
        w_glu = region.take([P, 4, D])
        w_ssm = region.take([P, 4, D])
        x = late.take([P, TILES, D])
        h = late.take([P, 2, D])
        hT = late.take([P, KD, P])
        w_attn = region.take([P, 4, D])
        glu = Region(c.arena, region.pos, AT_END).take([P, 4, TOK])
        y = region.take([NCH, CH, SW])
        route = Region(c.arena, region.pos, AT_END)
        tmp = region.take([P, 2, 2, 512])
        yT = region.take([P, 4, TOK])
        g_ffn = region.take([P, D])
        w_route = region.take([P, KD, 36])
        b_route = region.take([P, 36])

        ss = route.take([P, TILES])
        lg = route.take([P, TILES, 36])
        gm = route.take([P, TILES])
        goh = route.take([P, TILES, 4])
        t4 = route.take([P, TILES, 4])
        gw = route.take([P, TILES])
        el = route.take([P, TILES, 32])
        t32 = route.take([P, TILES, 32])
        top = route.take([P, 2, TILES])
        pick = route.take([P, TILES])
        M = route.take([P, 3, TILES, 32])
        nb = route.take([P, 4, 32])
        dest = route.take([P, TILES])
        be = route.take([1, BLOCKS, 32])
        bf = route.take([1, BLOCKS + 1])

        sig_in, wg_in, ws_in, wa_in, wo_in, x_in, rt_in, table_in = (
            sem("sig_in"), sem("wg_in"), sem("ws_in"), sem("wa_in"), sem("wo_in"), sem("m_x_in"), sem("rt_in"),
            sem("slots_in"))
        y_ps, sq_done, u_ready, y_tanh, y_done, yt_ps, yt_out = (
            sem("y_ps"), sem("sq_done"), sem("u_ready"), sem("y_tanh"), sem("y_done"), sem("yt_ps"), sem("yt_out"))
        glu_ps, glu_tanh, glu_done, proj_ps, proj_done, out_ps, x_done, x_zero = (
            sem("glu_ps"), sem("glu_tanh"), sem("glu_done"), sem("proj_ps"), sem("proj_done"), sem("out_ps"),
            sem("x_done"), sem("x_zero"))
        sq2, h_ready, h_stored, ht_ps, ht_out, lg_ps = (
            sem("sq2"), sem("h_ready"), sem("h_stored"), sem("ht_ps"), sem("ht_out"), sem("lg_ps"))
        ge_ready, ge_exp, te_ready, te_exp, m_ready, rank_ps, dest_ready, scattered = (
            sem("ge_ready"), sem("ge_exp"), sem("te_ready"), sem("te_exp"), sem("m_ready"), sem("rank_ps"),
            sem("dest_ready"), sem("scattered"))
        mean2, root2 = sem("mean2"), sem("root2")
        NY = GROUPS // 4

        block = ctx.enter_context(nc.Block())

        @block.sync
        def _(sp):
            sp.dma_start(w_glu[:], c.d["w_glu"]).then_inc(wg_in, 16)
            sp.dma_start(w_ssm[:], c.d["w_ssm"]).then_inc(ws_in, 16)
            sp.dma_start(w_attn[:], c.d["w_attn"]).then_inc(wa_in, 16)
            sp.dma_start(sig[:], c.d["sig"].rearrange("m p t -> p m t")).then_inc(sig_in, 16)
            sp.dma_start(g_ffn[:], c.d["g_ffn"]).then_inc(rt_in, 16)
            sp.dma_start(w_route[:], c.d["w_route"]).then_inc(rt_in, 16)
            sp.dma_start(b_route[:], c.d["b_route"]).then_inc(rt_in, 16)
            sp.dma_start(c.token[:], c.d["token_ids"]).then_inc(rt_in, 16)
            sp.dma_start(c.d["slot_token"].rearrange("(b p) o -> b (p o)", p=P), c.d["unused"]).then_inc(table_in, 16)
            sp.wait_ge(y_ps, NY)
            sp.dma_start(w_out[:], c.d["w_out"]).then_inc(wo_in, 16)
            sp.wait_ge(proj_ps, 32)
            sp.dma_start(x[:, 0:4], c.d["x"][0:SEQ].rearrange("(i p) d -> p i d", p=P)).then_inc(x_in, 16)
            sp.dma_start(x[0:64, 4], c.d["x"][SEQ:TOK]).then_inc(x_in, 16)
            for i in range(TILES):
                sp.wait_ge(h_ready, i + 1)
                sp.dma_start(c.d["h"][i * P:i * P + ROWS[i]], h[0:ROWS[i], i % 2]).then_inc(h_stored, 16)
                sp.wait_ge(h_stored, 16 * (i + 1))
            sp.wait_ge(table_in, 16)

        @block.tensor
        def _(pe):
            for n in range(NY):
                if n >= 4:
                    pe.wait_ge(y_done, n - 3)
                for a in range(4):
                    g = 2 * (4 * (n // 2) + a) + n % 2
                    lo, tl = HD * (g % 2), g // 2
                    o = c.ps[0:NCH, n % 4, a * P:(a + 1) * P]
                    pe.matmul(o, c.U[:, g], c.KT[:, :, g * 16:(g + 1) * 16], start=True, stop=False)
                    for r in range(2):
                        mm = pe.matmul(o, c.XM[lo:lo + HD, r, tl], c.C[lo:lo + HD, r, tl].rearrange("p t e -> p (t e)"),
                                       start=False, stop=r == 1)
                mm.then_inc(y_ps, 1)
            pe.wait_ge(y_done, NY)
            for n in range(8):
                if n >= 2:
                    pe.wait_ge(yt_out, n - 1)
                for a in range(4):
                    t = 4 * (n % 2) + a
                    mm = pe.transpose(c.ps[:, 4 + n % 2, a * NCH:(a + 1) * NCH], y[:, t, n // 2 * P:(n // 2 + 1) * P],
                                      c.k("ident")[0:NCH, 0:NCH])
                mm.then_inc(yt_ps, 1)
            pe.wait_ge(yt_out, 8)
            pe.wait_ge(wg_in, 16)
            for u in range(8):
                j, t = u // 2, slice(u % 2 * HALF, (u % 2 + 1) * HALF)
                if u >= 2:
                    pe.wait_ge(glu_done, u - 1)
                for e in range(2):
                    for k in range(4):
                        mm = pe.matmul(c.ps[:, 2 * e + u % 2, 0:HALF], w_glu[:, k, (4 * e + j) * P:(4 * e + j + 1) * P],
                                       yT[:, k, t], start=k == 0, stop=k == 3)
                    mm.then_inc(glu_ps, 1)
            pe.wait_ge(glu_done, 8)
            pe.wait_ge(ws_in, 16)
            pe.wait_ge(wa_in, 16)
            for u in range(16):
                m, t = u // 2, slice(u % 2 * HALF, (u % 2 + 1) * HALF)
                if u >= 2:
                    pe.wait_ge(proj_done, u - 1)
                for e, (w, mov) in enumerate(((w_ssm, glu), (w_attn, c.aT))):
                    for k in range(4):
                        mm = pe.matmul(c.ps[:, 4 + 2 * e + u % 2, 0:HALF], w[:, k, m * P:(m + 1) * P], mov[:, k, t],
                                       start=k == 0, stop=k == 3)
                    mm.then_inc(proj_ps, 1)
            pe.wait_ge(proj_done, 16)
            pe.wait_ge(wo_in, 16)
            for i in range(TILES + 1):
                if i < TILES:
                    for n in range(2):
                        if i >= 1:
                            pe.wait_ge(x_done, 2 * i + n - 1)
                        for k in range(KD):
                            mm = pe.matmul(c.ps[0:ROWS[i], n, :], sig[:, k, i * P:i * P + ROWS[i]],
                                           w_out[:, k, n * 512:(n + 1) * 512], start=k == 0, stop=k == KD - 1)
                        mm.then_inc(out_ps, 1)
                if i >= 1:
                    r = ROWS[i - 1]
                    pe.wait_ge(h_ready, i)
                    if i >= 2:
                        pe.wait_ge(ht_out, 2 * (i - 1))
                    for n in range(2):
                        for a in range(4):
                            mm = pe.transpose(c.ps[:, 2 + n, a * P:a * P + r], h[0:r, (i - 1) % 2, (4 * n + a) * P:(4 * n + a + 1) * P],
                                              c.k("ident")[0:r, 0:r])
                        mm.then_inc(ht_ps, 1)
                    pe.wait_ge(ht_out, 2 * i)
                    pe.wait_ge(rt_in, 64)
                    for k in range(KD):
                        mm = pe.matmul(c.ps[0:r, 4, (i - 1) * 36:i * 36], hT[:, k, 0:r], w_route[:, k], start=k == 0,
                                       stop=k == KD - 1)
                    mm.then_inc(lg_ps, 1)
            pe.wait_ge(m_ready, 1)
            for i in range(TILES + 1):
                for a in range(min(i + 1, TILES)):
                    mm = pe.matmul(c.ps[:, 5, i * 32:(i + 1) * 32], c.k("tri") if a == i else c.k("ones"), M[:, 2, a],
                                   start=a == 0, stop=a == min(i, TILES - 1))
            mm.then_inc(rank_ps, 1)

        @block.scalar
        def _(act):
            def square(n):
                act.wait_ge(y_ps, n + 1)
                if n >= 2:
                    act.wait_ge(y_tanh, n - 1)
                act.activation(tmp[0:NCH, n % 2, 0], c.ps[0:NCH, n % 4, :], ACT.Square).then_inc(sq_done, 1)

            square(0)
            for n in range(NY):
                if n + 1 < NY:
                    square(n + 1)
                act.wait_ge(u_ready, n + 1)
                if n >= 2:
                    act.wait_ge(y_done, n - 1)
                act.activation(tmp[0:NCH, n % 2, 1], tmp[0:NCH, n % 2, 0], ACT.Tanh, scale=GELU_B).then_inc(y_tanh, 1)
            for n in range(8):
                act.wait_ge(yt_ps, n + 1)
                dst = yT[:, n // 2].rearrange("p (k t) -> p t k", t=CH)[:, 4 * (n % 2):4 * (n % 2) + 4]
                act.activation(dst, c.ps[:, 4 + n % 2, 0:4 * NCH].rearrange("p (t k) -> p t k", t=4), ACT.Copy).then_inc(yt_out, 1)
            for u in range(8):
                act.wait_ge(glu_ps, 2 * u + 2)
                if u >= 2:
                    act.wait_ge(glu_done, u - 1)
                act.activation(tmp[:, u % 2, 0, 0:HALF], c.ps[:, 2 + u % 2, 0:HALF], ACT.Tanh, scale=0.5).then_inc(glu_tanh, 1)
            for i in range(TILES):
                act.wait_ge(x_done, 2 * i + 2)
                if i:
                    act.wait_ge(h_ready, i)
                if i >= 2:
                    act.wait_ge(h_stored, 16 * (i - 1))
                act.activation(h[:, i % 2], x[:, i], ACT.Square, accum_out=ss[:, i:i + 1]).then_inc(sq2, 1)
                act.wait_ge(mean2, i + 1)
                act.activation(ss[:, i:i + 1], ss[:, i:i + 1], ACT.Sqrt).then_inc(root2, 1)
                for n in range(2):
                    act.wait_ge(ht_ps, 2 * i + n + 1)
                    if i and n == 0:
                        act.wait_ge(lg_ps, i)
                    r = ROWS[i]
                    src = c.ps[:, 2 + n, :].rearrange("p (a t) -> p a t", a=4)[:, :, 0:r]
                    act.activation(hT[:, 4 * n:4 * n + 4, 0:r], src, ACT.Copy).then_inc(ht_out, 1)
            act.wait_ge(ge_ready, 1)
            act.activation(t4[:], t4[:], ACT.Exp).then_inc(ge_exp, 1)
            act.wait_ge(te_ready, 1)
            act.activation(c.wt[:, 1], c.wt[:, 1], ACT.Exp).then_inc(te_exp, 1)

        @block.vector
        def _(dve):
            link = c.vsteps.on(dve)

            def before_exp(n):
                t, ps = tmp[0:NCH, n % 2, 0], c.ps[0:NCH, n % 4, :]
                dve.wait_ge(sq_done, n + 1)
                link(dve.tensor_scalar(t, t, GELU_A, 1.0, ALU.mult, ALU.add))
                dve.tensor_tensor(t, t, ps, ALU.mult).then_inc(u_ready, 1)

            before_exp(0)
            for n in range(NY):
                if n + 1 < NY:
                    before_exp(n + 1)
                e = tmp[0:NCH, n % 2, 1]
                dve.wait_ge(y_tanh, n + 1)
                link(dve.tensor_scalar(e, e, 0.5, 0.5, ALU.mult, ALU.add))
                by4 = "k (g t e) -> k g t e"
                dve.tensor_tensor(y[:].rearrange("k t (s h e) -> k s h t e", h=2, e=16)[:, 4 * (n // 2):4 * (n // 2) + 4, n % 2],
                                  c.ps[0:NCH, n % 4, :].rearrange(by4, g=4, t=CH),
                                  e.rearrange(by4, g=4, t=CH), ALU.mult).then_inc(y_done, 1)
            for u in range(8):
                e = tmp[:, u % 2, 0, 0:HALF]
                dve.wait_ge(glu_tanh, u + 1)
                link(dve.tensor_scalar(e, e, 0.5, 0.5, ALU.mult, ALU.add))
                if u == 0:
                    dve.wait_ge(yt_ps, 8)
                dve.tensor_tensor(glu[:, u // 2, u % 2 * HALF:(u % 2 + 1) * HALF], c.ps[:, u % 2, 0:HALF], e,
                                  ALU.mult).then_inc(glu_done, 1)
            dve.wait_ge(sig_in, 16)
            for u in range(16):
                m, t = u // 2, slice(u % 2 * HALF, (u % 2 + 1) * HALF)
                dve.wait_ge(proj_ps, 2 * u + 2)
                dve.tensor_tensor(sig[:, m, t], sig[:, m, t], c.ps[:, 4 + u % 2, 0:HALF], ALU.mult)
                link(dve.tensor_tensor(sig[:, 8 + m, t], sig[:, 8 + m, t], c.ps[:, 6 + u % 2, 0:HALF], ALU.mult))
                dve.tensor_tensor(sig[:, m, t], sig[:, m, t], sig[:, 8 + m, t], ALU.add).then_inc(proj_done, 1)
            dve.wait_ge(x_in, 32)
            dve.wait_ge(rt_in, 64)
            link(dve.memset(x[64:P, 4], 0.0))
            for i in range(TILES):
                r = ROWS[i]
                for n in range(2):
                    dve.wait_ge(out_ps, 2 * i + n + 1)
                    xs = x[0:r, i, n * 512:(n + 1) * 512]
                    dve.tensor_tensor(xs, c.ps[0:r, n, :], xs, ALU.add).then_inc(x_done, 1)
                dve.wait_ge(sq2, i + 1)
                dve.tensor_scalar(ss[:, i:i + 1], ss[:, i:i + 1], 1.0 / D, EPS, ALU.mult, ALU.add).then_inc(mean2, 1)
                dve.wait_ge(root2, i + 1)
                link(dve.reciprocal(ss[:, i:i + 1], ss[:, i:i + 1]))
                dve.scalar_tensor_tensor(h[:, i % 2], x[:, i], ss[:, i:i + 1], g_ffn[:], ALU.mult,
                                         ALU.mult).then_inc(h_ready, 1)
            dve.wait_ge(lg_ps, TILES)
            link(dve.memset(lg[:], 0.0))
            ps = c.ps[:, 4, 0:TILES * 36].rearrange("p (i e) -> p i e", e=36)
            link(dve.tensor_tensor(lg[:, 0:4], ps[:, 0:4], b_route.unsqueeze(1).broadcast_to([P, 4, 36]), ALU.add))
            link(dve.tensor_tensor(lg[0:64, 4], ps[0:64, 4], b_route[0:64], ALU.add))

            def wide(col, n):
                return col.unsqueeze(2).broadcast_to([P, TILES, n])

            def first_of_max(out, vals, mx, desc, n):
                link(dve.tensor_tensor(out, vals, wide(mx, n), ALU.is_equal))
                link(dve.tensor_tensor(out, out, desc.unsqueeze(1).broadcast_to([P, TILES, n]), ALU.mult))
                link(dve.tensor_reduce(pick[:], out, AX, ALU.max))
                link(dve.tensor_tensor(out, out, wide(pick[:], n), ALU.is_equal))

            gl = lg[:, :, 0:4]
            link(dve.tensor_reduce(gm[:], gl, AX, ALU.max))
            dve.tensor_tensor(t4[:], gl, wide(gm[:], 4), ALU.subtract).then_inc(ge_ready, 1)
            first_of_max(goh[:], gl, gm[:], c.k("desc4"), 4)
            dve.wait_ge(ge_exp, 1)
            link(dve.tensor_reduce(gw[:], t4[:], AX, ALU.add))
            link(dve.reciprocal(gw[:], gw[:]))
            link(dve.tensor_scalar(t4[:], goh[:], -1.0, -NEG, ALU.add, ALU.mult))
            link(dve.tensor_tensor(el[:].rearrange("p i (g e) -> p i g e", g=4),
                                   lg[:, :, 4:36].rearrange("p i (g e) -> p i g e", g=4),
                                   t4[:].unsqueeze(3).broadcast_to([P, TILES, 4, 8]), ALU.add))
            link(dve.tensor_reduce(top[:, 0], el[:], AX, ALU.max))
            first_of_max(M[:, 0], el[:], top[:, 0], c.k("desc32"), 32)
            link(dve.scalar_tensor_tensor(t32[:], M[:, 0], -3.0e38, el[:], ALU.mult, ALU.add))
            link(dve.tensor_reduce(top[:, 1], t32[:], AX, ALU.max))
            first_of_max(M[:, 1], t32[:], top[:, 1], c.k("desc32"), 32)
            for j in range(2):
                link(dve.tensor_tensor(M[:, j], M[:, j], wide(c.k("valid"), 32), ALU.mult))
            dve.tensor_tensor(M[:, 2], M[:, 0], M[:, 1], ALU.add).then_inc(m_ready, 1)
            dve.tensor_tensor(c.wt[:, 1], top[:, 1], top[:, 0], ALU.subtract).then_inc(te_ready, 1)
            dve.wait_ge(te_exp, 1)
            link(dve.tensor_scalar(c.wt[:, 0], c.wt[:, 1], 1.0, None, ALU.add))
            link(dve.reciprocal(c.wt[:, 0], c.wt[:, 0]))
            link(dve.tensor_tensor(c.wt[:, 0], c.wt[:, 0], gw[:], ALU.mult))
            link(dve.tensor_tensor(c.wt[:, 1], c.wt[:, 1], c.wt[:, 0], ALU.mult))
            dve.wait_ge(rank_ps, 1)
            cnt = c.ps[:, 5, 5 * 32:6 * 32]
            link(dve.tensor_scalar(nb[:, 0], cnt, 0.0, None, ALU.is_gt))
            for k in range(1, 5):
                link(dve.tensor_scalar(nb[:, 3], cnt, float(P * k), None, ALU.is_gt))
                link(dve.tensor_tensor(nb[:, 0], nb[:, 0], nb[:, 3], ALU.add))
            link(dve.tensor_tensor_scan(nb[:, 1], c.k("ones")[:, 0:32], nb[:, 0], 0.0, ALU.mult, ALU.add))
            link(dve.tensor_tensor(nb[:, 2], nb[:, 1], nb[:, 0], ALU.subtract))
            link(dve.tensor_scalar(nb[:, 2], nb[:, 2], float(P), None, ALU.mult))
            link(dve.tensor_tensor(t32[:], c.ps[:, 5, 0:5 * 32].rearrange("p (i e) -> p i e", e=32),
                                   nb[:, 2].unsqueeze(1).broadcast_to([P, TILES, 32]), ALU.add))
            for j in range(2):
                link(dve.tensor_tensor(el[:], M[:, j], t32[:], ALU.mult))
                link(dve.tensor_reduce(dest[:], el[:], AX, ALU.add))
                link(dve.tensor_copy(c.dest[:, j], dest[:]))
            link(dve.tensor_tensor(be[:], nb[0:1, 1].unsqueeze(1).broadcast_to([1, BLOCKS, 32]),
                                   c.k("blkno")[0:1].unsqueeze(2).broadcast_to([1, BLOCKS, 32]), ALU.is_le))
            link(dve.tensor_reduce(bf[:, 0:BLOCKS], be[:], AX, ALU.add))
            link(dve.tensor_scalar(bf[:, 0:BLOCKS], bf[:, 0:BLOCKS], float(N_EXP - 1), None, ALU.min))
            half = BLOCKS // 2
            link(dve.tensor_scalar(be[:, 0, 0:half], c.k("blkno")[0:1, 0:half], 2.0, nb[0:1, 1, 31:32], ALU.mult, ALU.is_lt))
            link(dve.tensor_reduce(bf[:, BLOCKS:BLOCKS + 1], be[:, 0, 0:half], AX, ALU.add))
            dve.tensor_copy(c.blocks[:], bf[:]).then_inc(dest_ready, 1)

        @block.gpsimd
        def _(pool):
            pool.wait_ge(dest_ready, 1)
            pool.wait_ge(rt_in, 64)
            pool.wait_ge(table_in, 16)
            for i in range(TILES):
                for j in range(2):
                    r = ROWS[i]
                    pool.indirect_dma_start(c.d["slot_token"], bass.IndirectOffsetOnAxis(ap=c.dest[0:r, j, i:i + 1].bitcast(U32), axis=0),
                                            c.token[0:r, i, j], None).then_inc(scattered, 16)
            pool.wait_ge(scattered, 16 * 2 * TILES)


def experts(nc, c):
    with ExitStack() as ctx:
        def sem(name):
            return c.sem("experts_" + name)

        wbuf = Region(c.arena, AT_Z4, AT_STATE)
        wg = wbuf.take([P, 2, KD, DE])
        wu = wbuf.take([P, 2, KD, DE])
        wd = wbuf.take([P, 2, KE, D])
        region = Region(c.arena, AT_STATE, AT_END)
        c.x2 = region.take([P, TILES, D])
        X = region.take([P, 2, D])
        XT = region.take([P, 2, KD, P])
        e = region.take([P, DE])
        H = region.take([P, DE])
        HT = region.take([P, KE, P])
        Y = region.take([P, 2, D])
        table = region.take([P, BLOCKS + 1, 2], I32)
        idx = region.take([P, 2, 2], I32)
        none = region.take([P, 1], I32)
        tick = region.take([1, 8])

        wgu_in = [sem(f"w_gate_up_in{i}") for i in range(2)]
        wd_in = [sem(f"w_down_in{i}") for i in range(2)]
        table_in, idx_copied = sem("table_in"), sem("idx_copied")
        rows_in = [sem(f"rows_in{i}") for i in range(2)]
        y_stored = [sem(f"y_stored{i}") for i in range(2)]
        x_zero, gate_ps, xt_ps, xt_out, gate_tanh, h_ready, ht_ps, ht_out, y_out, silu_steps = (
            sem("e_x_zero"), sem("gate_ps"), sem("xt_ps"), sem("xt_out"), sem("gate_tanh"), sem("e_h_ready"),
            sem("e_ht_ps"), sem("e_ht_out"), sem("y_out"), sem("silu_steps"))
        up_ps, down_ps = sem("up_ps"), sem("down_ps")
        UP0, DOWN0, XT0, HT0, Y0, H0, TURN0, STORED0 = 2, 4, 1, 1, 2, 1, 1, 16
        turn, store_turn = sem("turn"), sem("store_turn")

        def pairs(eng):
            return eng.value_load(c.blocks[0:1, BLOCKS:BLOCKS + 1], min_val=1, max_val=BLOCKS // 2)

        block = ctx.enter_context(nc.Block())

        @block.sync
        def _(sp):
            sp.dma_start(table[:], c.d["slot_token"].rearrange("(b p) o -> p b o", p=P)).then_inc(table_in, 16)
            with sp.Fori(0, pairs(sp)) as i:
                for q in range(2):
                    b = i * 2 + q
                    x = sp.value_load(c.blocks[0:1, bass.ds(b, 1)], min_val=0, max_val=N_EXP - 1)
                    sp.wait_ge(up_ps, b - 1 + UP0)
                    sp.dma_start(wg[:, q], c.d["w_gate"][bass.ds(x, 1)].rearrange("o p k n -> (o p) k n")).then_inc(wgu_in[q], 16)
                    sp.dma_start(wu[:, q], c.d["w_up"][bass.ds(x, 1)].rearrange("o p k n -> (o p) k n")).then_inc(wgu_in[q], 16)
                    sp.wait_ge(down_ps, i * 4 + 2 * (q - 1) + DOWN0)
                    sp.dma_start(wd[:, q], c.d["w_down"][bass.ds(x, 1)].rearrange("o p k n -> (o p) k n")).then_inc(wd_in[q], 16)

        @block.gpsimd
        def _(pool):
            def gather(q):
                pool.indirect_dma_start(X[:, q], None, c.d["h"], bass.IndirectOffsetOnAxis(ap=idx[:, q, 0:1].bitcast(U32), axis=0),
                                        bounds_check=TOK - 1, oob_is_err=False).then_inc(rows_in[q], 16)

            def scatter(q, at):
                pool.indirect_dma_start(c.d["rows"], bass.IndirectOffsetOnAxis(ap=at.bitcast(U32), axis=0), Y[:, q], None,
                                        bounds_check=2 * TOK - 1, oob_is_err=False).then_inc(y_stored[q], 16)

            n = pairs(pool)
            pool.memset(tick, 0.0)
            pool.engine_nop().then_inc(store_turn, TURN0)
            pool.memset(none[:], BIG).then_inc(x_zero, 1)
            pool.memset(Y[:], 0.0).then_inc(x_zero, 1)
            pool.memset(X[:], 0.0).then_inc(x_zero, 1)
            pool.wait_ge(table_in, 16)
            pool.tensor_copy(idx[:, 0], table[:, 0]).then_inc(idx_copied, 1)
            pool.wait_ge(x_zero, 3)
            pool.wait_ge(idx_copied, 1)
            gather(0)
            for q in range(2):
                scatter(q, none[:])
            with pool.Fori(0, n) as i:
                for q in range(2):
                    pool.wait_ge(y_stored[1 - q], i * 16 + 16 * q + STORED0)
                    pool.tensor_copy(idx[:, 1 - q], table[:, bass.ds(i * 2 + q + 1, 1)].rearrange("p a b -> p (a b)")).then_inc(idx_copied, 1)
                    pool.wait_ge(idx_copied, i * 2 + q + 2)
                    pool.wait_ge(xt_ps, i * 2 + q + XT0)
                    pool.tensor_tensor(tick[:, 1 + q:2 + q], tick[:, 0:1], tick[:, 0:1], ALU.mult).then_inc(turn, 1)
                    gather(1 - q)
                    pool.wait_ge(y_out, i * 4 + 2 * q + 2 + Y0)
                    pool.tensor_tensor(tick[:, 3 + q:4 + q], tick[:, 0:1], tick[:, 0:1], ALU.mult).then_inc(store_turn, 1)
                    scatter(q, idx[:, q, 1:2])
            for q in range(2):
                pool.wait_ge(y_stored[q], n * 16 + STORED0)
                pool.tensor_tensor(tick[:, 5 + q:6 + q], tick[:, 0:1], tick[:, 0:1], ALU.mult)

        @block.tensor
        def _(pe):
            def transpose_rows(q):
                for k in range(KD):
                    mm = pe.transpose(c.ps[:, k // 4, k % 4 * P:(k % 4 + 1) * P], X[:, q, k * P:(k + 1) * P], c.k("ident"))
                mm.then_inc(xt_ps, 1)

            n = pairs(pe)
            pe.nop().then_inc(up_ps, UP0)
            pe.nop().then_inc(down_ps, DOWN0)
            pe.nop().then_inc(xt_ps, XT0)
            pe.nop().then_inc(ht_ps, HT0)
            pe.wait_ge(rows_in[0], 16)
            transpose_rows(0)
            with pe.Fori(0, n) as i:
                for q in range(2):
                    pe.wait_ge(xt_out, i * 4 + 2 * (q + 1))
                    pe.wait_ge(wgu_in[q], i * 32 + 32)
                    for w, bank, done in ((wg, 2, gate_ps), (wu, 3, up_ps)):
                        for k in range(KD):
                            mm = pe.matmul(c.ps[:, bank, :], XT[:, q, k], w[:, q, k], start=k == 0, stop=k == KD - 1)
                        mm.then_inc(done, 1)
                    pe.wait_ge(turn, i * 2 + q + 1)
                    pe.wait_ge(rows_in[1 - q], i * 16 + 16 * (1 + q))
                    transpose_rows(1 - q)
                    pe.wait_ge(h_ready, i * 2 + q + 1 + H0)
                    for k in range(KE):
                        mm = pe.transpose(c.ps[:, 4, k * P:(k + 1) * P], H[:, k * P:(k + 1) * P], c.k("ident"))
                    mm.then_inc(ht_ps, 1)
                    pe.wait_ge(ht_out, i * 2 + q + 1)
                    pe.wait_ge(wd_in[q], i * 16 + 16)
                    pe.wait_ge(y_out, i * 4 + 2 * q + Y0)
                    for h in range(2):
                        for k in range(KE):
                            mm = pe.matmul(c.ps[:, 6 + h, :], HT[:, k], wd[:, q, k, h * 512:(h + 1) * 512], start=k == 0,
                                           stop=k == KE - 1)
                        mm.then_inc(down_ps, 1)

        @block.scalar
        def _(act):
            n = pairs(act)
            act.nop().then_inc(y_out, Y0)
            with act.Fori(0, n) as i:
                for q in range(2):
                    act.wait_ge(gate_ps, i * 2 + q + 1)
                    act.wait_ge(h_ready, i * 2 + q + H0)
                    act.activation(e[:], c.ps[:, 2, :], ACT.Tanh, scale=0.5).then_inc(gate_tanh, 1)
                    act.wait_ge(ht_ps, i * 2 + q + 1 + HT0)
                    act.wait_ge(down_ps, i * 4 + 2 * q + DOWN0)
                    act.activation(HT[:], c.ps[:, 4, :].rearrange("p (k t) -> p k t", k=KE), ACT.Copy).then_inc(ht_out, 1)
                    act.wait_ge(store_turn, i * 2 + q + TURN0)
                    act.wait_ge(y_stored[q], i * 16 + STORED0)
                    for h in range(2):
                        act.wait_ge(down_ps, i * 4 + 2 * q + DOWN0 + h + 1)
                        act.activation(Y[:, q, h * 512:(h + 1) * 512], c.ps[:, 6 + h, :], ACT.Copy).then_inc(y_out, 1)

        @block.vector
        def _(dve):
            def rows_out(q):
                for a in range(2):
                    dve.tensor_copy(XT[:, q, 4 * a:4 * a + 4], c.ps[:, a, :].rearrange("p (k t) -> p k t", k=4)).then_inc(xt_out, 1)

            n = pairs(dve)
            dve.engine_nop().then_inc(h_ready, H0)
            dve.wait_ge(xt_ps, 1 + XT0)
            rows_out(0)
            with dve.Fori(0, n) as i:
                for q in range(2):
                    dve.wait_ge(gate_tanh, i * 2 + q + 1)
                    dve.wait_ge(ht_ps, i * 2 + q + HT0)
                    dve.scalar_tensor_tensor(H[:], e[:], 1.0, c.ps[:, 2, :], ALU.add, ALU.mult).then_inc(silu_steps, 1)
                    dve.wait_ge(silu_steps, i * 2 + q + 1)
                    dve.wait_ge(up_ps, i * 2 + q + 1 + UP0)
                    dve.scalar_tensor_tensor(H[:], H[:], 0.5, c.ps[:, 3, :], ALU.mult, ALU.mult).then_inc(h_ready, 1)
                    dve.wait_ge(xt_ps, i * 2 + q + 2 + XT0)
                    rows_out(1 - q)


def combine(nc, c):
    with ExitStack() as ctx:
        def sem(name):
            return c.sem("combine_" + name)

        region = Region(c.arena, AT_Z4, AT_STATE)
        R = region.take([P, TILES, 2, D])
        g = region.take([P, D])
        y = region.take([P, TILES, D])
        ss = region.take([P, TILES])
        g_in, r_in, x_done, sq_done, y_done, stored, r_zero = (
            sem("g_final_in"), [[sem(f"r_in{i}{j}") for j in range(2)] for i in range(TILES)], sem("c_x_done"),
            sem("c_sq_done"), sem("c_y_done"), sem("c_stored"), sem("r_zero"))
        mean_ready, root_done = sem("c_mean_ready"), sem("c_root_done")

        block = ctx.enter_context(nc.Block())

        @block.sync
        def _(sp):
            sp.dma_start(g[:], c.d["g_final"]).then_inc(g_in, 16)
            for i in range(TILES):
                for j in range(2):
                    at = j * TOK + i * P
                    sp.dma_start(R[0:ROWS[i], i, j], c.d["rows"][at:at + ROWS[i]]).then_inc(r_in[i][j], 16)
            for i in range(TILES):
                sp.wait_ge(y_done, i + 1)
                sp.dma_start(c.o["y"][i * P:i * P + ROWS[i]], y[0:ROWS[i], i]).then_inc(stored, 16)
            sp.wait_ge(stored, 16 * TILES)

        @block.scalar
        def _(act):
            for i in range(TILES):
                r = ROWS[i]
                act.wait_ge(x_done, i + 1)
                act.activation(y[0:r, i], c.x2[0:r, i], ACT.Square, accum_out=ss[0:r, i:i + 1]).then_inc(sq_done, 1)
                act.wait_ge(mean_ready, i + 1)
                act.activation(ss[0:r, i:i + 1], ss[0:r, i:i + 1], ACT.Sqrt).then_inc(root_done, 1)

        @block.vector
        def _(dve):
            link = c.vsteps.on(dve)
            dve.wait_ge(g_in, 16)
            for i in range(TILES):
                r = ROWS[i]
                x, s = c.x2[0:r, i], ss[0:r, i:i + 1]
                dve.wait_ge(r_in[i][0], 16)
                link(dve.scalar_tensor_tensor(x, R[0:r, i, 0], c.wt[0:r, 0, i:i + 1], x, ALU.mult, ALU.add))
                dve.wait_ge(r_in[i][1], 16)
                dve.scalar_tensor_tensor(x, R[0:r, i, 1], c.wt[0:r, 1, i:i + 1], x, ALU.mult, ALU.add).then_inc(x_done, 1)
                dve.wait_ge(sq_done, i + 1)
                dve.tensor_scalar(s, s, 1.0 / D, EPS, ALU.mult, ALU.add).then_inc(mean_ready, 1)
                dve.wait_ge(root_done, i + 1)
                link(dve.reciprocal(s, s))
                dve.scalar_tensor_tensor(y[0:r, i], x, s, g[0:r], ALU.mult, ALU.mult).then_inc(y_done, 1)


def build(nc, d, o):
    c = Core()
    c.d, c.o = d, o
    with ExitStack() as ctx:
        c.arena = ctx.enter_context(nc.sbuf_tensor("arena", [P, AT_END], F32))
        c.ps = ctx.enter_context(nc.psum_tensor("ps", [P, 8, 512], F32))
        taken = []

        def phase_semaphore(name):
            taken.append(nc.alloc_semaphore(name))
            return taken[-1]

        c.sem = phase_semaphore
        c.vsteps = Steps(ctx.enter_context(nc.semaphore("vector_steps")))
        c.gsteps = Steps(ctx.enter_context(nc.semaphore("gpsimd_steps")))
        c.asteps = Steps(ctx.enter_context(nc.semaphore("scalar_steps")))
        c.w1_in = ctx.enter_context(nc.semaphore("cmp_weights_in"))
        low = Region(c.arena, 0, AT_Z4)
        c.K = low.take([P, CW])
        c.k = lambda name: c.K[:, COFF[name]:COFF[name] + CONST[name]]
        c.gate = low.take([P, TILES, 24])
        c.gs = low.take([P, 4, 24])
        c.w1 = low.take([P, 2, 8, P])
        c.w2 = low.take([HD, 2, HD])
        c.pe = low.take([P, 2, 16])
        c.b1 = low.take([HD, 2])
        c.A8 = low.take([P, 2, 2, ST])
        c.fin = low.take([P, 1 + NB, 2, ST])
        c.wt = low.take([P, 2, TILES])
        c.dest = low.take([P, 2, TILES], I32)
        c.token = low.take([P, TILES, 2, 2], I32)
        c.blocks = low.take([1, BLOCKS + 1], I32)
        c.z4 = Region(c.arena, AT_Z4, AT_Z).take([P, ZW])
        c.z = Region(c.arena, AT_Z, AT_SSM).take([P, TILES, ZW])
        s5 = Region(c.arena, AT_SSM, AT_LOCAL)
        c.U = s5.take([P, GROUPS, NCH])
        c.KT = s5.take([P, CH, GROUPS * 16])
        c.C = s5.take([P, 2, ST, CH, 16])
        c.XM = s5.take([P, 2, ST, NCH])
        c.aT = s5.take([P, 4, TOK])
        c.X = s5.take([P, NCH + 1, 2, ST])
        c.S = s5.take([P, NCH, 2, ST])
        for phase in (project, ssm_build, prompt, sample, merge, experts, combine):
            phase(nc, c)
            if phase is not combine:
                nc.clear_and_free_semaphores(taken)
                taken.clear()
                nc.all_engine_barrier()


_OUTS = {"y": (TOK, D), "kv": (TOK, 512), "win_p": (SEQ, 256), "win_s": (NB, SEQ, 256), "ssm": (P, (1 + NB) * 2 * ST)}
_SCRATCH = {"u": ((TOK, SW), F32), "sig": ((16, P, TOK), F32), "h": ((TOK, D), F32),
            "slot_token": (((BLOCKS + 1) * P, 2), I32), "rows": ((2 * TOK, D), F32)}


def layouts(i):
    def by_state(a):
        a = a.reshape((ST, 2 * HD) + a.shape[2:])
        return np.moveaxis(a, 0, 1)

    def k_tiles(w, tiles):
        return w.reshape(tiles, P, -1).transpose(1, 0, 2)

    x = np.concatenate([i["x_prompt"][0], i["x_sample"].reshape(NB * NT, D)], 0)
    w = i["w_in"][0]
    q = w[:, SW:SW + 512].reshape(D, 2, HG, HD).transpose(0, 2, 1, 3).reshape(D, 512)
    w = np.concatenate([w[:, :SW], q, w[:, SW + 512:]], 1)
    wt = k_tiles(w, KD)
    o = {"x": x, "xT": k_tiles(x.T, KD), "g_mix": i["g_mix"][0].reshape(KD, P).T}
    o["w_tok"] = wt[:, :, 0:1536].reshape(P, KD, 3, 512).transpose(2, 0, 1, 3)
    o["w_tail"] = wt[:, :, 1536:ZW]
    o["w_chan"] = wt[:, :, ZW:].reshape(P, KD, 4, 512).transpose(2, 0, 1, 3)
    dt = np.repeat(i["ssm_log_dt"][0][:, None], HD, 1)
    o["ssm_par"] = np.stack([by_state(i["ssm_a_re"][0]), by_state(i["ssm_a_im"][0]), by_state(dt)], 1)
    o["ssm_b"] = np.stack([by_state(i["ssm_b_re"][0]), by_state(i["ssm_b_im"][0])], 1)
    o["ssm_c"] = np.stack([by_state(i["ssm_c_re"][0].transpose(0, 2, 1)), by_state(i["ssm_c_im"][0].transpose(0, 2, 1))], 1)
    o["ssm_d"] = np.broadcast_to(i["ssm_d"][0], (P, GROUPS, 16))
    o["state"] = i["state_ssm"][0].reshape(NB, ST, P, 2).transpose(2, 0, 3, 1)
    w1 = np.stack([i["cmp_w1_k"][0], i["cmp_w1_v"][0]]).reshape(2, 2, 8, P, HD)
    o["cmp_w1"] = w1.transpose(3, 0, 2, 1, 4).reshape(P, 2, 8, P)
    o["cmp_w2"] = np.stack([i["cmp_w2_k"][0], i["cmp_w2_v"][0]]).transpose(1, 0, 2)
    o["cmp_pe"] = np.stack([i["cmp_pe_k"][0], i["cmp_pe_v"][0]]).reshape(2, 16, P).transpose(2, 0, 1)
    o["cmp_b1"] = np.stack([i["cmp_b1_k"][0], i["cmp_b1_v"][0]]).T
    cache = i["cache_kv"][0]
    cmp_ = cache[:, :, 0:2].reshape(POOL, 8, 8, 2, 2, 2, HD)
    cmp_ = cmp_.transpose(0, 3, 6, 4, 5, 2, 1).reshape(POOL, P, 2, P)
    ks = cache[:, :, 2].reshape(POOL, P, P).transpose(0, 2, 1)[:, :, None]
    vs = cache[:, :, 3].reshape(POOL, P, 1, P)
    o["cache"] = np.concatenate([cmp_, ks, vs], 2)
    win = i["cache_win"][0]
    o["win_rows"] = win.reshape(NB, SEQ, 256)
    o["win_kT"] = win[:, :, 0].reshape(NB, SEQ, P).transpose(2, 0, 1)
    o["win_v"] = win[:, :, 1].reshape(NB, 4, P, P).transpose(2, 0, 1, 3)
    o["page_table"] = i["page_table"].reshape(1, -1)
    o["w_glu"] = k_tiles(i["w_glu"][0], 4)
    o["w_ssm"] = k_tiles(i["w_ssm_proj"][0], 4)
    o["w_attn"] = k_tiles(i["w_attn_proj"][0], 4)
    o["w_out"] = k_tiles(i["w_out"][0], KD)
    o["g_ffn"] = np.broadcast_to(i["g_ffn"][0], (P, D))
    o["g_final"] = np.broadcast_to(i["g_final"], (P, D))
    o["w_route"] = k_tiles(np.concatenate([i["w_router_group"][0], i["w_router_expert"][0]], 1), KD)
    o["b_route"] = np.broadcast_to(np.concatenate([i["b_router_group"][0], i["b_router_expert"][0]]), (P, 36))
    o["w_gate"] = i["w_exp_gate"][0].reshape(N_EXP, KD, P, DE).transpose(0, 2, 1, 3)
    o["w_up"] = i["w_exp_up"][0].reshape(N_EXP, KD, P, DE).transpose(0, 2, 1, 3)
    o["w_down"] = i["w_exp_down"][0].reshape(N_EXP, KE, P, D).transpose(0, 2, 1, 3)
    o["consts"] = constants()
    token = np.arange(TILES)[None, :] * P + np.arange(P)[:, None]
    o["token_ids"] = np.stack([np.stack([token, token + j * TOK], -1) for j in range(2)], 2).astype(np.int32)
    o["unused"] = np.full((BLOCKS + 1, 2 * P), BIG, np.int32)
    return {k: np.ascontiguousarray(v) for k, v in o.items()}


def kernel(**inputs):
    import concourse.bacc as _bacc
    from concourse.bass_utils import run_bass_kernel_spmd as _run

    nc = _bacc.Bacc("TRN2", target_bir_lowering=False, num_devices=1)
    arrays, d, o = {}, {}, {}
    for name, a in layouts({k: np.asarray(v) for k, v in inputs.items()}).items():
        arrays[f"in_{name}"] = a
        d[name] = nc.dram_tensor(f"in_{name}", a.shape, mybir.dt.from_np(a.dtype), kind="ExternalInput").ap()
    for name, shape in _OUTS.items():
        o[name] = nc.dram_tensor(f"out_{name}", shape, F32, kind="ExternalOutput").ap()
    for name, (shape, dt) in _SCRATCH.items():
        d[name] = nc.dram_tensor(f"scratch_{name}", shape, dt, kind="Internal").ap()
    build(nc, d, o)
    r = _run(nc, [arrays], core_ids=[0]).results[0]
    y, kv, win_p, win_s, ssm = (np.asarray(r[f"out_{n}"]) for n in _OUTS)
    ssm = ssm.reshape(P, 1 + NB, 2, ST).transpose(1, 3, 0, 2).reshape(1 + NB, GROUPS, HD, 2)
    return (y[:SEQ].reshape(1, SEQ, D), y[SEQ:].reshape(NB, NT, D),
            kv[:SEQ].reshape(1, 1, SEQ, 4, 2, HD), kv[SEQ:].reshape(1, NB, NT, 4, 2, HD),
            win_p.reshape(1, 1, SEQ, 2, 2, HD), win_s.reshape(1, NB, SEQ, 2, 2, HD),
            ssm[None, :1], ssm[None, 1:])
```

```python
from contextlib import ExitStack

import numpy as np

import concourse.bass as bass
from concourse import mybir

F32 = mybir.dt.float32
F32R = mybir.dt.float32r
I32 = mybir.dt.int32
U32 = mybir.dt.uint32
ALU = mybir.AluOpType
ACT = mybir.ActivationFunctionType
AX = mybir.AxisListType.X

P = 128
D = 1024
KD = D // P
SEQ = 512
NB, NT = 8, 8
TOK = SEQ + NB * NT
HALF = TOK // 2
TILES = 5
ROWS = [P, P, P, P, NB * NT]
PAST = 1024
PAGE = 128
PAGES = PAST // PAGE
POOL = 80
SW = 512
GROUPS = 32
ST = 16
CH = 8
PCH = SEQ // CH
NCH = PCH + NB
HD = 64
HG = 4
QKV = 512 + 768
ZW = SW + QKV + 24
ZQ, ZK, ZG = SW, SW + 512, SW + QKV
PW = 256
TOK_PIECES = 8
TAIL = ZW - 7 * PW
W_PIECES = TOK_PIECES + 2 * D // PW
GATES_AFTER = [[], [], [], [], list(range(16))]
N_EXP = 32
DE = 512
KE = DE // P
PIECES = 6
BLOCKS = 42
BIG = 1 << 20
NEG = -1.0e30
EPS = 1e-6
SCALE = HD ** -0.5
TWO_PI = 2 * np.pi
GELU_A = 0.044715
GELU_B = float(np.sqrt(2 / np.pi))

CONST = {
    "ident": P, "ones": P, "tri": P, "causal": P, "same": P, "cos": TILES * 32, "sin": TILES * 32,
    "cmask": 4 * 32, "newmask": 4 * 64, "winmask": 8, "expand": 4 * P, "headpick": 8, "eye7": 16,
    "blk17": 17, "force17": 17, "desc4": 4, "desc32": 32, "valid": TILES, "blkno": BLOCKS,
}
COFF, _o = {}, 0
for _n, _w in CONST.items():
    COFF[_n] = _o
    _o += _w
CW = _o


def constants():
    r = np.arange(P)
    c = {n: np.zeros((P, w), np.float32) for n, w in CONST.items()}
    c["ident"][:] = np.eye(P)
    c["ones"][:] = 1
    c["tri"][:] = r[:, None] < r[None, :]
    c["causal"][:] = np.where(r[None, :] <= r[:, None], 0, NEG)
    b2, g, hg, t = r // 64, r // 32 % 2, r // 8 % 4, r % 8
    c["same"][:] = (b2[:, None] == b2) & (g[:, None] == g) & (t[:, None] == t)
    pos = np.concatenate([np.arange(SEQ), PAST + np.arange(64) % 8, np.zeros(64)]).reshape(TILES, P)
    inv = np.float32(10000.0) ** (-np.arange(32, dtype=np.float32) / np.float32(32))
    ang = (pos.astype(np.float32)[:, :, None] * inv.astype(np.float32)).astype(np.float32)
    c["cos"][:] = np.cos(ang.astype(np.float64)).transpose(1, 0, 2).reshape(P, -1)
    c["sin"][:] = np.sin(ang.astype(np.float64)).transpose(1, 0, 2).reshape(P, -1)
    q = np.arange(4)[None, :, None] * P + r[:, None, None]
    j = np.arange(32)
    c["cmask"][:] = np.where((j * 16 + 31 <= q) & (j < 31), 0, NEG).reshape(P, -1)
    s = np.arange(64)
    bp = np.arange(4)[None, :, None]
    ok = (s // 8 == 2 * bp + b2[:, None, None]) & (s % 8 <= t[:, None, None])
    c["newmask"][:] = np.where(ok, 0, NEG).reshape(P, -1)
    c["winmask"][:] = np.where(np.arange(8)[None, :] > t[:, None], 0, NEG)
    e = (np.arange(64)[:, None, None] // 8 == 2 * bp + b2[None, None, :]) & (np.arange(64)[:, None, None] % 8 == t)
    c["expand"][:64] = e.reshape(64, -1)
    c["headpick"][:] = (g * 4 + hg)[:, None] == np.arange(8)
    c["eye7"][:] = r[:, None] == 112 + np.arange(16)
    c["blk17"][:] = 1 + np.arange(17)
    c["force17"][:] = np.isin(np.arange(17), [0, 15, 16])
    c["desc4"][:] = 4 - np.arange(4)
    c["desc32"][:] = 32 - np.arange(32)
    c["valid"][:] = np.arange(TILES) * P + r[:, None] < TOK
    c["blkno"][:] = np.arange(BLOCKS)
    return np.concatenate([c[n] for n in CONST], 1)


class Steps:

    def __init__(self, sem):
        self.sem, self.n = sem, 0

    def on(self, eng):
        def link(ins):
            self.n += 1
            ins.then_inc(self.sem, 1)
            eng.wait_ge(self.sem, self.n)
        return link


class Core:
    pass


class Region:

    def __init__(self, arena, start, end):
        self.arena, self.pos, self.end = arena, start, end

    def take(self, shape, dt=F32):
        n = int(np.prod(shape[1:]))
        ap = self.arena[0:shape[0], self.pos:self.pos + n]
        self.pos += n
        assert self.pos <= self.end, (self.pos, self.end)
        if dt is not F32:
            ap = ap.bitcast(dt)
        names = "abcdef"[:len(shape) - 1]
        if len(names) > 1:
            ap = ap.rearrange(f"p ({' '.join(names)}) -> p {' '.join(names)}", **dict(zip(names, shape[1:])))
        return ap


AT_Z4 = 4992
AT_Z = AT_Z4 + ZW
AT_SSM = AT_Z + TILES * ZW
AT_KT = AT_SSM + GROUPS * NCH
AT_XM = AT_KT + 2 * 4096
AT_AT = AT_XM + 2 * ST * NCH
AT_STATE = AT_AT + 4 * TOK
AT_LOCAL = AT_STATE + (NCH + 1) * 2 * ST + NCH * 2 * ST
AT_END = 53100
AT_X2_END = AT_XM + TILES * D
LOCAL = AT_END - AT_LOCAL


def local_tensor(nc, ctx, name, dt=F32):
    return ctx.enter_context(nc.sbuf_tensor("local_" + name, [P, LOCAL], dt))


def project(nc, c):
    with ExitStack() as ctx:
        region = Region(c.arena, AT_SSM, AT_XM)
        high = Region(c.arena, AT_STATE, AT_LOCAL)
        def sem(name):
            return c.sem("project_" + name)

        over_x = Region(c.arena, AT_SSM, AT_XM)
        x = region.take([P, TILES, D])
        sg = over_x.take([P, 4, TOK])
        rt = over_x.take([P, 4, 512])
        raw = region.take([P, 2, KD, PW])
        junk = Region(c.arena, region.pos, AT_XM).take([P, D])
        diag = region.take([P, TILES, P])
        rinv_row = region.take([P, TOK])
        ss = region.take([P, TILES])
        rinv = region.take([P, TILES])
        gcol = high.take([P, KD])
        over_xT = Region(c.arena, high.pos, AT_LOCAL)
        xT = high.take([P, KD, TOK])
        bb = over_xT.take([P, 2, ST, 16])
        t4 = over_xT.take([P, 2, 1024])
        split = Region(local_tensor(nc, ctx, "project", F32R), 0, LOCAL)
        XG = split.take([P, 2, KD, TOK], F32)
        W = split.take([P, 2, 2, KD, PW], F32)

        s5_scratch = Region(c.arena, AT_Z4 + 2 * 9 * ST, AT_Z)
        par = s5_scratch.take([P, 3, ST])
        b = s5_scratch.take([P, 2, ST, 16])
        v = s5_scratch.take([P, 14, ST])
        vi = s5_scratch.take([P, ST], I32)
        tw = s5_scratch.take([P, 4, 4, ST])
        pw, cc, Z = c.pw, c.cc, c.Z

        consts_in, x_in, g_in = sem("consts_in"), sem("x_in"), sem("g_in")
        xT_in = [sem(f"xT_in{i}") for i in range(2)]
        raw_in = [sem(f"raw_in{i}") for i in range(2)]
        xg_hi, xg_lo, w_hi, w_lo = sem("xg_hi"), sem("xg_lo"), sem("w_hi"), sem("w_lo")
        square_done, diag_ready, row_ps = sem("square_done"), sem("diag_ready"), sem("row_ps")
        rinv_ready, tail_zero = sem("rinv_ready"), sem("tail_zero")
        tok_ps, tok_out, chan_ps, chan_scaled, chan_tanh = (
            sem("tok_ps"), sem("tok_out"), sem("chan_ps"), sem("chan_scaled"), sem("chan_tanh"))
        gates_ready, roped, stored = sem("gates_tanh"), sem("roped"), sem("stored")
        gate_ready, mean_ready, root_done = sem("gate_ready"), sem("mean_ready"), sem("root_done")
        gate_stored = [sem(f"gate_stored{i}") for i in range(4)]
        par_in, dt_exp, mag_exp, sin_ready, sin_done = (
            sem("par_in"), sem("dt_exp"), sem("mag_exp"), sem("sin_ready"), sem("sin_done"))
        NTU = TOK_PIECES * TILES

        def wait_used(eng, n):
            if n < TOK_PIECES:
                eng.wait_ge(tok_ps, TILES * (n + 1))
            else:
                eng.wait_ge(chan_ps, 4 * (n - TOK_PIECES + 1))

        block = ctx.enter_context(nc.Block())

        @block.sync
        def _(sp):
            def load(n):
                if n == TOK_PIECES - 1:
                    sp.dma_start(raw[:, n % 2, :, 0:TAIL], c.d["w_tail"]).then_inc(raw_in[n % 2], 16)
                else:
                    sp.dma_start(raw[:, n % 2], c.d["w_in"][n if n < TOK_PIECES else n - 1]).then_inc(raw_in[n % 2], 16)

            sp.dma_start(gcol[:], c.d["g_mix"]).then_inc(g_in, 16)
            for a in range(2):
                sp.dma_start(xT[:, 4 * a:4 * a + 4], c.d["xT"][:, 4 * a:4 * a + 4]).then_inc(xT_in[a], 16)
            load(0)
            sp.dma_start(x[:, 0:4, :], c.d["x"][0:SEQ].rearrange("(i p) d -> p i d", p=P)).then_inc(x_in, 16)
            sp.dma_start(x[0:64, 4, :], c.d["x"][SEQ:TOK]).then_inc(x_in, 16)
            load(1)
            sp.dma_start(c.K[:], c.d["consts"]).then_inc(consts_in, 16)
            sp.dma_start(par[:], c.d["ssm_par"]).then_inc(par_in, 16)
            sp.dma_start(b[:], c.d["ssm_b"]).then_inc(par_in, 16)
            sp.dma_start(cc[:], c.d["ssm_c"]).then_inc(par_in, 16)
            for dst, name in ((c.w1, "cmp_w1"), (c.w2, "cmp_w2"), (c.pe, "cmp_pe"), (c.b1, "cmp_b1")):
                sp.dma_start(dst[:], c.d[name]).then_inc(c.w1_in, 16)
            for n in range(2, W_PIECES):
                sp.wait_ge(w_lo, n - 1)
                load(n)
                if n == 4:
                    sp.wait_ge(tok_out, 2 * TILES)
                    sp.dma_start(c.d["u"][0:SEQ].rearrange("(i p) d -> p i d", p=P), c.z[:, 0:4, 0:SW]).then_inc(stored, 16)
                    sp.dma_start(c.d["u"][SEQ:TOK], c.z[0:64, 4, 0:SW]).then_inc(stored, 16)
            sp.wait_ge(roped, TILES)
            kv = c.z[:, :, ZK:ZK + 512]
            win = c.z[:, :, ZK + 512:ZK + 768]
            sp.dma_start(c.o["kv"][0:SEQ].rearrange("(i p) d -> p i d", p=P), kv[:, 0:4]).then_inc(stored, 16)
            sp.dma_start(c.o["kv"][SEQ:TOK], kv[0:64, 4]).then_inc(stored, 16)
            sp.dma_start(c.o["win_p"].rearrange("(i p) d -> p i d", p=P), win[:, 0:4]).then_inc(stored, 16)
            for b_ in range(NB):
                sp.dma_start(c.o["win_s"][b_, SEQ - NT:SEQ], win[b_ * NT:(b_ + 1) * NT, 4]).then_inc(stored, 16)
            sp.wait_ge(stored, 16 * (5 + NB))

        @block.scalar
        def _(act):
            def hi(n):
                act.wait_ge(raw_in[n % 2], 16 * (n // 2 + 1))
                if n >= 2:
                    wait_used(act, n - 2)
                width = TAIL if n == TOK_PIECES - 1 else PW
                act.activation(W[:, n % 2, 0, :, 0:width], raw[:, n % 2, :, 0:width], ACT.Copy).then_inc(w_hi, 1)

            act.wait_ge(g_in, 16)
            for k in range(KD):
                act.wait_ge(xT_in[k // 4], 16)
                act.activation(XG[:, 0, k], xT[:, k], ACT.Copy, scale=gcol[:, k:k + 1]).then_inc(xg_hi, 1)
            hi(0)
            act.wait_ge(x_in, 32)
            act.wait_ge(tail_zero, 1)
            for i in range(TILES):
                if i:
                    act.wait_ge(square_done, i)
                act.activation(junk[:], x[:, i, :], ACT.Square, accum_out=ss[:, i:i + 1]).then_inc(square_done, 1)
            act.wait_ge(mean_ready, 1)
            act.activation(ss[:], ss[:], ACT.Sqrt).then_inc(root_done, 1)
            hi(1)
            act.wait_ge(rinv_ready, 1)
            for n in range(NTU):
                j, i = n // TILES, n % TILES
                r, width = ROWS[i], TAIL if j == TOK_PIECES - 1 else PW
                act.wait_ge(tok_ps, n + 1)
                act.activation(c.z[0:r, i, j * PW:j * PW + width], c.ps[0:r, n % 4, 0:width], ACT.Copy,
                               scale=rinv[0:r, i:i + 1]).then_inc(tok_out, 1)
                if i == TILES - 1:
                    hi(j + 2)
                    if j == 0:
                        act.wait_ge(par_in, 48)
                        act.activation(v[:, 0], par[:, 2], ACT.Exp).then_inc(dt_exp, 1)
                        act.wait_ge(mag_exp, 1)
                        act.activation(v[:, 2], v[:, 1], ACT.Exp).then_inc(dt_exp, 1)
                    if j == 1:
                        act.wait_ge(sin_ready, 1)
                        act.activation(v[:, 7:9], v[:, 5:7], ACT.Sin).then_inc(sin_done, 1)
            act.wait_ge(tok_out, NTU)
            act.activation(c.gate[:], c.z[:, :, ZG:ZW], ACT.Tanh, scale=0.5).then_inc(gates_ready, 1)
            for m in range(16):
                act.wait_ge(chan_scaled, 2 * m + 2)
                act.activation(sg[:, m % 4], sg[:, m % 4], ACT.Tanh, scale=0.5).then_inc(chan_tanh, 1)
                if m % 2 == 1 and m < 12:
                    hi(TOK_PIECES + m // 2 + 2)

        @block.tensor
        def _(pe):
            def product(out, stationary, moving):
                for k in range(KD):
                    for a, (s, m) in enumerate(((0, 0), (0, 1), (1, 0))):
                        mm = pe.matmul(out, stationary(s, k), moving(m, k), start=k == 0 and a == 0, stop=k == KD - 1 and a == 2)
                return mm

            pe.wait_ge(xg_lo, KD)
            for n in range(NTU):
                j, i = n // TILES, n % TILES
                r, width = ROWS[i], TAIL if j == TOK_PIECES - 1 else PW
                if i == 0:
                    pe.wait_ge(w_lo, j + 1)
                if n >= 4:
                    pe.wait_ge(tok_out, n - 3)
                product(c.ps[0:r, n % 4, 0:width], lambda s, k: XG[:, s, k, i * P:i * P + r],
                        lambda m, k: W[:, j % 2, m, k, 0:width]).then_inc(tok_ps, 1)
            pe.wait_ge(diag_ready, 1)
            pe.wait_ge(consts_in, 16)
            for i in range(TILES):
                r = ROWS[i]
                mm = pe.matmul(c.ps[:, 4 + i // 4, i % 4 * P:i % 4 * P + r], c.k("ones")[0:r], diag[0:r, i, 0:r],
                               start=True, stop=True)
            mm.then_inc(row_ps, 1)
            for m in range(16):
                n = TOK_PIECES + m // 2
                if m % 2 == 0:
                    pe.wait_ge(w_lo, n + 1)
                for h in range(2):
                    u = 2 * m + h
                    if u >= 4:
                        pe.wait_ge(chan_scaled, u - 3)
                    else:
                        pe.wait_ge(tok_out, NTU)
                    product(c.ps[:, u % 4, 0:HALF], lambda s, k: W[:, n % 2, s, k, m % 2 * P:(m % 2 + 1) * P],
                            lambda q, k: XG[:, q, k, h * HALF:(h + 1) * HALF]).then_inc(chan_ps, 1)

        @block.vector
        def _(dve):
            link = c.vsteps.on(dve)

            def lo(n):
                dve.wait_ge(w_hi, n + 1)
                width = TAIL if n == TOK_PIECES - 1 else PW
                dve.tensor_tensor(W[:, n % 2, 1, :, 0:width], raw[:, n % 2, :, 0:width],
                                  W[:, n % 2, 0, :, 0:width].bitcast(F32), ALU.subtract).then_inc(w_lo, 1)

            def finish_gate(m):
                dve.wait_ge(chan_tanh, m + 1)
                dve.tensor_scalar(sg[:, m % 4], sg[:, m % 4], 0.5, 0.5, ALU.mult, ALU.add).then_inc(gate_ready, 1)

            def mul(o, a, b_):
                return dve.tensor_tensor(o, a, b_, ALU.mult)

            def complex_mul(o_re, o_im, a, b_, tmp):
                mul(tmp[0], a[0], b_[0])
                mul(tmp[1], a[1], b_[1])
                mul(tmp[2], a[0], b_[1])
                link(mul(tmp[3], a[1], b_[0]))
                dve.tensor_tensor(o_re, tmp[0], tmp[1], ALU.subtract)
                link(dve.tensor_tensor(o_im, tmp[2], tmp[3], ALU.add))

            a_re, a_im = par[:, 0], par[:, 1]

            def s5_angles():
                dve.wait_ge(par_in, 48)
                link(dve.tensor_scalar(cc[:, 1], cc[:, 1], -1.0, None, ALU.mult))
                dve.wait_ge(dt_exp, 1)
                mul(v[:, 1], a_re, v[:, 0]).then_inc(mag_exp, 1)
                link(mul(v[:, 3], a_im, v[:, 0]))
                link(dve.tensor_scalar(v[:, 4], v[:, 3], 1.0 / TWO_PI, None, ALU.mult))
                link(dve.tensor_copy(vi[:], v[:, 4]))
                link(dve.tensor_copy(v[:, 4], vi[:]))
                hi = 6.28125
                link(dve.scalar_tensor_tensor(v[:, 3], v[:, 4], -hi, v[:, 3], ALU.mult, ALU.add))
                link(dve.scalar_tensor_tensor(v[:, 3], v[:, 4], -(TWO_PI - hi), v[:, 3], ALU.mult, ALU.add))
                link(dve.tensor_scalar(v[:, 4], v[:, 3], float(np.pi), -TWO_PI, ALU.is_gt, ALU.mult))
                link(dve.tensor_tensor(v[:, 3], v[:, 3], v[:, 4], ALU.add))
                link(dve.tensor_scalar(v[:, 4], v[:, 3], float(-np.pi), TWO_PI, ALU.is_lt, ALU.mult))
                link(dve.tensor_tensor(v[:, 3], v[:, 3], v[:, 4], ALU.add))
                link(dve.tensor_scalar(v[:, 5], v[:, 3], 0.5, None, ALU.mult))
                link(dve.tensor_scalar(v[:, 4], v[:, 5], -1.0, None, ALU.mult))
                link(dve.tensor_tensor(v[:, 4], v[:, 4], v[:, 5], ALU.max))
                dve.tensor_scalar(v[:, 6], v[:, 4], -1.0, float(np.pi / 2), ALU.mult, ALU.add).then_inc(sin_ready, 1)

            def s5_powers():
                dve.wait_ge(sin_done, 1)
                dve.wait_ge(dt_exp, 2)
                link(mul(v[:, 9], v[:, 7], v[:, 8]))
                link(mul(v[:, 10], v[:, 7], v[:, 7]))
                link(dve.tensor_scalar(v[:, 9], v[:, 9], 2.0, None, ALU.mult))
                link(dve.tensor_scalar(v[:, 10], v[:, 10], -2.0, 1.0, ALU.mult, ALU.add))
                mul(pw[:, 0, 1], v[:, 2], v[:, 10])
                link(mul(pw[:, 1, 1], v[:, 2], v[:, 9]))
                dve.memset(pw[:, 0, 0], 1.0)
                dve.memset(pw[:, 1, 0], 0.0)
                for n in (1, 2, 4):
                    a = [pw[:, r, 1:1 + n] for r in range(2)]
                    m = [pw[:, r, n:n + 1].broadcast_to([P, n, ST]) for r in range(2)]
                    complex_mul(pw[:, 0, n + 1:2 * n + 1], pw[:, 1, n + 1:2 * n + 1], a, m,
                                [tw[:, q, 0:n] for q in range(4)])

            tb, tt = ([t4[:, a, q * 256:(q + 1) * 256].rearrange("p (s e) -> p s e", s=ST) for q in range(4)]
                      for a in range(2))

            def s5_inputs():
                link(mul(v[:, 4], a_re, a_re))
                link(mul(v[:, 5], a_im, a_im))
                link(dve.tensor_tensor(v[:, 4], v[:, 4], v[:, 5], ALU.add))
                link(dve.reciprocal(v[:, 4], v[:, 4]))
                link(dve.tensor_scalar(v[:, 5], pw[:, 0, 1], -1.0, None, ALU.add))
                mul(v[:, 6], v[:, 5], a_re)
                mul(v[:, 7], pw[:, 1, 1], a_im)
                mul(v[:, 8], pw[:, 1, 1], a_re)
                link(mul(v[:, 9], v[:, 5], a_im))
                dve.tensor_tensor(v[:, 10], v[:, 6], v[:, 7], ALU.add)
                link(dve.tensor_tensor(v[:, 11], v[:, 8], v[:, 9], ALU.subtract))
                mul(v[:, 12], v[:, 10], v[:, 4])
                link(mul(v[:, 13], v[:, 11], v[:, 4]))
                f = [v[:, 12 + r].unsqueeze(2).broadcast_to([P, ST, 16]) for r in range(2)]
                complex_mul(bb[:, 0], bb[:, 1], f, [b[:, 0], b[:, 1]], tb)

            def s5_slots(first):
                for s in (first, first + 1):
                    complex_mul(Z[:, 0, :, s], Z[:, 1, :, s], [by_channel(pw, r, CH - 1 - s) for r in range(2)],
                                [bb[:, 0], bb[:, 1]], tt if s % 2 else tb)

            dve.memset(x[64:P, 4, :], 0.0).then_inc(tail_zero, 1)
            dve.memset(c.z[64:P, 4, :], 0.0)
            dve.wait_ge(g_in, 16)
            for k in range(KD):
                dve.wait_ge(xg_hi, k + 1)
                dve.scalar_tensor_tensor(XG[:, 1, k], xT[:, k], gcol[:, k:k + 1], XG[:, 0, k].bitcast(F32), ALU.mult,
                                         ALU.subtract).then_inc(xg_lo, 1)
            lo(0)
            dve.wait_ge(square_done, TILES)
            dve.tensor_scalar(ss[:], ss[:], 1.0 / D, EPS, ALU.mult, ALU.add).then_inc(mean_ready, 1)
            dve.wait_ge(root_done, 1)
            dve.reciprocal(rinv[:], ss[:]).then_inc(rinv_ready, 1)
            lo(1)
            dve.wait_ge(rinv_ready, 1)
            dve.wait_ge(consts_in, 16)
            for i in range(TILES):
                ins = dve.tensor_scalar(diag[:, i], c.k("ident"), rinv[:, i:i + 1], None, ALU.mult)
            ins.then_inc(diag_ready, 1)
            lo(2)
            s5_angles()
            lo(3)
            s5_powers()
            lo(4)
            s5_inputs()
            for n in range(4):
                lo(5 + n)
                dve.wait_ge(xg_lo, KD)
                s5_slots(2 * n)
            lo(9)
            dve.wait_ge(row_ps, 1)
            link(dve.tensor_copy(rinv_row[:, 0:512], c.ps[:, 4, :]))
            link(dve.tensor_copy(rinv_row[:, 512:TOK], c.ps[:, 5, 0:64]))
            dve.wait_ge(gates_ready, 1)
            link(dve.tensor_scalar(c.gate[:], c.gate[:], 0.5, 0.5, ALU.mult, ALU.add))
            for m in range(16):
                for h in range(2):
                    u = 2 * m + h
                    dve.wait_ge(chan_ps, u + 1)
                    if m >= 4:
                        dve.wait_ge(gate_stored[m % 4], 16 * (m // 4))
                    dve.tensor_tensor(sg[:, m % 4, h * HALF:(h + 1) * HALF], c.ps[:, u % 4, 0:HALF],
                                      rinv_row[:, h * HALF:(h + 1) * HALF], ALU.mult).then_inc(chan_scaled, 1)
                if m >= 1:
                    finish_gate(m - 1)
                if m % 2 == 1 and m < 12:
                    lo(TOK_PIECES + m // 2 + 2)
            finish_gate(15)

        @block.gpsimd
        def _(pool):
            link = c.gsteps.on(pool)
            pool.wait_ge(consts_in, 16)
            for i in range(TILES):
                pool.wait_ge(tok_out, NTU - TILES + i + 1)
                co = c.k("cos")[:, i * 32:(i + 1) * 32]
                si = c.k("sin")[:, i * 32:(i + 1) * 32]
                q = c.z[:, i, ZQ:ZQ + 512].rearrange("p (h f d) -> p h f d", f=2, d=32)
                kk = c.z[:, i, ZK:ZK + 768].rearrange("p (s v g f d) -> p s v g f d", s=3, v=2, g=2, f=2)
                parts = [(q[:, :, 0], q[:, :, 1], 8)]
                parts += [(kk[:, s, 0, :, 0], kk[:, s, 0, :, 1], 2) for s in range(3)]
                for lo, hi, n in parts:
                    cb = co.unsqueeze(1).broadcast_to([P, n, 32])
                    sb_ = si.unsqueeze(1).broadcast_to([P, n, 32])
                    t = [rt[:, a, 0:n * 32].rearrange("p (h d) -> p h d", d=32) for a in range(4)]
                    pool.tensor_tensor(t[0], lo, cb, ALU.mult)
                    pool.tensor_tensor(t[1], hi, sb_, ALU.mult)
                    pool.tensor_tensor(t[2], hi, cb, ALU.mult)
                    link(pool.tensor_tensor(t[3], lo, sb_, ALU.mult))
                    pool.tensor_tensor(lo, t[0], t[1], ALU.subtract)
                    link(pool.tensor_tensor(hi, t[2], t[3], ALU.add))
                pool.engine_nop().then_inc(roped, 1)
                for m in GATES_AFTER[i]:
                    pool.wait_ge(gate_ready, m + 1)
                    pool.dma_start(c.d["sig"][m], sg[:, m % 4]).then_inc(gate_stored[m % 4], 16)
            for i in range(4):
                pool.wait_ge(gate_stored[i], 64)


def by_channel(pw, r, k):
    return pw[:, r, k].unsqueeze(2).broadcast_to([P, ST, 16])


def ssm_build(nc, c):
    with ExitStack() as ctx:
        local = local_tensor(nc, ctx, "ssm_build")
        region = Region(local, 0, LOCAL)
        def sem(name):
            return c.sem("ssm_build_" + name)

        dd = region.take([P, GROUPS, 16])
        t4 = region.take([P, 2, 1024])
        pw, cc, Z = c.pw, c.cc, c.Z
        u_rows = region.take([NCH, CH, GROUPS, 16])
        ch = region.take([NCH, GROUPS, CH * 16])
        wt = region.take([P, 2, ST, P])
        mt = region.take([P, GROUPS * 16])

        d_in, u_in, u_grouped = sem("d_in"), sem("u_in"), sem("u_grouped")
        tr_ps, tr_out, mt_ps, mt_ready, kt_zero, kt_in, st_ps, st_out, h0_in = (
            sem("tr_ps"), sem("tr_out"), sem("mt_ps"), sem("mt_ready"), sem("kt_zero"), sem("kt_in"),
            sem("st_ps"), sem("st_out"), sem("h0_in"))
        UB = 4
        NU = GROUPS // UB
        NZ = 2 * ST // 4

        block = ctx.enter_context(nc.Block())

        @block.sync
        def _(sp):
            sp.dma_start(u_rows.rearrange("k s g e -> k (s g e)"), c.d["u"].rearrange("(k s) d -> k (s d)", s=CH)).then_inc(u_in, 16)
            sp.dma_start(dd[:], c.d["ssm_d"]).then_inc(d_in, 16)
            sp.dma_start(c.X[:, PCH + 1:PCH + 1 + NB], c.d["state"]).then_inc(h0_in, 16)
            sp.wait_ge(mt_ready, 2)
            sp.wait_ge(kt_zero, 1)
            for t in range(CH):
                sp.dma_start(c.KT[0:16 * (t + 1), t, :], mt[16 * (CH - 1 - t):P, :]).then_inc(kt_in, 16)
            sp.wait_ge(kt_in, 16 * CH)
            sp.wait_ge(h0_in, 16)

        @block.scalar
        def _(act):
            for n in range(NU + NZ):
                act.wait_ge(tr_ps, n + 1)
                if n < NU:
                    act.activation(c.U[:, UB * n:UB * (n + 1)],
                                   c.ps[:, n % 2, 0:UB * NCH].rearrange("p (g k) -> p g k", g=UB),
                                   ACT.Copy).then_inc(tr_out, 1)
                else:
                    m = n - NU
                    dst = wt[:].rearrange("p r s q -> p (r s q)")[:, 512 * m:512 * (m + 1)]
                    act.activation(dst, c.ps[:, n % 2, :], ACT.Copy).then_inc(tr_out, 1)
            for tl in range(ST):
                act.wait_ge(st_ps, tl + 1)
                src = c.ps[:, 4 + tl % 2, 0:2 * NCH].rearrange("p (r k) -> p k r", r=2)
                act.activation(c.S[:, :, :, tl], src, ACT.Copy).then_inc(st_out, 1)

        @block.tensor
        def _(pe):
            pe.wait_ge(u_grouped, 2)
            for n in range(NU):
                if n >= 2:
                    pe.wait_ge(tr_out, n - 1)
                for a in range(UB):
                    g = UB * n + a
                    mm = pe.transpose(c.ps[:, n % 2, a * NCH:(a + 1) * NCH], ch[:, g], c.k("ident")[0:NCH, 0:NCH])
                mm.then_inc(tr_ps, 1)
            zf = Z[:].rearrange("p r s k e -> p (r s) (k e)")
            for n in range(NU, NU + NZ):
                pe.wait_ge(tr_out, n - 1)
                for a in range(4):
                    mm = pe.transpose(c.ps[:, n % 2, a * P:(a + 1) * P], zf[:, 4 * (n - NU) + a], c.k("ident"))
                mm.then_inc(tr_ps, 1)
            for g in range(GROUPS):
                lo = HD * (g % 2)
                for r in range(2):
                    mm = pe.matmul(c.ps[:, 2 + g % 2, g // 2 * 16:(g // 2 + 1) * 16], zf[lo:lo + HD, r * ST + g // 2],
                                   cc[lo:lo + HD, r, g // 2], start=r == 0, stop=r == 1)
            mm.then_inc(mt_ps, 1)
            pe.wait_ge(tr_out, NU + NZ)
            for tl in range(ST):
                if tl >= 2:
                    pe.wait_ge(st_out, tl - 1)
                for r in range(2):
                    for h in range(2):
                        mm = pe.matmul(c.ps[HD * h:HD * (h + 1), 4 + tl % 2, r * NCH:(r + 1) * NCH],
                                       wt[:, r, tl, HD * h:HD * (h + 1)], c.U[:, 2 * tl + h],
                                       start=True, stop=True)
                mm.then_inc(st_ps, 1)

        @block.gpsimd
        def _(pool):
            pool.memset(c.KT[:], 0.0).then_inc(kt_zero, 1)
            pool.memset(c.X[:, 0:1], 0.0)

        @block.vector
        def _(dve):
            link = c.vsteps.on(dve)

            def mul(o, a, bb_):
                return dve.tensor_tensor(o, a, bb_, ALU.mult)

            dve.wait_ge(u_in, 16)
            for a in range(2):
                half = slice(a * GROUPS // 2, (a + 1) * GROUPS // 2)
                dve.tensor_copy(ch[:, half].rearrange("k g (s e) -> k s g e", s=CH), u_rows[:, :, half]).then_inc(u_grouped, 1)
            dve.wait_ge(u_grouped, 2)
            tb, tt = ([t4[:, a, q * 256:(q + 1) * 256].rearrange("p (s e) -> p s e", s=ST) for q in range(4)]
                      for a in range(2))
            for t in range(CH):
                p_re, p_im = by_channel(pw, 0, t + 1), by_channel(pw, 1, t + 1)
                q4 = tt if t % 2 else tb
                mul(q4[0], cc[:, 0], p_re)
                mul(q4[1], cc[:, 1], p_im)
                mul(q4[2], cc[:, 1], p_re)
                link(mul(q4[3], cc[:, 0], p_im))
                dve.tensor_tensor(c.C[:, 0, :, t], q4[0], q4[1], ALU.add)
                link(dve.tensor_tensor(c.C[:, 1, :, t], q4[2], q4[3], ALU.subtract))
            dve.tensor_copy(c.A8[:, 0, 0], pw[:, 0, 8])
            dve.tensor_copy(c.A8[:, 0, 1], pw[:, 0, 8])
            dve.tensor_scalar(c.A8[:, 1, 0], pw[:, 1, 8], -1.0, None, ALU.mult)
            dve.tensor_copy(c.A8[:, 1, 1], pw[:, 1, 8])
            e7 = c.k("eye7").unsqueeze(1).broadcast_to([P, GROUPS, 16])
            dve.wait_ge(d_in, 16)
            link(mul(dd[:], dd[:], e7))
            dve.wait_ge(mt_ps, 1)
            for h in range(2):
                dve.tensor_tensor(mt[:].rearrange("p (s h e) -> p s h e", h=2, e=16)[:, :, h],
                                  c.ps[:, 2 + h, 0:ST * 16].rearrange("p (s e) -> p s e", e=16),
                                  dd[:].rearrange("p (s h) e -> p s h e", h=2)[:, :, h], ALU.add).then_inc(mt_ready, 1)


def prompt(nc, c):
    with ExitStack() as ctx:
        region = Region(local_tensor(nc, ctx, "prompt"), 0, LOCAL)
        def sem(name):
            return c.sem("prompt_" + name)

        kT = region.take([P, 2, SEQ])
        qT = region.take([P, HG, SEQ])
        rows = region.take([32, 2, 2, 16 * HD])
        hT = region.take([P, 32, 32])
        trail = region.take([HD, 4, 32])
        hid = region.take([HD, 4, 32])
        gt = region.take([HD, 2, 4, 32])
        kc = region.take([P, 32])
        vc = region.take([32, P])
        pr = region.take([P, 4, 512])
        pt = region.take([P, 2, 512])
        st = region.take([P, 8, 4])
        at = region.take([P, 4, 512])
        sc = region.take([P, 2, 2, ST])

        rows_in, tr_ps, tr_out, cmp_ps, trail_out, hid_add, hid_scaled, hid_tanh, hid_ready, kc_ps, kc_out = (
            sem("rows_in"), sem("tr_ps"), sem("tr_out"), sem("cmp_ps"), sem("trail_out"), sem("hid_add"),
            sem("hid_scaled"), sem("hid_tanh"), sem("hid_ready"), sem("kc_ps"), sem("kc_out"))
        score_ps, bias_ready, exp_done, pt_ps, pt_out, pv_ps, unit_out, at_ps, at_out, scanned, pe_ps = (
            sem("score_ps"), sem("bias_ready"), sem("exp_done"), sem("pt_ps"), sem("pt_out"), sem("pv_ps"),
            sem("unit_out"), sem("at_ps"), sem("at_out"), sem("scanned"), sem("pe_ps"))

        win_moved = sem("win_moved")

        work = [([c.z[:, i, ZK + 256 * (1 + s):ZK + 256 * (1 + s) + P] for i in range(4)], kT[:, s, :])
                for s in range(2)]
        for h in range(HG):
            work.append(([c.z[:, i, ZQ + h * P:ZQ + (h + 1) * P]
                          for i in range(4)], qT[:, h, :]))
        units = [(i, g, h, s) for i in range(4) for g in range(2) for h in range(HG) for s in range(3)]
        N = len(units)
        LAG = 3

        block = ctx.enter_context(nc.Block())

        @block.sync
        def _(sp):
            src = c.o["kv"][0:SEQ].rearrange("(n l) (s g d) -> n s g l d", l=16, s=4, g=2)
            for s in range(2):
                for g in range(2):
                    sp.dma_start(rows[:, s, g].rearrange("n (l d) -> n l d", l=16), src[:, s, g]).then_inc(rows_in, 16)
            sp.dma_start(c.o["win_s"][:, 0:SEQ - NT], c.d["win_rows"][:, NT:SEQ]).then_inc(win_moved, 16)
            sp.wait_ge(rows_in, 64)
            sp.wait_ge(win_moved, 16)

        @block.tensor
        def _(pe):
            for n, (srcs, _) in enumerate(work):
                if n >= 2:
                    pe.wait_ge(tr_out, n - 1)
                for a, src in enumerate(srcs):
                    mm = pe.transpose(c.ps[:, n % 2, a * P:(a + 1) * P], src, c.k("ident"))
                mm.then_inc(tr_ps, 1)
            pe.wait_ge(rows_in, 64)
            for n in range(2):
                pe.wait_ge(tr_out, len(work) + n - 1)
                for g in range(2):
                    for j in range(8):
                        a = g * 8 + j
                        mm = pe.transpose(c.ps[:, n % 2, a * 32:(a + 1) * 32], rows[:, n, g, j * P:(j + 1) * P], c.k("ident")[0:32, 0:32])
                mm.then_inc(tr_ps, 1)
            pe.wait_ge(tr_out, len(work) + 2)
            pe.wait_ge(c.w1_in, 16 * 4)
            for s in range(2):
                for g in range(2):
                    for j in range(8):
                        mm = pe.matmul(c.ps[:, 2, (s * 2 + g) * 32:(s * 2 + g + 1) * 32], c.w1[:, s, j],
                                       hT[:, s * 16 + g * 8 + j], start=j == 0, stop=j == 7)
            mm.then_inc(cmp_ps, 1)
            for s in range(2):
                for a in range(16):
                    mm = pe.matmul(c.ps[0:HD, 3, 64 + s:65 + s], c.w1[:, s, a % 8, a // 8 * HD:(a // 8 + 1) * HD],
                                   c.pe[:, s, a:a + 1], start=a == 0, stop=a == 15)
            mm.then_inc(pe_ps, 1)
            pe.wait_ge(hid_ready, 1)
            for g in range(2):
                pe.matmul(c.ps[HD * g:HD * (g + 1), 3, 0:32], c.w2[:, 0], hid[:, g], start=True, stop=True)
                mm = pe.matmul(c.ps[0:32, 4, g * HD:(g + 1) * HD], hid[:, 2 + g], c.w2[:, 1], start=True, stop=True)
            mm.then_inc(kc_ps, 1)
            pe.wait_ge(kc_out, 2)
            for step in range(N + LAG + 1):
                if step < N:
                    i, g, h, s = units[step]
                    lo, n = HD * g, 32 if s == 0 else (i + 1) * P
                    if step >= 4:
                        pe.wait_ge(exp_done, step - 3)
                    k = kc[lo:lo + HD, :] if s == 0 else kT[lo:lo + HD, s - 1, 0:n]
                    pe.matmul(c.ps[:, step % 4, 0:n], qT[lo:lo + HD, h, i * P:(i + 1) * P], k,
                              start=True, stop=True).then_inc(score_ps, 1)
                u = step - LAG
                if 0 <= u < N:
                    i, g, h, s = units[u]
                    pe.wait_ge(exp_done, u + 1)
                    if u >= 2:
                        pe.wait_ge(pt_out, u - 1)
                    if s == 0:
                        mm = pe.transpose(c.ps[0:32, 4 + u % 2, 0:P], pr[:, u % 4, 0:32], c.k("ident"))
                    else:
                        for a in range(i + 1):
                            mm = pe.transpose(c.ps[:, 4 + u % 2, a * P:(a + 1) * P], pr[:, u % 4, a * P:(a + 1) * P],
                                              c.k("ident"))
                    mm.then_inc(pt_ps, 1)
                u = step - LAG - 1
                if 0 <= u < N:
                    i, g, h, s = units[u]
                    pe.wait_ge(pt_out, u + 1)
                    if u >= 2:
                        pe.wait_ge(unit_out, u - 1)
                    if s == 0:
                        mm = pe.matmul(c.ps[:, 6 + u % 2, 0:HD], pt[0:31, u % 2, 0:P], vc[0:31, g * HD:(g + 1) * HD],
                                       start=True, stop=True)
                    else:
                        col = ZK + 256 * s + P + g * HD
                        for a in range(i + 1):
                            mm = pe.matmul(c.ps[:, 6 + u % 2, 0:HD], pt[:, u % 2, a * P:(a + 1) * P],
                                           c.z[:, a, col:col + HD], start=a == 0, stop=a == i)
                    mm.then_inc(pv_ps, 1)
            for n in range(4):
                if n == 0:
                    pe.wait_ge(unit_out, N)
                if n >= 2:
                    pe.wait_ge(at_out, n - 1)
                for i in range(4):
                    mm = pe.transpose(c.ps[:, n % 2, i * P:(i + 1) * P], at[:, i, n * P:(n + 1) * P], c.k("ident"))
                mm.then_inc(at_ps, 1)

        @block.scalar
        def _(act):
            for n, (_, dst) in enumerate(work):
                act.wait_ge(tr_ps, n + 1)
                act.activation(dst, c.ps[:, n % 2, :], ACT.Copy).then_inc(tr_out, 1)
            for n in range(2):
                act.wait_ge(tr_ps, len(work) + n + 1)
                act.activation(hT[:, n * 16:(n + 1) * 16], c.ps[:, n % 2, :].rearrange("p (a n) -> p a n", n=32),
                               ACT.Copy).then_inc(tr_out, 1)
            act.wait_ge(cmp_ps, 1)
            for s in range(2):
                act.activation(trail[:, 2 * s:2 * s + 2], c.ps[HD:P, 2, s * 64:(s + 1) * 64].rearrange("p (g n) -> p g n", g=2),
                               ACT.Copy).then_inc(trail_out, 1)
            act.wait_ge(hid_scaled, 1)
            act.activation(gt[:, 1, :, 0:31], gt[:, 0, :, 0:31], ACT.Tanh, scale=GELU_B).then_inc(hid_tanh, 1)
            act.wait_ge(kc_ps, 1)
            act.activation(kc[:], c.ps[:, 3, 0:32], ACT.Copy).then_inc(kc_out, 1)
            act.activation(vc[:], c.ps[0:32, 4, 0:P], ACT.Copy).then_inc(kc_out, 1)
            for step in range(N + LAG):
                if step < N:
                    i, g, h, s = units[step]
                    n = 32 if s == 0 else (i + 1) * P
                    act.wait_ge(bias_ready, step + 1)
                    if step >= 4:
                        act.wait_ge(pt_ps, step - 3)
                    if step >= 8:
                        act.wait_ge(unit_out, step - 7)
                    act.activation(pr[:, step % 4, 0:n], c.ps[:, step % 4, 0:n], ACT.Exp, bias=st[:, step % 8, 1:2],
                                   scale=SCALE, accum_out=st[:, step % 8, 2:3]).then_inc(exp_done, 1)
                u = step - LAG
                if u >= 0:
                    i, g, h, s = units[u]
                    act.wait_ge(pt_ps, u + 1)
                    if u >= 2:
                        act.wait_ge(pv_ps, u - 1)
                    r, n = (32, P) if s == 0 else (P, (i + 1) * P)
                    act.activation(pt[0:r, u % 2, 0:n], c.ps[0:r, 4 + u % 2, 0:n], ACT.Copy).then_inc(pt_out, 1)
            for n in range(4):
                act.wait_ge(at_ps, n + 1)
                act.activation(c.aT[:, n, 0:SEQ], c.ps[:, n % 2, :], ACT.Copy).then_inc(at_out, 1)

        @block.vector
        def _(dve):
            link = c.vsteps.on(dve)
            dve.tensor_copy(c.z4[:], c.z[:, 4])
            dve.wait_ge(pe_ps, 1)
            link(dve.tensor_tensor(c.b1[:], c.b1[:], c.ps[0:HD, 3, 64:66], ALU.add))
            dve.wait_ge(trail_out, 2)
            link(dve.memset(hid[:], 0.0))
            gelu_hidden(dve, link, c.b1, hid[:, :, 0:31],
                        c.ps[0:HD, 2, 0:P].rearrange("p (a n) -> p a n", a=4)[:, :, 0:31],
                        trail[:, :, 1:32], gt[:, :, :, 0:31], lambda ins: ins.then_inc(hid_scaled, 1),
                        lambda: dve.wait_ge(hid_tanh, 1))
            dve.engine_nop().then_inc(hid_ready, 1)
            for step in range(N + LAG + 1):
                if step < N:
                    i, g, h, s = units[step]
                    n = 32 if s == 0 else (i + 1) * P
                    dve.wait_ge(score_ps, step + 1)
                    S = c.ps[:, step % 4]
                    if s == 0:
                        link(dve.tensor_tensor(S[:, 0:32], S[:, 0:32], c.k("cmask")[:, i * 32:(i + 1) * 32], ALU.add))
                    else:
                        link(dve.tensor_tensor(S[:, i * P:n], S[:, i * P:n], c.k("causal"), ALU.add))
                    if step >= 4:
                        dve.wait_ge(exp_done, step - 3)
                    link(dve.tensor_reduce(st[:, step % 8, 0:1], S[:, 0:n], AX, ALU.max))
                    dve.tensor_scalar(st[:, step % 8, 1:2], st[:, step % 8, 0:1], -1.0e25, -SCALE, ALU.max,
                                      ALU.mult).then_inc(bias_ready, 1)
                u = step - LAG - 1
                if 0 <= u < N:
                    i, g, h, s = units[u]
                    head = g * HG + h
                    dve.wait_ge(exp_done, u + 1)
                    link(dve.tensor_scalar(st[:, u % 8, 3:4], st[:, u % 8, 2:3], 1.0e-30, None, ALU.max))
                    link(dve.reciprocal(st[:, u % 8, 3:4], st[:, u % 8, 3:4]))
                    link(dve.tensor_tensor(st[:, u % 8, 3:4], st[:, u % 8, 3:4], c.gate[:, i, head * 3 + s:head * 3 + s + 1],
                                           ALU.mult))
                    dve.wait_ge(pv_ps, u + 1)
                    o = at[:, i, head * HD:(head + 1) * HD]
                    if s == 0:
                        dve.tensor_scalar(o, c.ps[:, 6 + u % 2, 0:HD], st[:, u % 8, 3:4], None,
                                          ALU.mult).then_inc(unit_out, 1)
                    else:
                        dve.wait_ge(unit_out, u)
                        dve.scalar_tensor_tensor(o, c.ps[:, 6 + u % 2, 0:HD], st[:, u % 8, 3:4], o, ALU.mult,
                                                 ALU.add).then_inc(unit_out, 1)

        @block.gpsimd
        def _(pool):
            link = c.gsteps.on(pool)
            for k in range(PCH):
                x = c.X[:, k]
                pool.tensor_tensor(sc[:, 0], c.A8[:, 0], x, ALU.mult)
                link(pool.tensor_tensor(sc[:, 1], c.A8[:, 1], x[:, ::-1], ALU.mult))
                link(pool.tensor_tensor(sc[:, 0], sc[:, 0], c.S[:, k], ALU.add))
                link(pool.tensor_tensor(c.X[:, k + 1], sc[:, 0], sc[:, 1], ALU.add))
            pool.tensor_copy(c.XM[:, :, :, 0:PCH], c.X[:, 0:PCH].rearrange("p k r s -> p r s k"))
            pool.tensor_copy(c.XM[:, :, :, PCH:NCH], c.X[:, PCH + 1:PCH + 1 + NB].rearrange("p k r s -> p r s k"))
            pool.tensor_copy(c.fin[:, 0], c.X[:, PCH])
            for b in range(NB):
                x = c.X[:, PCH + 1 + b]
                pool.tensor_tensor(sc[:, 0], c.A8[:, 0], x, ALU.mult)
                link(pool.tensor_tensor(sc[:, 1], c.A8[:, 1], x[:, ::-1], ALU.mult))
                link(pool.tensor_tensor(sc[:, 0], sc[:, 0], c.S[:, PCH + b], ALU.add))
                link(pool.tensor_tensor(c.fin[:, 1 + b], sc[:, 0], sc[:, 1], ALU.add))
            pool.dma_start(c.o["ssm"], c.fin[:].rearrange("p k r s -> p (k r s)")).then_inc(scanned, 16)
            pool.wait_ge(scanned, 16)


def gelu_hidden(dve, link, bias, out, lead, trail, tmp, scaled, wait_tanh):
    n = out.shape[1] // 2
    for s in range(2):
        link(dve.scalar_tensor_tensor(out[:, s * n:(s + 1) * n], lead[:, s * n:(s + 1) * n], bias[:, s:s + 1],
                                      trail[:, s * n:(s + 1) * n], ALU.add, ALU.add))
    gelu_tail(dve, link, out, out, tmp[:, 0], tmp[:, 1], scaled, wait_tanh)


def gelu_tail(dve, link, out, x, t, e, scaled, wait_tanh):
    link(dve.tensor_tensor(t, x, x, ALU.mult))
    link(dve.tensor_scalar(t, t, GELU_A, 1.0, ALU.mult, ALU.add))
    scaled(dve.tensor_tensor(t, t, x, ALU.mult))
    wait_tanh()
    link(dve.tensor_scalar(e, e, 0.5, 0.5, ALU.mult, ALU.add))
    link(dve.tensor_tensor(out, x, e, ALU.mult))


def sample(nc, c):
    with ExitStack() as ctx:
        low = Region(c.arena, AT_STATE, AT_LOCAL)
        region = Region(local_tensor(nc, ctx, "sample"), 0, LOCAL)
        def sem(name):
            return c.sem("sample_" + name)

        NP = NB // 2
        pgt = region.take([1, NB * PAGES], I32)
        pg = [Region(c.arena, AT_Z, AT_SSM).take([P, 2 * PAGES, 4, P]), region.take([P, 2 * PAGES, 4, P])]
        wk = low.take([P, 2, 2, SEQ])
        wv = low.take([P, 2, 2, 4, P])
        qs = low.take([P, HG, 64])
        kn = region.take([P, 2, 64])
        qb = region.take([P, NB, 2, HG, NT])
        trail = region.take([HD, 4, P])
        hid = region.take([HD, 4, P])
        gt = region.take([HD, 2, 4, P])
        kc = region.take([P, P])
        vc = region.take([63, 2, P])
        S = region.take([P, 1088 + 576])
        pc = region.take([P, 64])
        imp = region.take([P, 70])
        half = region.take([P, 68])
        b17 = region.take([P, 6, 17])
        s1 = region.take([P, 16])
        gb = region.take([P, 3, 8])
        gsel = region.take([P, 3])
        pt = region.take([P, 16 * P])
        o = region.take([P, 2 * HD])

        imp_out = sem("imp_out")
        table_in, small_ps, small_out, qb_zero = (
            sem("table_in"), sem("small_ps"), sem("small_out"), sem("qb_zero"))
        pages_in = [sem(f"pages_in{i}") for i in range(2)]
        cmp_ps, trail_out, hid_scaled, hid_tanh, hid_ready, kc_ps, kc_out = (
            sem("s_cmp_ps"), sem("s_trail_out"), sem("s_hid_scaled"), sem("s_hid_tanh"), sem("s_hid_ready"),
            sem("s_kc_ps"), sem("s_kc_out"))
        wide_ps, sc_ps, bias_c, exp_c, pc_ready, imp_ps, pct_ps, pct_out = (
            sem("wide_ps"), sem("sc_ps"), sem("bias_c"), sem("exp_c"), sem("pc_ready"),
            sem("imp_ps"), sem("pct_ps"), sem("pct_out"))
        bias_w, exp_w, pt_ps, pt_out, pv_ps, o_ready, ot_ps, ot_out = (
            sem("bias_w"), sem("exp_w"), sem("s_pt_ps"), sem("s_pt_out"), sem("s_pv_ps"), sem("o_ready"),
            sem("ot_ps"), sem("ot_out"))
        KT = [(0, a, P) for a in range(PAGES)] + [(0, PAGES, 64)] + [(1, a, P) for a in range(4)] + [(1, 4, 64)]
        OFF = [a * P for a in range(PAGES)] + [PAST] + [1088 + a * P for a in range(4)] + [1088 + SEQ]
        GROUPED = [list(range(a, min(a + 4, len(KT)))) for a in range(0, len(KT), 4)]

        block = ctx.enter_context(nc.Block())

        @block.sync
        def _(sp):
            sp.dma_start(pgt[:], c.d["page_table"]).then_inc(table_in, 16)
            sp.wait_ge(table_in, 16)
            for p in range(NP):
                if p >= 2:
                    sp.wait_ge(ot_out, 4 * (p - 1))
                for a in range(2 * PAGES):
                    v = sp.value_load(pgt[0:1, 2 * PAGES * p + a:2 * PAGES * p + a + 1], min_val=0, max_val=POOL - 1)
                    sp.dma_start(pg[p % 2][:, a], c.d["cache"][bass.ds(v, 1)].rearrange("o p s e -> (o p) s e")).then_inc(pages_in[p % 2], 16)
                sp.dma_start(wk[:, p % 2], c.d["win_kT"][:, 2 * p:2 * p + 2]).then_inc(pages_in[p % 2], 16)
                sp.dma_start(wv[:, p % 2], c.d["win_v"][:, 2 * p:2 * p + 2]).then_inc(pages_in[p % 2], 16)

        @block.tensor
        def _(pe):
            z4 = c.z4[0:64]
            idn = c.k("ident")[0:64, 0:64]
            for h in range(HG):
                pe.transpose(c.ps[:, 0, h * 64:(h + 1) * 64],
                             z4[:, ZQ + h * P:ZQ + (h + 1) * P], idn)
            for s in range(2):
                pe.transpose(c.ps[:, 0, 256 + s * 64:320 + s * 64], z4[:, ZK + 256 * (s + 1):ZK + 256 * (s + 1) + P], idn)
            for p in range(NP):
                mm = pe.matmul(c.ps[:, 1, p * 24:(p + 1) * 24], c.k("expand")[0:64, p * P:(p + 1) * P], c.gate[0:64, 4],
                               start=True, stop=True)
            mm.then_inc(small_ps, 1)
            pe.wait_ge(small_out, 3)
            pe.wait_ge(qb_zero, 9)
            for p in range(NP):
                b = p % 2
                pe.wait_ge(pages_in[b], 16 * (2 * PAGES + 2) * (p // 2 + 1))
                if p:
                    pe.wait_ge(ot_out, 4 * p)
                for s in range(2):
                    for g in range(2):
                        for j in range(8):
                            mov = pg[b][:, :, s].rearrange("p a (g j n) -> p a g j n", g=2, j=8)[:, :, g, j]
                            mm = pe.matmul(c.ps[:, 5, (s * 2 + g) * P:(s * 2 + g + 1) * P], c.w1[:, s, j], mov,
                                           start=j == 0, stop=j == 7)
                mm.then_inc(cmp_ps, 1)
                for e in range(2):
                    row = slice(HD * e, HD * (e + 1))
                    q = qb[:, 2 * p + e].rearrange("p g h t -> p (g h t)")
                    for a in range(2):
                        pe.matmul(c.ps[row, a, :], q, pg[b][:, e * PAGES + 4 * a:e * PAGES + 4 * a + 4, 2], start=True, stop=True)
                    pe.matmul(c.ps[row, 2, 0:64], q, kn[:, 0], start=True, stop=True)
                    pe.matmul(c.ps[row, 3, :], q, wk[:, b, e], start=True, stop=True)
                    mm = pe.matmul(c.ps[row, 4, 0:64], q, kn[:, 1], start=True, stop=True)
                mm.then_inc(wide_ps, 1)
                pe.wait_ge(hid_ready, p + 1)
                for g in range(2):
                    pe.matmul(c.ps[HD * g:HD * (g + 1), 6, 0:P], c.w2[:, 0], hid[:, g], start=True, stop=True)
                    for e in range(2):
                        mm = pe.matmul(c.ps[0:63, 7, e * P + g * HD:e * P + (g + 1) * HD], hid[:, 2 + g, e * 64:e * 64 + 63],
                                       c.w2[:, 1], start=True, stop=True)
                mm.then_inc(kc_ps, 1)
                pe.wait_ge(kc_out, 2 * p + 2)
                for e in range(2):
                    mm = pe.matmul(c.ps[HD * e:HD * (e + 1), 5, 0:63], qb[:, 2 * p + e].rearrange("p g h t -> p (g h t)"),
                                   kc[:, e * 64:e * 64 + 63], start=True, stop=True)
                mm.then_inc(sc_ps, 1)
                pe.wait_ge(pc_ready, p + 1)
                pe.matmul(c.ps[:, 7, 256:319], c.k("same"), pc[:, 0:63], start=True, stop=True).then_inc(imp_ps, 1)
                pe.transpose(c.ps[0:63, 6, 0:P], pc[:, 0:63], c.k("ident")).then_inc(pct_ps, 1)
                pe.wait_ge(pct_out, p + 1)
                pe.wait_ge(imp_out, p + 1)
                for e in range(2):
                    for g in range(2):
                        lo = 64 * e + 32 * g
                        mm = pe.matmul(c.ps[lo:lo + 32, 7, 0:HD], pt[0:63, lo:lo + 32], vc[0:63, e, g * HD:(g + 1) * HD],
                                       start=True, stop=True, tile_position=(0, lo))
                mm.then_inc(pv_ps, 1)
                for n, tiles in enumerate(GROUPED):
                    m = len(GROUPED) * p + n
                    pe.wait_ge(exp_w, 2 * p + 1 + max(KT[t][0] for t in tiles))
                    if m >= 2:
                        pe.wait_ge(pt_out, m - 1)
                    for a, t in enumerate(tiles):
                        r = KT[t][2]
                        mm = pe.transpose(c.ps[0:r, m % 2, a * P:(a + 1) * P], S[:, OFF[t]:OFF[t] + r], c.k("ident"))
                    mm.then_inc(pt_ps, 1)
                pe.wait_ge(pt_out, len(GROUPED) * (p + 1))
                for w in range(2):
                    tiles = [t for t in range(len(KT)) if KT[t][0] == w]
                    for e in range(2):
                        for g in range(2):
                            lo = 64 * e + 32 * g
                            for t in tiles:
                                a, r = KT[t][1], KT[t][2]
                                if r == 64:
                                    v = c.z4[0:64, ZK + 256 * (w + 1) + P + g * HD:ZK + 256 * (w + 1) + P + (g + 1) * HD]
                                elif w == 0:
                                    v = pg[b][:, e * PAGES + a, 3, g * HD:(g + 1) * HD]
                                else:
                                    v = wv[:, b, e, a, g * HD:(g + 1) * HD]
                                mm = pe.matmul(c.ps[lo:lo + 32, 3 + w, 0:HD], pt[0:r, t * P + lo:t * P + lo + 32], v,
                                               start=t == tiles[0], stop=t == tiles[-1], tile_position=(0, lo))
                    mm.then_inc(pv_ps, 1)
                pe.wait_ge(o_ready, p + 1)
                pe.transpose(c.ps[:, 2, 0:P], o[:], c.k("ident")).then_inc(ot_ps, 1)

        @block.scalar
        def _(act):
            act.wait_ge(small_ps, 1)
            act.activation(qs[:], c.ps[:, 0, 0:256].rearrange("p (h t) -> p h t", h=HG), ACT.Copy).then_inc(small_out, 1)
            act.activation(kn[:], c.ps[:, 0, 256:384].rearrange("p (s t) -> p s t", s=2), ACT.Copy).then_inc(small_out, 1)
            act.activation(c.gs[:], c.ps[:, 1, 0:96].rearrange("p (a e) -> p a e", a=4), ACT.Copy).then_inc(small_out, 1)
            act.wait_ge(small_out, 1)
            act.wait_ge(qb_zero, 1)
            for g in range(2):
                r = slice(HD * g, HD * (g + 1))
                for h in range(HG):
                    act.activation(qb[r, :, g, h], qs[r, h].rearrange("p (b t) -> p b t", b=NB), ACT.Copy).then_inc(qb_zero, 1)
            for p in range(NP):
                act.wait_ge(cmp_ps, p + 1)
                if p:
                    act.wait_ge(hid_ready, p)
                for s in range(2):
                    act.activation(trail[:, 2 * s:2 * s + 2], c.ps[HD:P, 5, s * 256:(s + 1) * 256].rearrange("p (g n) -> p g n", g=2),
                                   ACT.Copy).then_inc(trail_out, 1)
                act.wait_ge(hid_scaled, p + 1)
                g4 = gt[:].rearrange("p r a (b n) -> p r (a b) n", b=2)[:, :, :, 0:63]
                act.activation(g4[:, 1], g4[:, 0], ACT.Tanh, scale=GELU_B).then_inc(hid_tanh, 1)
                act.wait_ge(kc_ps, p + 1)
                act.activation(kc[:], c.ps[:, 6, 0:P], ACT.Copy).then_inc(kc_out, 1)
                act.activation(vc[:], c.ps[0:63, 7, 0:2 * P].rearrange("p (e n) -> p e n", e=2), ACT.Copy).then_inc(kc_out, 1)
                act.wait_ge(bias_c, p + 1)
                act.activation(pc[:, 0:63], c.ps[:, 5, 0:63], ACT.Exp, bias=s1[:, 1:2], scale=SCALE,
                               accum_out=s1[:, 2:3]).then_inc(exp_c, 1)
                act.wait_ge(pct_ps, p + 1)
                act.activation(pt[0:63, 0:P], c.ps[0:63, 6, 0:P], ACT.Copy).then_inc(pct_out, 1)
                for w in range(2):
                    act.wait_ge(bias_w, 2 * p + w + 1)
                    s = S[:, 1088 * w:1088 + 576 * w]
                    act.activation(s, s, ACT.Exp, bias=s1[:, 4 + 3 * w:5 + 3 * w], scale=SCALE,
                                   accum_out=s1[:, 5 + 3 * w:6 + 3 * w]).then_inc(exp_w, 1)
                act.wait_ge(pv_ps, 3 * p + 1)
                for n, tiles in enumerate(GROUPED):
                    m = len(GROUPED) * p + n
                    act.wait_ge(pt_ps, m + 1)
                    full = [t for t in tiles if KT[t][2] == P]
                    for t0, t1, r in ([(tiles[0], tiles[-1] + 1, P)] if len(full) == len(tiles) else
                                      [(t, t + 1, KT[t][2]) for t in tiles]):
                        a = t0 - tiles[0]
                        ins = act.activation(pt[0:r, t0 * P:t1 * P], c.ps[0:r, m % 2, a * P:(a + t1 - t0) * P], ACT.Copy)
                    ins.then_inc(pt_out, 1)
                act.wait_ge(ot_ps, p + 1)
                for h2 in range(2):
                    src = c.ps[HD * h2:HD * (h2 + 1), 2, 0:P].rearrange("p (b n f t) -> p b n f t", b=2, n=4, f=2)[:, :, :, h2]
                    dst = c.aT[HD * h2:HD * (h2 + 1), :, SEQ + 16 * p:SEQ + 16 * (p + 1)].rearrange("p n (b t) -> p b n t", b=2)
                    for e in range(2):
                        act.activation(dst[:, e], src[:, e], ACT.Copy).then_inc(ot_out, 1)

        @block.vector
        def _(dve):
            link = c.vsteps.on(dve)
            dve.memset(s1[:], 0.0)
            dve.memset(hid[:], 0.0)
            dve.memset(imp[:], 0.0)
            dve.memset(qb[:], 0.0).then_inc(qb_zero, 1)
            dve.wait_ge(small_out, 3)
            for p in range(NP):
                dve.wait_ge(trail_out, 2 * p + 2)
                if p:
                    dve.wait_ge(kc_ps, p)
                    dve.wait_ge(ot_out, 4 * p)

                def v3(ap):
                    return ap.rearrange("p a (b n) -> p (a b) n", b=2)
                gelu_hidden(dve, link, c.b1, v3(hid[:])[:, :, 0:63],
                            c.ps[0:HD, 5, :].rearrange("p (a n) -> p a n", n=64)[:, :, 0:63],
                            v3(trail[:])[:, :, 1:64],
                            gt[:].rearrange("p r a (b n) -> p r (a b) n", b=2)[:, :, :, 0:63],
                            lambda ins: ins.then_inc(hid_scaled, 1), lambda: dve.wait_ge(hid_tanh, p + 1))
                dve.engine_nop().then_inc(hid_ready, 1)
                g3 = c.gs[:, p].rearrange("p (h r) -> p r h", r=3)
                link(dve.tensor_tensor(gb[:], g3, c.k("headpick").unsqueeze(1).broadcast_to([P, 3, 8]), ALU.mult))
                link(dve.tensor_reduce(gsel[:], gb[:], AX, ALU.add))
                dve.wait_ge(sc_ps, p + 1)
                link(dve.tensor_reduce(s1[:, 0:1], c.ps[:, 5, 0:63], AX, ALU.max))
                dve.tensor_scalar(s1[:, 1:2], s1[:, 0:1], -SCALE, None, ALU.mult).then_inc(bias_c, 1)
                dve.wait_ge(exp_c, p + 1)
                link(dve.reciprocal(s1[:, 3:4], s1[:, 2:3]))
                dve.tensor_scalar(pc[:, 0:63], pc[:, 0:63], s1[:, 3:4], None, ALU.mult).then_inc(pc_ready, 1)
                dve.wait_ge(wide_ps, p + 1)
                W = S[:, 1088:1088 + 576]
                dve.tensor_tensor(W[:, 0:8], c.ps[:, 3, 0:8], c.k("winmask"), ALU.add)
                dve.tensor_copy(W[:, 8:SEQ], c.ps[:, 3, 8:SEQ])
                nm = c.k("newmask")[:, 64 * p:64 * (p + 1)]
                link(dve.tensor_tensor(W[:, SEQ:SEQ + 64], c.ps[:, 4, 0:64], nm, ALU.add))
                link(dve.tensor_reduce(s1[:, 6:7], W, AX, ALU.max))
                link(dve.tensor_scalar(s1[:, 7:8], s1[:, 6:7], -SCALE, None, ALU.mult))
                dve.wait_ge(imp_ps, p + 1)
                dve.tensor_copy(imp[:, 1:64], c.ps[:, 7, 256:319]).then_inc(imp_out, 1)
                dve.wait_ge(imp_out, p + 1)
                link(dve.tensor_tensor(half[:], imp[:, 1:69], imp[:, 0:68], ALU.add))
                link(dve.tensor_reduce(b17[:, 0], half[:].rearrange("p (b n) -> p b n", n=4), AX, ALU.add))
                fo = c.k("force17")
                link(dve.tensor_scalar(b17[:, 1], fo, -1.0, 1.0, ALU.mult, ALU.add))
                link(dve.tensor_tensor(b17[:, 1], b17[:, 1], b17[:, 0], ALU.mult))
                link(dve.scalar_tensor_tensor(b17[:, 1], fo, 1.0e4, b17[:, 1], ALU.mult, ALU.add))
                link(dve.tensor_reduce(s1[:, 12:13], b17[:, 1], AX, ALU.min))
                link(dve.tensor_scalar(b17[:, 2], b17[:, 1], s1[:, 12:13], None, ALU.is_equal))
                link(dve.tensor_tensor(b17[:, 2], b17[:, 2], c.k("blk17"), ALU.mult))
                link(dve.tensor_reduce(s1[:, 13:14], b17[:, 2], AX, ALU.max))
                link(dve.tensor_scalar(b17[:, 3], b17[:, 2], s1[:, 13:14], NEG, ALU.is_equal, ALU.mult))
                for a in range(2):
                    link(dve.tensor_tensor(S[:, 512 * a:512 * (a + 1)].rearrange("p (b n) -> p b n", n=64),
                                           c.ps[:, a, :].rearrange("p (b n) -> p b n", n=64),
                                           b17[:, 3, 8 * a:8 * a + 8].unsqueeze(2).broadcast_to([P, 8, 64]), ALU.add))
                link(dve.tensor_tensor(S[:, PAST:PAST + 64], c.ps[:, 2, 0:64], nm, ALU.add))
                link(dve.tensor_reduce(s1[:, 14:15], S[:, 0:1088], AX, ALU.max))
                dve.tensor_scalar(s1[:, 4:5], s1[:, 14:15], -SCALE, None, ALU.mult).then_inc(bias_w, 1)
                dve.engine_nop().then_inc(bias_w, 1)
                dve.wait_ge(exp_w, 2 * p + 2)
                link(dve.reciprocal(s1[:, 9:10], s1[:, 5:6]))
                link(dve.reciprocal(s1[:, 10:11], s1[:, 8:9]))
                link(dve.tensor_tensor(s1[:, 9:11], s1[:, 9:11], gsel[:, 1:3], ALU.mult))
                dve.wait_ge(pv_ps, 3 * p + 3)
                link(dve.tensor_scalar(o[:, 0:HD], c.ps[:, 7, 0:HD], gsel[:, 0:1], None, ALU.mult))
                link(dve.scalar_tensor_tensor(o[:, 0:HD], c.ps[:, 3, 0:HD], s1[:, 9:10], o[:, 0:HD], ALU.mult, ALU.add))
                link(dve.scalar_tensor_tensor(o[:, 0:HD], c.ps[:, 4, 0:HD], s1[:, 10:11], o[:, 0:HD], ALU.mult, ALU.add))
                dve.tensor_copy(o[:, HD:2 * HD], o[:, 0:HD]).then_inc(o_ready, 1)


def merge(nc, c):
    with ExitStack() as ctx:
        def sem(name):
            return c.sem("merge_" + name)

        local = local_tensor(nc, ctx, "merge")
        region = Region(local, 0, LOCAL)
        small = Region(c.arena, AT_Z4 + 16 * TOK, AT_SSM)
        sig = Region(c.arena, AT_Z4, AT_SSM).take([P, 16, TOK])
        w_out = Region(c.arena, AT_KT, AT_XM).take([P, KD, D])
        late = Region(local, 0, 8192)
        w_glu = region.take([P, 4, D])
        w_ssm = region.take([P, 4, D])
        c.x2 = x = Region(c.arena, AT_XM, AT_X2_END).take([P, TILES, D])
        h = late.take([P, 2, D])
        hT = late.take([P, KD, P])
        w_attn = Region(c.arena, AT_X2_END, AT_LOCAL).take([P, 4, D])
        glu = Region(local, region.pos, LOCAL).take([P, 4, TOK])
        y = region.take([NCH, CH, SW])
        route = Region(local, region.pos, LOCAL)
        tmp = region.take([P, 2, 2, 512])
        yT = region.take([P, 4, TOK])
        g_ffn = small.take([P, D])
        w_route = small.take([P, KD, 36])
        b_route = small.take([P, 36])

        ss = route.take([P, TILES])
        lg = route.take([P, TILES, 36])
        gm = route.take([P, TILES])
        goh = route.take([P, TILES, 4])
        t4 = route.take([P, TILES, 4])
        gw = route.take([P, TILES])
        el = route.take([P, TILES, 32])
        t32 = route.take([P, TILES, 32])
        top = route.take([P, 2, TILES])
        pick = route.take([P, TILES])
        M = route.take([P, 3, TILES, 32])
        nb = route.take([P, 4, 32])
        dest = route.take([P, TILES])
        be = route.take([1, BLOCKS, 32])
        bf = route.take([1, BLOCKS + 1])

        sig_in, wg_in, ws_in, wa_in, wo_in, x_in, rt_in, table_in = (
            sem("sig_in"), sem("wg_in"), sem("ws_in"), sem("wa_in"), sem("wo_in"), sem("m_x_in"), sem("rt_in"),
            sem("slots_in"))
        y_ps, sq_done, u_ready, y_tanh, y_done, yt_ps, yt_out = (
            sem("y_ps"), sem("sq_done"), sem("u_ready"), sem("y_tanh"), sem("y_done"), sem("yt_ps"), sem("yt_out"))
        glu_ps, glu_tanh, glu_done, proj_ps, proj_done, out_ps, x_done, x_zero = (
            sem("glu_ps"), sem("glu_tanh"), sem("glu_done"), sem("proj_ps"), sem("proj_done"), sem("out_ps"),
            sem("x_done"), sem("x_zero"))
        sq2, h_ready, h_stored, ht_ps, ht_out, lg_ps = (
            sem("sq2"), sem("h_ready"), sem("h_stored"), sem("ht_ps"), sem("ht_out"), sem("lg_ps"))
        ge_ready, ge_exp, te_ready, te_exp, m_ready, rank_ps = (
            sem("ge_ready"), sem("ge_exp"), sem("te_ready"), sem("te_exp"), sem("m_ready"), sem("rank_ps"))
        mean2, root2 = sem("mean2"), sem("root2")
        NY = GROUPS // 4

        block = ctx.enter_context(nc.Block())

        @block.sync
        def _(sp):
            sp.dma_start(w_glu[:], c.d["w_glu"]).then_inc(wg_in, 16)
            sp.dma_start(w_ssm[:], c.d["w_ssm"]).then_inc(ws_in, 16)
            sp.dma_start(w_attn[:], c.d["w_attn"]).then_inc(wa_in, 16)
            sp.dma_start(sig[:], c.d["sig"].rearrange("m p t -> p m t")).then_inc(sig_in, 16)
            sp.dma_start(g_ffn[:], c.d["g_ffn"]).then_inc(rt_in, 16)
            sp.dma_start(w_route[:], c.d["w_route"]).then_inc(rt_in, 16)
            sp.dma_start(b_route[:], c.d["b_route"]).then_inc(rt_in, 16)
            sp.dma_start(c.token[:], c.d["token_ids"]).then_inc(rt_in, 16)
            sp.dma_start(c.d["slot_token"].rearrange("(b p) o -> b (p o)", p=P), c.d["unused"]).then_inc(table_in, 16)
            sp.wait_ge(y_ps, NY)
            sp.dma_start(w_out[:], c.d["w_out"]).then_inc(wo_in, 16)
            sp.wait_ge(proj_ps, 32)
            sp.dma_start(x[:, 0:4], c.d["x"][0:SEQ].rearrange("(i p) d -> p i d", p=P)).then_inc(x_in, 16)
            sp.dma_start(x[0:64, 4], c.d["x"][SEQ:TOK]).then_inc(x_in, 16)
            for i in range(TILES):
                sp.wait_ge(h_ready, i + 1)
                sp.dma_start(c.d["h"][i * P:i * P + ROWS[i]], h[0:ROWS[i], i % 2]).then_inc(h_stored, 16)
                sp.wait_ge(h_stored, 16 * (i + 1))
            sp.wait_ge(table_in, 16)

        @block.tensor
        def _(pe):
            for n in range(NY):
                if n >= 4:
                    pe.wait_ge(y_done, n - 3)
                for a in range(4):
                    g = 2 * (4 * (n // 2) + a) + n % 2
                    lo, tl = HD * (g % 2), g // 2
                    o = c.ps[0:NCH, n % 4, a * P:(a + 1) * P]
                    pe.matmul(o, c.U[:, g], c.KT[:, :, g * 16:(g + 1) * 16], start=True, stop=False)
                    for r in range(2):
                        mm = pe.matmul(o, c.XM[lo:lo + HD, r, tl], c.C[lo:lo + HD, r, tl].rearrange("p t e -> p (t e)"),
                                       start=False, stop=r == 1)
                mm.then_inc(y_ps, 1)
            pe.wait_ge(y_done, NY)
            for n in range(8):
                if n >= 2:
                    pe.wait_ge(yt_out, n - 1)
                for a in range(4):
                    t = 4 * (n % 2) + a
                    mm = pe.transpose(c.ps[:, 4 + n % 2, a * NCH:(a + 1) * NCH], y[:, t, n // 2 * P:(n // 2 + 1) * P],
                                      c.k("ident")[0:NCH, 0:NCH])
                mm.then_inc(yt_ps, 1)
            pe.wait_ge(yt_out, 8)
            pe.wait_ge(wg_in, 16)
            for u in range(8):
                j, t = u // 2, slice(u % 2 * HALF, (u % 2 + 1) * HALF)
                if u >= 2:
                    pe.wait_ge(glu_done, u - 1)
                for e in range(2):
                    for k in range(4):
                        mm = pe.matmul(c.ps[:, 2 * e + u % 2, 0:HALF], w_glu[:, k, (4 * e + j) * P:(4 * e + j + 1) * P],
                                       yT[:, k, t], start=k == 0, stop=k == 3)
                    mm.then_inc(glu_ps, 1)
            pe.wait_ge(glu_done, 8)
            pe.wait_ge(ws_in, 16)
            pe.wait_ge(wa_in, 16)
            for u in range(16):
                m, t = u // 2, slice(u % 2 * HALF, (u % 2 + 1) * HALF)
                if u >= 2:
                    pe.wait_ge(proj_done, u - 1)
                for e, (w, mov) in enumerate(((w_ssm, glu), (w_attn, c.aT))):
                    for k in range(4):
                        mm = pe.matmul(c.ps[:, 4 + 2 * e + u % 2, 0:HALF], w[:, k, m * P:(m + 1) * P], mov[:, k, t],
                                       start=k == 0, stop=k == 3)
                    mm.then_inc(proj_ps, 1)
            pe.wait_ge(proj_done, 16)
            pe.wait_ge(wo_in, 16)
            for i in range(TILES + 1):
                if i < TILES:
                    for n in range(2):
                        if i >= 1:
                            pe.wait_ge(x_done, 2 * i + n - 1)
                        for k in range(KD):
                            mm = pe.matmul(c.ps[0:ROWS[i], n, :], sig[:, k, i * P:i * P + ROWS[i]],
                                           w_out[:, k, n * 512:(n + 1) * 512], start=k == 0, stop=k == KD - 1)
                        mm.then_inc(out_ps, 1)
                if i >= 1:
                    r = ROWS[i - 1]
                    pe.wait_ge(h_ready, i)
                    if i >= 2:
                        pe.wait_ge(ht_out, 2 * (i - 1))
                    for n in range(2):
                        for a in range(4):
                            mm = pe.transpose(c.ps[:, 2 + n, a * P:a * P + r], h[0:r, (i - 1) % 2, (4 * n + a) * P:(4 * n + a + 1) * P],
                                              c.k("ident")[0:r, 0:r])
                        mm.then_inc(ht_ps, 1)
                    pe.wait_ge(ht_out, 2 * i)
                    pe.wait_ge(rt_in, 64)
                    for k in range(KD):
                        mm = pe.matmul(c.ps[0:r, 4, (i - 1) * 36:i * 36], hT[:, k, 0:r], w_route[:, k], start=k == 0,
                                       stop=k == KD - 1)
                    mm.then_inc(lg_ps, 1)
            pe.wait_ge(m_ready, 1)
            for i in range(TILES + 1):
                for a in range(min(i + 1, TILES)):
                    mm = pe.matmul(c.ps[:, 5, i * 32:(i + 1) * 32], c.k("tri") if a == i else c.k("ones"), M[:, 2, a],
                                   start=a == 0, stop=a == min(i, TILES - 1))
            mm.then_inc(rank_ps, 1)

        @block.scalar
        def _(act):
            def square(n):
                act.wait_ge(y_ps, n + 1)
                if n >= 2:
                    act.wait_ge(y_tanh, n - 1)
                act.activation(tmp[0:NCH, n % 2, 0], c.ps[0:NCH, n % 4, :], ACT.Square).then_inc(sq_done, 1)

            square(0)
            for n in range(NY):
                if n + 1 < NY:
                    square(n + 1)
                act.wait_ge(u_ready, n + 1)
                if n >= 2:
                    act.wait_ge(y_done, n - 1)
                act.activation(tmp[0:NCH, n % 2, 1], tmp[0:NCH, n % 2, 0], ACT.Tanh, scale=GELU_B).then_inc(y_tanh, 1)
            for n in range(8):
                act.wait_ge(yt_ps, n + 1)
                dst = yT[:, n // 2].rearrange("p (k t) -> p t k", t=CH)[:, 4 * (n % 2):4 * (n % 2) + 4]
                act.activation(dst, c.ps[:, 4 + n % 2, 0:4 * NCH].rearrange("p (t k) -> p t k", t=4), ACT.Copy).then_inc(yt_out, 1)
            for u in range(8):
                act.wait_ge(glu_ps, 2 * u + 2)
                if u >= 2:
                    act.wait_ge(glu_done, u - 1)
                act.activation(tmp[:, u % 2, 0, 0:HALF], c.ps[:, 2 + u % 2, 0:HALF], ACT.Tanh, scale=0.5).then_inc(glu_tanh, 1)
            for i in range(TILES):
                act.wait_ge(x_done, 2 * i + 2)
                if i:
                    act.wait_ge(h_ready, i)
                if i >= 2:
                    act.wait_ge(h_stored, 16 * (i - 1))
                act.activation(h[:, i % 2], x[:, i], ACT.Square, accum_out=ss[:, i:i + 1]).then_inc(sq2, 1)
                act.wait_ge(mean2, i + 1)
                act.activation(ss[:, i:i + 1], ss[:, i:i + 1], ACT.Sqrt).then_inc(root2, 1)
                for n in range(2):
                    act.wait_ge(ht_ps, 2 * i + n + 1)
                    if i and n == 0:
                        act.wait_ge(lg_ps, i)
                    r = ROWS[i]
                    src = c.ps[:, 2 + n, :].rearrange("p (a t) -> p a t", a=4)[:, :, 0:r]
                    act.activation(hT[:, 4 * n:4 * n + 4, 0:r], src, ACT.Copy).then_inc(ht_out, 1)
            act.wait_ge(ge_ready, 1)
            act.activation(t4[:], t4[:], ACT.Exp).then_inc(ge_exp, 1)
            act.wait_ge(te_ready, 1)
            act.activation(c.wt[:, 1], c.wt[:, 1], ACT.Exp).then_inc(te_exp, 1)

        @block.vector
        def _(dve):
            link = c.vsteps.on(dve)

            def before_exp(n):
                t, ps = tmp[0:NCH, n % 2, 0], c.ps[0:NCH, n % 4, :]
                dve.wait_ge(sq_done, n + 1)
                link(dve.tensor_scalar(t, t, GELU_A, 1.0, ALU.mult, ALU.add))
                dve.tensor_tensor(t, t, ps, ALU.mult).then_inc(u_ready, 1)

            before_exp(0)
            for n in range(NY):
                if n + 1 < NY:
                    before_exp(n + 1)
                e = tmp[0:NCH, n % 2, 1]
                dve.wait_ge(y_tanh, n + 1)
                link(dve.tensor_scalar(e, e, 0.5, 0.5, ALU.mult, ALU.add))
                by4 = "k (g t e) -> k g t e"
                dve.tensor_tensor(y[:].rearrange("k t (s h e) -> k s h t e", h=2, e=16)[:, 4 * (n // 2):4 * (n // 2) + 4, n % 2],
                                  c.ps[0:NCH, n % 4, :].rearrange(by4, g=4, t=CH),
                                  e.rearrange(by4, g=4, t=CH), ALU.mult).then_inc(y_done, 1)
            for u in range(8):
                e = tmp[:, u % 2, 0, 0:HALF]
                dve.wait_ge(glu_tanh, u + 1)
                link(dve.tensor_scalar(e, e, 0.5, 0.5, ALU.mult, ALU.add))
                if u == 0:
                    dve.wait_ge(yt_ps, 8)
                dve.tensor_tensor(glu[:, u // 2, u % 2 * HALF:(u % 2 + 1) * HALF], c.ps[:, u % 2, 0:HALF], e,
                                  ALU.mult).then_inc(glu_done, 1)
            dve.wait_ge(sig_in, 16)
            for u in range(16):
                m, t = u // 2, slice(u % 2 * HALF, (u % 2 + 1) * HALF)
                dve.wait_ge(proj_ps, 2 * u + 2)
                dve.tensor_tensor(sig[:, m, t], sig[:, m, t], c.ps[:, 4 + u % 2, 0:HALF], ALU.mult)
                link(dve.tensor_tensor(sig[:, 8 + m, t], sig[:, 8 + m, t], c.ps[:, 6 + u % 2, 0:HALF], ALU.mult))
                dve.tensor_tensor(sig[:, m, t], sig[:, m, t], sig[:, 8 + m, t], ALU.add).then_inc(proj_done, 1)
            dve.wait_ge(x_in, 32)
            dve.wait_ge(rt_in, 64)
            link(dve.memset(x[64:P, 4], 0.0))
            for i in range(TILES):
                r = ROWS[i]
                for n in range(2):
                    dve.wait_ge(out_ps, 2 * i + n + 1)
                    xs = x[0:r, i, n * 512:(n + 1) * 512]
                    dve.tensor_tensor(xs, c.ps[0:r, n, :], xs, ALU.add).then_inc(x_done, 1)
                dve.wait_ge(sq2, i + 1)
                dve.tensor_scalar(ss[:, i:i + 1], ss[:, i:i + 1], 1.0 / D, EPS, ALU.mult, ALU.add).then_inc(mean2, 1)
                dve.wait_ge(root2, i + 1)
                link(dve.reciprocal(ss[:, i:i + 1], ss[:, i:i + 1]))
                dve.scalar_tensor_tensor(h[:, i % 2], x[:, i], ss[:, i:i + 1], g_ffn[:], ALU.mult,
                                         ALU.mult).then_inc(h_ready, 1)
            dve.wait_ge(lg_ps, TILES)
            link(dve.memset(lg[:], 0.0))
            ps = c.ps[:, 4, 0:TILES * 36].rearrange("p (i e) -> p i e", e=36)
            link(dve.tensor_tensor(lg[:, 0:4], ps[:, 0:4], b_route.unsqueeze(1).broadcast_to([P, 4, 36]), ALU.add))
            link(dve.tensor_tensor(lg[0:64, 4], ps[0:64, 4], b_route[0:64], ALU.add))

            def wide(col, n):
                return col.unsqueeze(2).broadcast_to([P, TILES, n])

            def first_of_max(out, vals, mx, desc, n):
                link(dve.tensor_tensor(out, vals, wide(mx, n), ALU.is_equal))
                link(dve.tensor_tensor(out, out, desc.unsqueeze(1).broadcast_to([P, TILES, n]), ALU.mult))
                link(dve.tensor_reduce(pick[:], out, AX, ALU.max))
                link(dve.tensor_tensor(out, out, wide(pick[:], n), ALU.is_equal))

            gl = lg[:, :, 0:4]
            link(dve.tensor_reduce(gm[:], gl, AX, ALU.max))
            dve.tensor_tensor(t4[:], gl, wide(gm[:], 4), ALU.subtract).then_inc(ge_ready, 1)
            first_of_max(goh[:], gl, gm[:], c.k("desc4"), 4)
            dve.wait_ge(ge_exp, 1)
            link(dve.tensor_reduce(gw[:], t4[:], AX, ALU.add))
            link(dve.reciprocal(gw[:], gw[:]))
            link(dve.tensor_scalar(t4[:], goh[:], -1.0, -NEG, ALU.add, ALU.mult))
            link(dve.tensor_tensor(el[:].rearrange("p i (g e) -> p i g e", g=4),
                                   lg[:, :, 4:36].rearrange("p i (g e) -> p i g e", g=4),
                                   t4[:].unsqueeze(3).broadcast_to([P, TILES, 4, 8]), ALU.add))
            link(dve.tensor_reduce(top[:, 0], el[:], AX, ALU.max))
            first_of_max(M[:, 0], el[:], top[:, 0], c.k("desc32"), 32)
            link(dve.scalar_tensor_tensor(t32[:], M[:, 0], -3.0e38, el[:], ALU.mult, ALU.add))
            link(dve.tensor_reduce(top[:, 1], t32[:], AX, ALU.max))
            first_of_max(M[:, 1], t32[:], top[:, 1], c.k("desc32"), 32)
            for j in range(2):
                link(dve.tensor_tensor(M[:, j], M[:, j], wide(c.k("valid"), 32), ALU.mult))
            dve.tensor_tensor(M[:, 2], M[:, 0], M[:, 1], ALU.add).then_inc(m_ready, 1)
            dve.tensor_tensor(c.wt[:, 1], top[:, 1], top[:, 0], ALU.subtract).then_inc(te_ready, 1)
            dve.wait_ge(te_exp, 1)
            link(dve.tensor_scalar(c.wt[:, 0], c.wt[:, 1], 1.0, None, ALU.add))
            link(dve.reciprocal(c.wt[:, 0], c.wt[:, 0]))
            link(dve.tensor_tensor(c.wt[:, 0], c.wt[:, 0], gw[:], ALU.mult))
            link(dve.tensor_tensor(c.wt[:, 1], c.wt[:, 1], c.wt[:, 0], ALU.mult))
            dve.wait_ge(rank_ps, 1)
            cnt = c.ps[:, 5, 5 * 32:6 * 32]
            link(dve.tensor_scalar(nb[:, 0], cnt, 0.0, None, ALU.is_gt))
            for k in range(1, 5):
                link(dve.tensor_scalar(nb[:, 3], cnt, float(P * k), None, ALU.is_gt))
                link(dve.tensor_tensor(nb[:, 0], nb[:, 0], nb[:, 3], ALU.add))
            link(dve.tensor_tensor_scan(nb[:, 1], c.k("ones")[:, 0:32], nb[:, 0], 0.0, ALU.mult, ALU.add))
            link(dve.tensor_tensor(nb[:, 2], nb[:, 1], nb[:, 0], ALU.subtract))
            link(dve.tensor_scalar(nb[:, 2], nb[:, 2], float(P), None, ALU.mult))
            link(dve.tensor_tensor(t32[:], c.ps[:, 5, 0:5 * 32].rearrange("p (i e) -> p i e", e=32),
                                   nb[:, 2].unsqueeze(1).broadcast_to([P, TILES, 32]), ALU.add))
            for j in range(2):
                link(dve.tensor_tensor(el[:], M[:, j], t32[:], ALU.mult))
                link(dve.tensor_reduce(dest[:], el[:], AX, ALU.add))
                link(dve.tensor_copy(c.dest[:, j], dest[:]))
            link(dve.tensor_tensor(be[:], nb[0:1, 1].unsqueeze(1).broadcast_to([1, BLOCKS, 32]),
                                   c.k("blkno")[0:1].unsqueeze(2).broadcast_to([1, BLOCKS, 32]), ALU.is_le))
            link(dve.tensor_reduce(bf[:, 0:BLOCKS], be[:], AX, ALU.add))
            link(dve.tensor_scalar(bf[:, 0:BLOCKS], bf[:, 0:BLOCKS], float(N_EXP - 1), None, ALU.min))
            half = BLOCKS // 2
            link(dve.tensor_scalar(be[:, 0, 0:half], c.k("blkno")[0:1, 0:half], 2.0, nb[0:1, 1, 31:32], ALU.mult, ALU.is_lt))
            link(dve.tensor_reduce(bf[:, BLOCKS:BLOCKS + 1], be[:, 0, 0:half], AX, ALU.add))
            dve.tensor_copy(c.blocks[:], bf[:])


def experts(nc, c):
    with ExitStack() as ctx:
        def sem(name):
            return c.sem("experts_" + name)

        region = Region(c.arena, AT_Z4, AT_XM)
        raw = region.take([P, PIECES, 4, 512])
        X = region.take([P, 2, D])
        e = region.take([P, DE])
        H = region.take([P, DE])
        Y = region.take([P, 2, D])
        table = region.take([P, BLOCKS + 2, 2], I32)
        token = region.take([P, 2, 1], I32)
        dest = region.take([P, 2, 1], I32)
        none = region.take([P, 1], I32)
        tick = region.take([1, 8])
        SPLIT = 3
        split = Region(local_tensor(nc, ctx, "experts", F32R), 0, LOCAL)
        W = split.take([P, SPLIT, 2, 4, 512], F32)
        XT = split.take([P, 2, KD, P], F32)
        HT = split.take([P, 2, KE, P], F32)

        piece_in = [sem(f"piece_in{i}") for i in range(PIECES)]
        w_hi, w_lo, w_used = sem("w_hi"), sem("w_lo"), sem("w_used")
        scattered, table_in, idx_copied = sem("scattered"), sem("table_in"), sem("idx_copied")
        rows_in = [sem(f"rows_in{i}") for i in range(2)]
        y_stored = [sem(f"y_stored{i}") for i in range(2)]
        x_zero, gate_tanh, h_ready, y_out, silu_steps = (
            sem("e_x_zero"), sem("gate_tanh"), sem("e_h_ready"), sem("y_out"),
            sem("silu_steps"))
        xt_ps, xt_hi, xt_lo, ht_ps, ht_hi, ht_lo = (
            sem("xt_ps"), sem("xt_hi"), sem("xt_lo"), sem("e_ht_ps"), sem("e_ht_hi"), sem("e_ht_lo"))
        XT0, Y0, TURN0, STORED0, LO0, USED0 = 1, 2, 1, 16, PIECES, SPLIT
        turn, store_turn = sem("turn"), sem("store_turn")

        def pairs(eng):
            return eng.value_load(c.blocks[0:1, BLOCKS:BLOCKS + 1], min_val=1, max_val=BLOCKS // 2)

        block = ctx.enter_context(nc.Block())

        @block.sync
        def _(sp):
            n = pairs(sp)
            with sp.Fori(0, n) as i:
                for q in range(2):
                    x = sp.value_load(c.blocks[0:1, bass.ds(i * 2 + q, 1)], min_val=0, max_val=N_EXP - 1)
                    for p in range(PIECES):
                        sp.wait_ge(w_lo, i * 12 + 6 * q + p + 1)
                        sp.dma_start(raw[:, p], c.d["w_exp"][bass.ds(x, 1), p].rearrange("o p k n -> (o p) k n")).then_inc(piece_in[p], 16)
            for p in range(2):
                sp.wait_ge(w_lo, n * 12 + p + 1)
                sp.dma_start(raw[:, p], c.d["w_exp"][0, p]).then_inc(piece_in[p], 16)

        @block.gpsimd
        def _(pool):
            def gather(q):
                pool.indirect_dma_start(X[:, q], None, c.d["h"], bass.IndirectOffsetOnAxis(ap=token[:, q].bitcast(U32), axis=0),
                                        bounds_check=TOK - 1, oob_is_err=False).then_inc(rows_in[q], 16)

            def scatter(q, at):
                pool.indirect_dma_start(c.d["rows"], bass.IndirectOffsetOnAxis(ap=at.bitcast(U32), axis=0), Y[:, q], None,
                                        bounds_check=2 * TOK - 1, oob_is_err=False).then_inc(y_stored[q], 16)

            for i in range(TILES):
                for j in range(2):
                    r = ROWS[i]
                    pool.indirect_dma_start(c.d["slot_token"], bass.IndirectOffsetOnAxis(ap=c.dest[0:r, j, i:i + 1].bitcast(U32), axis=0),
                                            c.token[0:r, i, j], None).then_inc(scattered, 16)
            n = pairs(pool)
            pool.memset(tick, 0.0)
            pool.engine_nop().then_inc(store_turn, TURN0)
            pool.memset(none[:], BIG).then_inc(x_zero, 1)
            pool.memset(Y[:], 0.0).then_inc(x_zero, 1)
            pool.memset(X[:], 0.0).then_inc(x_zero, 1)
            pool.wait_ge(scattered, 16 * 2 * TILES)
            pool.dma_start(table[:], c.d["slot_token"].rearrange("(b p) o -> p b o", p=P)).then_inc(table_in, 16)
            pool.wait_ge(table_in, 16)
            pool.tensor_copy(token[:], table[:, 0:2, 0:1]).then_inc(idx_copied, 1)
            pool.wait_ge(x_zero, 3)
            pool.wait_ge(idx_copied, 1)
            pool.engine_nop().then_inc(turn, 1)
            gather(0)
            gather(1)
            for q in range(2):
                scatter(q, none[:])
            with pool.Fori(0, n) as i:
                for q in range(2):
                    pool.wait_ge(xt_ps, i * 2 + q + 1 + XT0)
                    pool.tensor_copy(token[:, q], table[:, bass.ds(i * 2 + q + 2, 1), 0:1].rearrange("p a b -> p (a b)")).then_inc(idx_copied, 1)
                    pool.wait_ge(idx_copied, i * 4 + 2 * q + 2)
                    pool.tensor_tensor(tick[:, 1 + q:2 + q], tick[:, 0:1], tick[:, 0:1], ALU.mult).then_inc(turn, 1)
                    gather(q)
                    pool.wait_ge(y_stored[q], i * 16 + STORED0)
                    pool.tensor_copy(dest[:, q], table[:, bass.ds(i * 2 + q, 1), 1:2].rearrange("p a b -> p (a b)")).then_inc(idx_copied, 1)
                    pool.wait_ge(idx_copied, i * 4 + 2 * q + 3)
                    pool.wait_ge(y_out, i * 4 + 2 * q + 2 + Y0)
                    pool.tensor_tensor(tick[:, 3 + q:4 + q], tick[:, 0:1], tick[:, 0:1], ALU.mult).then_inc(store_turn, 1)
                    scatter(q, dest[:, q])
            pool.wait_ge(rows_in[1], n * 16 + 16)
            pool.tensor_tensor(tick[:, 7:8], tick[:, 0:1], tick[:, 0:1], ALU.mult)
            for q in range(2):
                pool.wait_ge(y_stored[q], n * 16 + STORED0)
                pool.tensor_tensor(tick[:, 5 + q:6 + q], tick[:, 0:1], tick[:, 0:1], ALU.mult)

        @block.tensor
        def _(pe):
            def transpose_rows(q):
                for k in range(KD):
                    mm = pe.transpose(c.ps[:, k // 4, k % 4 * P:(k % 4 + 1) * P], X[:, q, k * P:(k + 1) * P], c.k("ident"))
                mm.then_inc(xt_ps, 1)

            n = pairs(pe)
            pe.nop().then_inc(xt_ps, XT0)
            pe.nop().then_inc(w_used, USED0)
            pe.wait_ge(rows_in[0], 16)
            transpose_rows(0)

            with pe.Fori(0, n) as i:
                def piece(q, p, bank, tokens, k0, first, last):
                    pe.wait_ge(w_lo, i * 12 + 6 * q + p + 1 + LO0)
                    for k in range(4):
                        for n_, (a, b) in enumerate(((0, 0), (0, 1), (1, 0))):
                            mm = pe.matmul(c.ps[:, bank, :], tokens[:, a, k0 + k], W[:, p % SPLIT, b, k],
                                           start=first and k == 0 and n_ == 0, stop=last and k == 3 and n_ == 2)
                    mm.then_inc(w_used, 1)

                for q in range(2):
                    pe.wait_ge(xt_lo, i * 4 + 2 * (q + 1))
                    piece(q, 0, 2, XT, 0, True, False)
                    piece(q, 1, 2, XT, 4, False, True)
                    piece(q, 2, 3, XT, 0, True, False)
                    piece(q, 3, 3, XT, 4, False, True)
                    pe.wait_ge(turn, i * 2 + q + 1)
                    pe.wait_ge(rows_in[1 - q], i * 16 + 16 * (1 + q))
                    transpose_rows(1 - q)
                    pe.wait_ge(h_ready, i * 2 + q + 1)
                    for k in range(KE):
                        mm = pe.transpose(c.ps[:, 4, k * P:(k + 1) * P], H[:, k * P:(k + 1) * P], c.k("ident"))
                    mm.then_inc(ht_ps, 1)
                    pe.wait_ge(ht_lo, i * 2 + q + 1)
                    pe.wait_ge(y_out, i * 4 + 2 * q + Y0)
                    for h in range(2):
                        piece(q, 4 + h, 6 + h, HT, 0, True, True)

        @block.scalar
        def _(act):
            n = pairs(act)
            act.nop().then_inc(y_out, Y0)

            def rows_hi():
                for a in range(2):
                    act.activation(XT[:, 0, 4 * a:4 * a + 4], c.ps[:, a, :].rearrange("p (k t) -> p k t", k=4), ACT.Copy).then_inc(xt_hi, 1)

            def hi(p, arrived, used):
                act.wait_ge(piece_in[p], arrived)
                act.wait_ge(w_used, used)
                act.activation(W[:, p % SPLIT, 0], raw[:, p], ACT.Copy).then_inc(w_hi, 1)

            for p in range(2):
                hi(p, 16, p + 1)
            act.wait_ge(xt_ps, 1 + XT0)
            rows_hi()
            with act.Fori(0, n) as i:
                for q in range(2):
                    m = i * 12 + 6 * q + 1
                    for p in (2, 3, 4):
                        hi(p, i * 32 + 16 * q + 16, m + p)
                    act.wait_ge(w_used, m + 1 + USED0)
                    act.activation(e[:], c.ps[:, 2, :], ACT.Tanh, scale=0.5).then_inc(gate_tanh, 1)
                    hi(5, i * 32 + 16 * q + 16, m + 5)
                    act.wait_ge(xt_ps, i * 2 + q + 2 + XT0)
                    rows_hi()
                    act.wait_ge(ht_ps, i * 2 + q + 1)
                    act.activation(HT[:, 0], c.ps[:, 4, :].rearrange("p (k t) -> p k t", k=KE), ACT.Copy).then_inc(ht_hi, 1)
                    for h in range(2):
                        hi(h, i * 32 + 16 * q + 32, m + 6 + h)
                        if h == 0:
                            act.wait_ge(store_turn, i * 2 + q + TURN0)
                            act.wait_ge(y_stored[q], i * 16 + STORED0)
                        act.wait_ge(w_used, m + 4 + h + USED0)
                        act.activation(Y[:, q, h * 512:(h + 1) * 512], c.ps[:, 6 + h, :], ACT.Copy).then_inc(y_out, 1)

        @block.vector
        def _(dve):
            n = pairs(dve)
            dve.engine_nop().then_inc(w_lo, LO0)

            def rows_lo(done):
                for a in range(2):
                    dve.wait_ge(xt_hi, done + a)
                    dve.tensor_tensor(XT[:, 1, 4 * a:4 * a + 4], c.ps[:, a, :].rearrange("p (k t) -> p k t", k=4),
                                      XT[:, 0, 4 * a:4 * a + 4].bitcast(F32), ALU.subtract).then_inc(xt_lo, 1)

            def lo(p, done):
                dve.wait_ge(w_hi, done)
                dve.tensor_tensor(W[:, p % SPLIT, 1], raw[:, p], W[:, p % SPLIT, 0].bitcast(F32), ALU.subtract).then_inc(w_lo, 1)

            for p in range(2):
                lo(p, p + 1)
            rows_lo(1)
            with dve.Fori(0, n) as i:
                for q in range(2):
                    m = i * 12 + 6 * q + 1
                    for p in (2, 3, 4):
                        lo(p, m + p)
                    dve.wait_ge(gate_tanh, i * 2 + q + 1)
                    dve.scalar_tensor_tensor(H[:], e[:], 1.0, c.ps[:, 2, :], ALU.add, ALU.mult).then_inc(silu_steps, 1)
                    dve.wait_ge(silu_steps, i * 2 + q + 1)
                    dve.wait_ge(w_used, m + 3 + USED0)
                    dve.scalar_tensor_tensor(H[:], H[:], 0.5, c.ps[:, 3, :], ALU.mult, ALU.mult).then_inc(h_ready, 1)
                    rows_lo(i * 4 + 2 * q + 3)
                    dve.wait_ge(ht_hi, i * 2 + q + 1)
                    dve.tensor_tensor(HT[:, 1], c.ps[:, 4, :].rearrange("p (k t) -> p k t", k=KE),
                                      HT[:, 0].bitcast(F32), ALU.subtract).then_inc(ht_lo, 1)
                    for p in (5, 6, 7):
                        lo(p % PIECES, m + p)


def combine(nc, c):
    with ExitStack() as ctx:
        def sem(name):
            return c.sem("combine_" + name)

        region = Region(c.arena, AT_Z4, AT_XM)
        R = region.take([P, TILES, 2, D])
        g = region.take([P, D])
        y = region.take([P, TILES, D])
        ss = region.take([P, TILES])
        g_in, r_in, x_done, sq_done, y_done, stored, r_zero = (
            sem("g_final_in"), [[sem(f"r_in{i}{j}") for j in range(2)] for i in range(TILES)], sem("c_x_done"),
            sem("c_sq_done"), sem("c_y_done"), sem("c_stored"), sem("r_zero"))
        mean_ready, root_done = sem("c_mean_ready"), sem("c_root_done")

        block = ctx.enter_context(nc.Block())

        @block.sync
        def _(sp):
            sp.dma_start(g[:], c.d["g_final"]).then_inc(g_in, 16)
            for i in range(TILES):
                for j in range(2):
                    at = j * TOK + i * P
                    sp.dma_start(R[0:ROWS[i], i, j], c.d["rows"][at:at + ROWS[i]]).then_inc(r_in[i][j], 16)
            for i in range(TILES):
                sp.wait_ge(y_done, i + 1)
                sp.dma_start(c.o["y"][i * P:i * P + ROWS[i]], y[0:ROWS[i], i]).then_inc(stored, 16)
            sp.wait_ge(stored, 16 * TILES)

        @block.scalar
        def _(act):
            for i in range(TILES):
                r = ROWS[i]
                act.wait_ge(x_done, i + 1)
                act.activation(y[0:r, i], c.x2[0:r, i], ACT.Square, accum_out=ss[0:r, i:i + 1]).then_inc(sq_done, 1)
                act.wait_ge(mean_ready, i + 1)
                act.activation(ss[0:r, i:i + 1], ss[0:r, i:i + 1], ACT.Sqrt).then_inc(root_done, 1)

        @block.vector
        def _(dve):
            link = c.vsteps.on(dve)
            dve.wait_ge(g_in, 16)
            for i in range(TILES):
                r = ROWS[i]
                x, s = c.x2[0:r, i], ss[0:r, i:i + 1]
                dve.wait_ge(r_in[i][0], 16)
                link(dve.scalar_tensor_tensor(x, R[0:r, i, 0], c.wt[0:r, 0, i:i + 1], x, ALU.mult, ALU.add))
                dve.wait_ge(r_in[i][1], 16)
                dve.scalar_tensor_tensor(x, R[0:r, i, 1], c.wt[0:r, 1, i:i + 1], x, ALU.mult, ALU.add).then_inc(x_done, 1)
                dve.wait_ge(sq_done, i + 1)
                dve.tensor_scalar(s, s, 1.0 / D, EPS, ALU.mult, ALU.add).then_inc(mean_ready, 1)
                dve.wait_ge(root_done, i + 1)
                link(dve.reciprocal(s, s))
                dve.scalar_tensor_tensor(y[0:r, i], x, s, g[0:r], ALU.mult, ALU.mult).then_inc(y_done, 1)


def build(nc, d, o):
    c = Core()
    c.d, c.o = d, o
    with ExitStack() as ctx:
        c.arena = ctx.enter_context(nc.sbuf_tensor("arena", [P, AT_LOCAL], F32))
        c.ps = ctx.enter_context(nc.psum_tensor("ps", [P, 8, 512], F32))
        taken = []

        def phase_semaphore(name):
            taken.append(nc.alloc_semaphore(name))
            return taken[-1]

        c.sem = phase_semaphore
        c.vsteps = Steps(ctx.enter_context(nc.semaphore("vector_steps")))
        c.gsteps = Steps(ctx.enter_context(nc.semaphore("gpsimd_steps")))
        c.asteps = Steps(ctx.enter_context(nc.semaphore("scalar_steps")))
        c.w1_in = ctx.enter_context(nc.semaphore("cmp_weights_in"))
        low = Region(c.arena, 0, AT_Z4)
        c.K = low.take([P, CW])
        c.k = lambda name: c.K[:, COFF[name]:COFF[name] + CONST[name]]
        c.gate = low.take([P, TILES, 24])
        c.gs = low.take([P, 4, 24])
        c.w1 = low.take([P, 2, 8, P])
        c.w2 = low.take([HD, 2, HD])
        c.pe = low.take([P, 2, 16])
        c.b1 = low.take([HD, 2])
        c.A8 = low.take([P, 2, 2, ST])
        c.fin = low.take([P, 1 + NB, 2, ST])
        c.wt = low.take([P, 2, TILES])
        c.dest = low.take([P, 2, TILES], I32)
        c.token = low.take([P, TILES, 2, 2], I32)
        c.blocks = low.take([1, BLOCKS + 1], I32)
        c.pw = Region(c.arena, AT_Z4, AT_Z).take([P, 2, 9, ST])
        build_s5 = Region(c.arena, AT_XM, AT_STATE)
        c.Z = build_s5.take([P, 2, ST, CH, 16])
        c.cc = build_s5.take([P, 2, ST, 16])
        c.z4 = Region(c.arena, AT_Z4, AT_Z).take([P, ZW])
        c.z = Region(c.arena, AT_Z, AT_SSM).take([P, TILES, ZW])
        s5 = Region(c.arena, AT_SSM, AT_LOCAL)
        c.U = s5.take([P, GROUPS, NCH])
        c.KT = s5.take([P, CH, GROUPS * 16])
        c.C = s5.take([P, 2, ST, CH, 16])
        c.XM = s5.take([P, 2, ST, NCH])
        c.aT = s5.take([P, 4, TOK])
        c.X = s5.take([P, NCH + 1, 2, ST])
        c.S = s5.take([P, NCH, 2, ST])
        for phase in (project, ssm_build, prompt, sample, merge, experts, combine):
            phase(nc, c)
            if phase is not combine:
                nc.clear_and_free_semaphores(taken)
                taken.clear()
                nc.all_engine_barrier()


_OUTS = {"y": (TOK, D), "kv": (TOK, 512), "win_p": (SEQ, 256), "win_s": (NB, SEQ, 256), "ssm": (P, (1 + NB) * 2 * ST)}
_SCRATCH = {"u": ((TOK, SW), F32), "sig": ((16, P, TOK), F32), "h": ((TOK, D), F32),
            "slot_token": (((BLOCKS + 2) * P, 2), I32), "rows": ((2 * TOK, D), F32)}


def layouts(i):
    def by_state(a):
        a = a.reshape((ST, 2 * HD) + a.shape[2:])
        return np.moveaxis(a, 0, 1)

    def k_tiles(w, tiles):
        return w.reshape(tiles, P, -1).transpose(1, 0, 2)

    x = np.concatenate([i["x_prompt"][0], i["x_sample"].reshape(NB * NT, D)], 0)
    w = i["w_in"][0]
    q = w[:, SW:SW + 512].reshape(D, 2, HG, HD).transpose(0, 2, 1, 3).reshape(D, 512)
    w = np.concatenate([w[:, :SW], q, w[:, SW + 512:]], 1)
    wt = k_tiles(w, KD)
    o = {"x": x, "xT": k_tiles(x.T, KD), "g_mix": i["g_mix"][0].reshape(KD, P).T}
    o["w_tail"] = wt[:, :, 7 * PW:ZW]
    wt = np.concatenate([wt[:, :, :7 * PW], wt[:, :, ZW:]], 2)
    o["w_in"] = wt.reshape(P, KD, W_PIECES - 1, PW).transpose(2, 0, 1, 3)
    dt = np.repeat(i["ssm_log_dt"][0][:, None], HD, 1)
    o["ssm_par"] = np.stack([by_state(i["ssm_a_re"][0]), by_state(i["ssm_a_im"][0]), by_state(dt)], 1)
    o["ssm_b"] = np.stack([by_state(i["ssm_b_re"][0]), by_state(i["ssm_b_im"][0])], 1)
    o["ssm_c"] = np.stack([by_state(i["ssm_c_re"][0].transpose(0, 2, 1)), by_state(i["ssm_c_im"][0].transpose(0, 2, 1))], 1)
    o["ssm_d"] = np.broadcast_to(i["ssm_d"][0], (P, GROUPS, 16))
    o["state"] = i["state_ssm"][0].reshape(NB, ST, P, 2).transpose(2, 0, 3, 1)
    w1 = np.stack([i["cmp_w1_k"][0], i["cmp_w1_v"][0]]).reshape(2, 2, 8, P, HD)
    o["cmp_w1"] = w1.transpose(3, 0, 2, 1, 4).reshape(P, 2, 8, P)
    o["cmp_w2"] = np.stack([i["cmp_w2_k"][0], i["cmp_w2_v"][0]]).transpose(1, 0, 2)
    o["cmp_pe"] = np.stack([i["cmp_pe_k"][0], i["cmp_pe_v"][0]]).reshape(2, 16, P).transpose(2, 0, 1)
    o["cmp_b1"] = np.stack([i["cmp_b1_k"][0], i["cmp_b1_v"][0]]).T
    cache = i["cache_kv"][0]
    cmp_ = cache[:, :, 0:2].reshape(POOL, 8, 8, 2, 2, 2, HD)
    cmp_ = cmp_.transpose(0, 3, 6, 4, 5, 2, 1).reshape(POOL, P, 2, P)
    ks = cache[:, :, 2].reshape(POOL, P, P).transpose(0, 2, 1)[:, :, None]
    vs = cache[:, :, 3].reshape(POOL, P, 1, P)
    o["cache"] = np.concatenate([cmp_, ks, vs], 2)
    win = i["cache_win"][0]
    o["win_rows"] = win.reshape(NB, SEQ, 256)
    o["win_kT"] = win[:, :, 0].reshape(NB, SEQ, P).transpose(2, 0, 1)
    o["win_v"] = win[:, :, 1].reshape(NB, 4, P, P).transpose(2, 0, 1, 3)
    o["page_table"] = i["page_table"].reshape(1, -1)
    o["w_glu"] = k_tiles(i["w_glu"][0], 4)
    o["w_ssm"] = k_tiles(i["w_ssm_proj"][0], 4)
    o["w_attn"] = k_tiles(i["w_attn_proj"][0], 4)
    o["w_out"] = k_tiles(i["w_out"][0], KD)
    o["g_ffn"] = np.broadcast_to(i["g_ffn"][0], (P, D))
    o["g_final"] = np.broadcast_to(i["g_final"], (P, D))
    o["w_route"] = k_tiles(np.concatenate([i["w_router_group"][0], i["w_router_expert"][0]], 1), KD)
    o["b_route"] = np.broadcast_to(np.concatenate([i["b_router_group"][0], i["b_router_expert"][0]]), (P, 36))
    def by_k(w):
        return w.reshape(N_EXP, 2, 4, P, DE).transpose(0, 1, 3, 2, 4)

    down = i["w_exp_down"][0].reshape(N_EXP, KE, P, 2, 512).transpose(0, 3, 2, 1, 4)
    o["w_exp"] = np.concatenate([by_k(i["w_exp_gate"][0]), by_k(i["w_exp_up"][0]), down], 1)
    o["consts"] = constants()
    token = np.arange(TILES)[None, :] * P + np.arange(P)[:, None]
    o["token_ids"] = np.stack([np.stack([token, token + j * TOK], -1) for j in range(2)], 2).astype(np.int32)
    o["unused"] = np.full((BLOCKS + 2, 2 * P), BIG, np.int32)
    return {k: np.ascontiguousarray(v) for k, v in o.items()}


def kernel(**inputs):
    import concourse.bacc as _bacc
    from concourse.bass_utils import run_bass_kernel_spmd as _run

    nc = _bacc.Bacc("TRN2", target_bir_lowering=False, num_devices=1)
    arrays, d, o = {}, {}, {}
    for name, a in layouts({k: np.asarray(v) for k, v in inputs.items()}).items():
        arrays[f"in_{name}"] = a
        d[name] = nc.dram_tensor(f"in_{name}", a.shape, mybir.dt.from_np(a.dtype), kind="ExternalInput").ap()
    for name, shape in _OUTS.items():
        o[name] = nc.dram_tensor(f"out_{name}", shape, F32, kind="ExternalOutput").ap()
    for name, (shape, dt) in _SCRATCH.items():
        d[name] = nc.dram_tensor(f"scratch_{name}", shape, dt, kind="Internal").ap()
    build(nc, d, o)
    r = _run(nc, [arrays], core_ids=[0]).results[0]
    y, kv, win_p, win_s, ssm = (np.asarray(r[f"out_{n}"]) for n in _OUTS)
    ssm = ssm.reshape(P, 1 + NB, 2, ST).transpose(1, 3, 0, 2).reshape(1 + NB, GROUPS, HD, 2)
    return (y[:SEQ].reshape(1, SEQ, D), y[SEQ:].reshape(NB, NT, D),
            kv[:SEQ].reshape(1, 1, SEQ, 4, 2, HD), kv[SEQ:].reshape(1, NB, NT, 4, 2, HD),
            win_p.reshape(1, 1, SEQ, 2, 2, HD), win_s.reshape(1, NB, SEQ, 2, 2, HD),
            ssm[None, :1], ssm[None, 1:])
```

```python
from contextlib import ExitStack

import numpy as np

import concourse.bass as bass
from concourse import mybir

F32 = mybir.dt.float32
F32R = mybir.dt.float32r
I32 = mybir.dt.int32
U32 = mybir.dt.uint32
ALU = mybir.AluOpType
ACT = mybir.ActivationFunctionType
AX = mybir.AxisListType.X

P = 128
D = 1024
KD = D // P
SEQ = 512
NB, NT = 8, 8
TOK = SEQ + NB * NT
HALF = TOK // 2
TILES = 5
ROWS = [P, P, P, P, NB * NT]
PAST = 1024
PAGE = 128
PAGES = PAST // PAGE
POOL = 80
SW = 512
GROUPS = 32
ST = 16
CH = 8
PCH = SEQ // CH
NCH = PCH + NB
HD = 64
HG = 4
QKV = 512 + 768
ZW = SW + QKV + 24
ZQ, ZK, ZG = SW, SW + 512, SW + QKV
PW = 260
TOK_PIECES = 7
WIDTHS = [PW] * 6 + [256] * 9
W_PIECES = len(WIDTHS)
GATES_AFTER = [[], [], [0], [1, 2], list(range(3, 16))]
N_EXP = 32
DE = 512
KE = DE // P
PIECES = 6
SLOTS = 64
BLOCKS = 2 * TOK // SLOTS + N_EXP
TABLE = BLOCKS + 2
BIG = 1 << 20
NEG = -1.0e30
EPS = 1e-6
SCALE = HD ** -0.5
TWO_PI = 2 * np.pi
GELU_A = 0.044715
GELU_B = float(np.sqrt(2 / np.pi))

CONST = {
    "ident": P, "ones": P, "tri": P, "causal": P, "same": P, "cos": TILES * 32, "sin": TILES * 32,
    "cmask": 4 * 32, "newmask": 4 * 64, "winmask": 8, "expand": 4 * P, "headpick": 8, "eye7": 16,
    "blk17": 17, "force17": 17, "desc4": 4, "desc32": 32, "valid": TILES, "blkno": BLOCKS,
    "blkslot": TABLE + 1, "slot": SLOTS, "ids": 4 * TILES,
}
COFF, _o = {}, 0
for _n, _w in CONST.items():
    COFF[_n] = _o
    _o += _w
CW = _o


def constants():
    r = np.arange(P)
    c = {n: np.zeros((P, w), np.float32) for n, w in CONST.items()}
    c["ident"][:] = np.eye(P)
    c["ones"][:] = 1
    c["tri"][:] = r[:, None] < r[None, :]
    c["causal"][:] = np.where(r[None, :] <= r[:, None], 0, NEG)
    b2, g, hg, t = r // 64, r // 32 % 2, r // 8 % 4, r % 8
    c["same"][:] = (b2[:, None] == b2) & (g[:, None] == g) & (t[:, None] == t)
    pos = np.concatenate([np.arange(SEQ), PAST + np.arange(64) % 8, np.zeros(64)]).reshape(TILES, P)
    inv = np.float32(10000.0) ** (-np.arange(32, dtype=np.float32) / np.float32(32))
    ang = (pos.astype(np.float32)[:, :, None] * inv.astype(np.float32)).astype(np.float32)
    c["cos"][:] = np.cos(ang.astype(np.float64)).transpose(1, 0, 2).reshape(P, -1)
    c["sin"][:] = np.sin(ang.astype(np.float64)).transpose(1, 0, 2).reshape(P, -1)
    q = np.arange(4)[None, :, None] * P + r[:, None, None]
    j = np.arange(32)
    c["cmask"][:] = np.where((j * 16 + 31 <= q) & (j < 31), 0, NEG).reshape(P, -1)
    s = np.arange(64)
    bp = np.arange(4)[None, :, None]
    ok = (s // 8 == 2 * bp + b2[:, None, None]) & (s % 8 <= t[:, None, None])
    c["newmask"][:] = np.where(ok, 0, NEG).reshape(P, -1)
    c["winmask"][:] = np.where(np.arange(8)[None, :] > t[:, None], 0, NEG)
    e = (np.arange(64)[:, None, None] // 8 == 2 * bp + b2[None, None, :]) & (np.arange(64)[:, None, None] % 8 == t)
    c["expand"][:64] = e.reshape(64, -1)
    c["headpick"][:] = (g * 4 + hg)[:, None] == np.arange(8)
    c["eye7"][:] = r[:, None] == 112 + np.arange(16)
    c["blk17"][:] = 1 + np.arange(17)
    c["force17"][:] = np.isin(np.arange(17), [0, 15, 16])
    c["desc4"][:] = 4 - np.arange(4)
    c["desc32"][:] = 32 - np.arange(32)
    c["valid"][:] = np.arange(TILES) * P + r[:, None] < TOK
    c["blkno"][:] = np.arange(BLOCKS)
    c["blkslot"][:] = SLOTS * np.arange(TABLE + 1)
    c["slot"][:] = np.arange(SLOTS) - SLOTS
    token = np.arange(TILES)[None, None, :, None] * P + r[:, None, None, None]
    row = np.array([0, 1])[None, :, None, None] * TOK + token
    c["ids"][:] = (np.concatenate([np.broadcast_to(token, row.shape), row], 3) - BIG).reshape(P, -1)
    return np.concatenate([c[n] for n in CONST], 1)


class Steps:

    def __init__(self, sem):
        self.sem, self.n = sem, 0

    def on(self, eng):
        def link(ins):
            self.n += 1
            ins.then_inc(self.sem, 1)
            eng.wait_ge(self.sem, self.n)
        return link


class Core:
    pass


class Region:

    def __init__(self, arena, start, end):
        self.arena, self.pos, self.end = arena, start, end

    def take(self, shape, dt=F32):
        n = int(np.prod(shape[1:]))
        ap = self.arena[0:shape[0], self.pos:self.pos + n]
        self.pos += n
        assert self.pos <= self.end, (self.pos, self.end)
        if dt is not F32:
            ap = ap.bitcast(dt)
        names = "abcdef"[:len(shape) - 1]
        if len(names) > 1:
            ap = ap.rearrange(f"p ({' '.join(names)}) -> p {' '.join(names)}", **dict(zip(names, shape[1:])))
        return ap


AT_Z4 = 4992
AT_Z = AT_Z4 + ZW
AT_SSM = AT_Z + TILES * ZW
AT_KT = AT_SSM + GROUPS * NCH
AT_XM = AT_KT + 2 * 4096
AT_AT = AT_XM + 2 * ST * NCH
AT_STATE = AT_AT + 4 * TOK
AT_LOCAL = AT_STATE + (NCH + 1) * 2 * ST + NCH * 2 * ST
AT_END = 53168
AT_X2_END = AT_XM + TILES * D
LOCAL = AT_END - AT_LOCAL


def local_tensor(nc, ctx, name, dt=F32):
    return ctx.enter_context(nc.sbuf_tensor("local_" + name, [P, LOCAL], dt))


def project(nc, c):
    with ExitStack() as ctx:
        region = Region(c.arena, AT_SSM, AT_XM)
        high = Region(c.arena, AT_STATE, AT_LOCAL)
        def sem(name):
            return c.sem("project_" + name)

        over_x = Region(c.arena, AT_SSM, AT_XM)
        x = region.take([P, TILES, D])
        sg = over_x.take([P, 4, TOK])
        rt = over_x.take([P, 4, 512])
        raw = region.take([P, 2, KD, PW])
        junk = Region(c.arena, region.pos, AT_XM).take([P, D])
        diag = region.take([P, TOK])
        rinv_row = region.take([P, TOK])
        ss = region.take([P, TILES])
        rinv = region.take([P, TILES])
        gcol = high.take([P, KD])
        over_xT = Region(c.arena, high.pos, AT_LOCAL)
        xT = high.take([P, KD, TOK])
        bb = over_xT.take([P, 2, ST, 16])
        t4 = over_xT.take([P, 2, 1024])
        split = Region(local_tensor(nc, ctx, "project", F32R), 0, LOCAL)
        XG = split.take([P, 2, KD, TOK], F32)
        W = split.take([P, 2, 2, KD, PW], F32)

        s5_scratch = Region(c.arena, AT_Z4 + 2 * 9 * ST, AT_Z)
        par = s5_scratch.take([P, 3, ST])
        b = s5_scratch.take([P, 2, ST, 16])
        v = s5_scratch.take([P, 14, ST])
        vi = s5_scratch.take([P, ST], I32)
        tw = s5_scratch.take([P, 4, 4, ST])
        pw, cc, Z = c.pw, c.cc, c.Z

        consts_in, x_in, g_in = sem("consts_in"), sem("x_in"), sem("g_in")
        xT_in = [sem(f"xT_in{i}") for i in range(2)]
        raw_in = [sem(f"raw_in{i}") for i in range(2)]
        xg_hi, xg_lo, w_hi, w_lo = sem("xg_hi"), sem("xg_lo"), sem("w_hi"), sem("w_lo")
        square_done, diag_ready, row_ps = sem("square_done"), sem("diag_ready"), sem("row_ps")
        rinv_ready, tail_zero = sem("rinv_ready"), sem("tail_zero")
        tok_ps, tok_out, chan_ps, chan_scaled, chan_tanh = (
            sem("tok_ps"), sem("tok_out"), sem("chan_ps"), sem("chan_scaled"), sem("chan_tanh"))
        gates_ready, roped, stored = sem("gates_tanh"), sem("roped"), sem("stored")
        gate_ready, mean_ready, root_done = sem("gate_ready"), sem("mean_ready"), sem("root_done")
        gate_stored = [sem(f"gate_stored{i}") for i in range(4)]
        par_in, dt_exp, mag_exp, sin_ready, sin_done = (
            sem("par_in"), sem("dt_exp"), sem("mag_exp"), sem("sin_ready"), sem("sin_done"))
        NTU = TOK_PIECES * TILES

        def wait_used(eng, n):
            if n < TOK_PIECES:
                eng.wait_ge(tok_ps, TILES * (n + 1))
            else:
                eng.wait_ge(chan_ps, 4 * (n - TOK_PIECES + 1))

        block = ctx.enter_context(nc.Block())

        @block.sync
        def _(sp):
            def load(n):
                src = c.d["w_wide"][n] if n < 6 else c.d["w_rest"][n - 6]
                sp.dma_start(raw[:, n % 2, :, 0:WIDTHS[n]], src).then_inc(raw_in[n % 2], 16)

            sp.dma_start(gcol[:], c.d["g_mix"]).then_inc(g_in, 16)
            load(0)
            for a in range(2):
                sp.dma_start(xT[:, 4 * a:4 * a + 4], c.d["xT"][:, 4 * a:4 * a + 4]).then_inc(xT_in[a], 16)
            sp.dma_start(x[:, 0:4, :], c.d["x"][0:SEQ].rearrange("(i p) d -> p i d", p=P)).then_inc(x_in, 16)
            sp.dma_start(x[0:64, 4, :], c.d["x"][SEQ:TOK]).then_inc(x_in, 16)
            load(1)
            sp.dma_start(c.K[:], c.d["consts"]).then_inc(consts_in, 16)
            sp.dma_start(c.pages[:], c.d["page_table"]).then_inc(consts_in, 16)
            sp.dma_start(par[:], c.d["ssm_par"]).then_inc(par_in, 16)
            sp.dma_start(b[:], c.d["ssm_b"]).then_inc(par_in, 16)
            sp.dma_start(cc[:], c.d["ssm_c"]).then_inc(par_in, 16)
            for dst, name in ((c.w1, "cmp_w1"), (c.w2, "cmp_w2"), (c.pe, "cmp_pe"), (c.b1, "cmp_b1")):
                sp.dma_start(dst[:], c.d[name]).then_inc(c.w1_in, 16)
            for n in range(2, W_PIECES):
                sp.wait_ge(w_lo, n - 1)
                load(n)
                if n == 4:
                    sp.wait_ge(tok_out, 2 * TILES)
                    sp.dma_start(c.d["u"][0:SEQ].rearrange("(i p) d -> p i d", p=P), c.z[:, 0:4, 0:SW]).then_inc(stored, 16)
                    sp.dma_start(c.d["u"][SEQ:TOK], c.z[0:64, 4, 0:SW]).then_inc(stored, 16)
            sp.wait_ge(roped, TILES)
            kv = c.z[:, :, ZK:ZK + 512]
            win = c.z[:, :, ZK + 512:ZK + 768]
            sp.dma_start(c.o["kv"][0:SEQ].rearrange("(i p) d -> p i d", p=P), kv[:, 0:4]).then_inc(stored, 16)
            sp.dma_start(c.o["kv"][SEQ:TOK], kv[0:64, 4]).then_inc(stored, 16)
            sp.dma_start(c.o["win_p"].rearrange("(i p) d -> p i d", p=P), win[:, 0:4]).then_inc(stored, 16)
            for b_ in range(NB):
                sp.dma_start(c.o["win_s"][b_, SEQ - NT:SEQ], win[b_ * NT:(b_ + 1) * NT, 4]).then_inc(stored, 16)
            sp.wait_ge(stored, 16 * (5 + NB))

        @block.scalar
        def _(act):
            def hi(n):
                act.wait_ge(raw_in[n % 2], 16 * (n // 2 + 1))
                if n >= 2:
                    wait_used(act, n - 2)
                width = WIDTHS[n]
                act.activation(W[:, n % 2, 0, :, 0:width], raw[:, n % 2, :, 0:width], ACT.Copy).then_inc(w_hi, 1)

            hi(0)
            act.wait_ge(g_in, 16)
            for k in range(KD):
                act.wait_ge(xT_in[k // 4], 16)
                act.activation(XG[:, 0, k], xT[:, k], ACT.Copy, scale=gcol[:, k:k + 1]).then_inc(xg_hi, 1)
            act.wait_ge(x_in, 32)
            act.wait_ge(tail_zero, 1)
            for i in range(TILES):
                if i:
                    act.wait_ge(square_done, i)
                act.activation(junk[:], x[:, i, :], ACT.Square, accum_out=ss[:, i:i + 1]).then_inc(square_done, 1)
            act.wait_ge(mean_ready, 1)
            act.activation(ss[:], ss[:], ACT.Sqrt).then_inc(root_done, 1)
            hi(1)
            act.wait_ge(rinv_ready, 1)
            for n in range(NTU):
                j, i = n // TILES, n % TILES
                r, width = ROWS[i], WIDTHS[j]
                act.wait_ge(tok_ps, n + 1)
                act.activation(c.z[0:r, i, j * PW:j * PW + width], c.ps[0:r, n % 4, 0:width], ACT.Copy,
                               scale=rinv[0:r, i:i + 1]).then_inc(tok_out, 1)
                if i == TILES - 1:
                    hi(j + 2)
                    if j == 0:
                        act.wait_ge(par_in, 48)
                        act.activation(v[:, 0], par[:, 2], ACT.Exp).then_inc(dt_exp, 1)
                        act.wait_ge(mag_exp, 1)
                        act.activation(v[:, 2], v[:, 1], ACT.Exp).then_inc(dt_exp, 1)
                    if j == 1:
                        act.wait_ge(sin_ready, 1)
                        act.activation(v[:, 7:9], v[:, 5:7], ACT.Sin).then_inc(sin_done, 1)
            act.wait_ge(tok_out, NTU)
            act.activation(c.gate[:], c.z[:, :, ZG:ZW], ACT.Tanh, scale=0.5).then_inc(gates_ready, 1)
            for m in range(16):
                act.wait_ge(chan_scaled, 2 * m + 2)
                act.activation(sg[:, m % 4], sg[:, m % 4], ACT.Tanh, scale=0.5).then_inc(chan_tanh, 1)
                if m % 2 == 1 and TOK_PIECES + m // 2 + 2 < W_PIECES:
                    hi(TOK_PIECES + m // 2 + 2)

        @block.tensor
        def _(pe):
            def product(out, stationary, moving):
                for k in range(KD):
                    for a, (s, m) in enumerate(((0, 0), (0, 1), (1, 0))):
                        mm = pe.matmul(out, stationary(s, k), moving(m, k), start=k == 0 and a == 0, stop=k == KD - 1 and a == 2)
                return mm

            pe.wait_ge(xg_lo, KD)
            for n in range(NTU):
                j, i = n // TILES, n % TILES
                r, width = ROWS[i], WIDTHS[j]
                if i == 0:
                    pe.wait_ge(w_lo, j + 1)
                if n >= 4:
                    pe.wait_ge(tok_out, n - 3)
                product(c.ps[0:r, n % 4, 0:width], lambda s, k: XG[:, s, k, i * P:i * P + r],
                        lambda m, k: W[:, j % 2, m, k, 0:width]).then_inc(tok_ps, 1)
            pe.wait_ge(diag_ready, 1)
            pe.wait_ge(consts_in, 32)
            for i in range(TILES):
                r = ROWS[i]
                mm = pe.matmul(c.ps[:, 4 + i // 4, i % 4 * P:i % 4 * P + r], c.k("ones")[0:r], diag[0:r, i * P:i * P + r],
                               start=True, stop=True)
            mm.then_inc(row_ps, 1)
            for m in range(16):
                n = TOK_PIECES + m // 2
                if m % 2 == 0:
                    pe.wait_ge(w_lo, n + 1)
                for h in range(2):
                    u = 2 * m + h
                    if u >= 4:
                        pe.wait_ge(chan_scaled, u - 3)
                    else:
                        pe.wait_ge(tok_out, NTU)
                    product(c.ps[:, u % 4, 0:HALF], lambda s, k: W[:, n % 2, s, k, m % 2 * P:(m % 2 + 1) * P],
                            lambda q, k: XG[:, q, k, h * HALF:(h + 1) * HALF]).then_inc(chan_ps, 1)

        @block.vector
        def _(dve):
            link = c.vsteps.on(dve)

            def lo(n):
                dve.wait_ge(w_hi, n + 1)
                width = WIDTHS[n]
                dve.tensor_tensor(W[:, n % 2, 1, :, 0:width], raw[:, n % 2, :, 0:width],
                                  W[:, n % 2, 0, :, 0:width].bitcast(F32), ALU.subtract).then_inc(w_lo, 1)

            def finish_gate(m):
                dve.wait_ge(chan_tanh, m + 1)
                dve.tensor_scalar(sg[:, m % 4], sg[:, m % 4], 0.5, 0.5, ALU.mult, ALU.add).then_inc(gate_ready, 1)

            def mul(o, a, b_):
                return dve.tensor_tensor(o, a, b_, ALU.mult)

            def complex_mul(o_re, o_im, a, b_, tmp):
                mul(tmp[0], a[0], b_[0])
                mul(tmp[1], a[1], b_[1])
                mul(tmp[2], a[0], b_[1])
                link(mul(tmp[3], a[1], b_[0]))
                dve.tensor_tensor(o_re, tmp[0], tmp[1], ALU.subtract)
                link(dve.tensor_tensor(o_im, tmp[2], tmp[3], ALU.add))

            a_re, a_im = par[:, 0], par[:, 1]

            def s5_angles():
                dve.wait_ge(par_in, 48)
                link(dve.tensor_scalar(cc[:, 1], cc[:, 1], -1.0, None, ALU.mult))
                dve.wait_ge(dt_exp, 1)
                mul(v[:, 1], a_re, v[:, 0]).then_inc(mag_exp, 1)
                link(mul(v[:, 3], a_im, v[:, 0]))
                link(dve.tensor_scalar(v[:, 4], v[:, 3], 1.0 / TWO_PI, None, ALU.mult))
                link(dve.tensor_copy(vi[:], v[:, 4]))
                link(dve.tensor_copy(v[:, 4], vi[:]))
                hi = 6.28125
                link(dve.scalar_tensor_tensor(v[:, 3], v[:, 4], -hi, v[:, 3], ALU.mult, ALU.add))
                link(dve.scalar_tensor_tensor(v[:, 3], v[:, 4], -(TWO_PI - hi), v[:, 3], ALU.mult, ALU.add))
                link(dve.tensor_scalar(v[:, 4], v[:, 3], float(np.pi), -TWO_PI, ALU.is_gt, ALU.mult))
                link(dve.tensor_tensor(v[:, 3], v[:, 3], v[:, 4], ALU.add))
                link(dve.tensor_scalar(v[:, 4], v[:, 3], float(-np.pi), TWO_PI, ALU.is_lt, ALU.mult))
                link(dve.tensor_tensor(v[:, 3], v[:, 3], v[:, 4], ALU.add))
                link(dve.tensor_scalar(v[:, 5], v[:, 3], 0.5, None, ALU.mult))
                link(dve.tensor_scalar(v[:, 4], v[:, 5], -1.0, None, ALU.mult))
                link(dve.tensor_tensor(v[:, 4], v[:, 4], v[:, 5], ALU.max))
                dve.tensor_scalar(v[:, 6], v[:, 4], -1.0, float(np.pi / 2), ALU.mult, ALU.add).then_inc(sin_ready, 1)

            def s5_powers():
                dve.wait_ge(sin_done, 1)
                dve.wait_ge(dt_exp, 2)
                link(mul(v[:, 9], v[:, 7], v[:, 8]))
                link(mul(v[:, 10], v[:, 7], v[:, 7]))
                link(dve.tensor_scalar(v[:, 9], v[:, 9], 2.0, None, ALU.mult))
                link(dve.tensor_scalar(v[:, 10], v[:, 10], -2.0, 1.0, ALU.mult, ALU.add))
                mul(pw[:, 0, 1], v[:, 2], v[:, 10])
                link(mul(pw[:, 1, 1], v[:, 2], v[:, 9]))
                dve.memset(pw[:, 0, 0], 1.0)
                dve.memset(pw[:, 1, 0], 0.0)
                for n in (1, 2, 4):
                    a = [pw[:, r, 1:1 + n] for r in range(2)]
                    m = [pw[:, r, n:n + 1].broadcast_to([P, n, ST]) for r in range(2)]
                    complex_mul(pw[:, 0, n + 1:2 * n + 1], pw[:, 1, n + 1:2 * n + 1], a, m,
                                [tw[:, q, 0:n] for q in range(4)])

            tb, tt = ([t4[:, a, q * 256:(q + 1) * 256].rearrange("p (s e) -> p s e", s=ST) for q in range(4)]
                      for a in range(2))

            def s5_inputs():
                link(mul(v[:, 4], a_re, a_re))
                link(mul(v[:, 5], a_im, a_im))
                link(dve.tensor_tensor(v[:, 4], v[:, 4], v[:, 5], ALU.add))
                link(dve.reciprocal(v[:, 4], v[:, 4]))
                link(dve.tensor_scalar(v[:, 5], pw[:, 0, 1], -1.0, None, ALU.add))
                mul(v[:, 6], v[:, 5], a_re)
                mul(v[:, 7], pw[:, 1, 1], a_im)
                mul(v[:, 8], pw[:, 1, 1], a_re)
                link(mul(v[:, 9], v[:, 5], a_im))
                dve.tensor_tensor(v[:, 10], v[:, 6], v[:, 7], ALU.add)
                link(dve.tensor_tensor(v[:, 11], v[:, 8], v[:, 9], ALU.subtract))
                mul(v[:, 12], v[:, 10], v[:, 4])
                link(mul(v[:, 13], v[:, 11], v[:, 4]))
                f = [v[:, 12 + r].unsqueeze(2).broadcast_to([P, ST, 16]) for r in range(2)]
                complex_mul(bb[:, 0], bb[:, 1], f, [b[:, 0], b[:, 1]], tb)

            def s5_slots(first):
                for s in (first, first + 1):
                    complex_mul(Z[:, 0, :, s], Z[:, 1, :, s], [by_channel(pw, r, CH - 1 - s) for r in range(2)],
                                [bb[:, 0], bb[:, 1]], tt if s % 2 else tb)

            dve.memset(x[64:P, 4, :], 0.0).then_inc(tail_zero, 1)
            dve.memset(c.z[64:P, 4, :], 0.0)
            lo(0)
            dve.wait_ge(g_in, 16)
            for k in range(KD):
                dve.wait_ge(xg_hi, k + 1)
                dve.scalar_tensor_tensor(XG[:, 1, k], xT[:, k], gcol[:, k:k + 1], XG[:, 0, k].bitcast(F32), ALU.mult,
                                         ALU.subtract).then_inc(xg_lo, 1)
            dve.wait_ge(square_done, TILES)
            dve.tensor_scalar(ss[:], ss[:], 1.0 / D, EPS, ALU.mult, ALU.add).then_inc(mean_ready, 1)
            dve.wait_ge(root_done, 1)
            dve.reciprocal(rinv[:], ss[:]).then_inc(rinv_ready, 1)
            lo(1)
            dve.wait_ge(rinv_ready, 1)
            dve.wait_ge(consts_in, 32)
            for i in range(TILES):
                ins = dve.tensor_scalar(diag[:, i * P:i * P + ROWS[i]], c.k("ident")[:, 0:ROWS[i]], rinv[:, i:i + 1], None, ALU.mult)
            ins.then_inc(diag_ready, 1)
            lo(2)
            s5_angles()
            lo(3)
            s5_powers()
            lo(4)
            s5_inputs()
            for n in range(4):
                lo(5 + n)
                dve.wait_ge(xg_lo, KD)
                s5_slots(2 * n)
            dve.wait_ge(row_ps, 1)
            link(dve.tensor_copy(rinv_row[:, 0:512], c.ps[:, 4, :]))
            link(dve.tensor_copy(rinv_row[:, 512:TOK], c.ps[:, 5, 0:64]))
            dve.wait_ge(gates_ready, 1)
            link(dve.tensor_scalar(c.gate[:], c.gate[:], 0.5, 0.5, ALU.mult, ALU.add))
            for m in range(16):
                for h in range(2):
                    u = 2 * m + h
                    dve.wait_ge(chan_ps, u + 1)
                    if m >= 4:
                        dve.wait_ge(gate_stored[m % 4], 16 * (m // 4))
                    dve.tensor_tensor(sg[:, m % 4, h * HALF:(h + 1) * HALF], c.ps[:, u % 4, 0:HALF],
                                      rinv_row[:, h * HALF:(h + 1) * HALF], ALU.mult).then_inc(chan_scaled, 1)
                if m >= 1:
                    finish_gate(m - 1)
                if m % 2 == 1 and TOK_PIECES + m // 2 + 2 < W_PIECES:
                    lo(TOK_PIECES + m // 2 + 2)
            finish_gate(15)

        @block.gpsimd
        def _(pool):
            link = c.gsteps.on(pool)
            pool.wait_ge(consts_in, 32)
            for i in range(TILES):
                pool.wait_ge(tok_out, NTU - TILES + i + 1)
                co = c.k("cos")[:, i * 32:(i + 1) * 32]
                si = c.k("sin")[:, i * 32:(i + 1) * 32]
                q = c.z[:, i, ZQ:ZQ + 512].rearrange("p (h f d) -> p h f d", f=2, d=32)
                kk = c.z[:, i, ZK:ZK + 768].rearrange("p (s v g f d) -> p s v g f d", s=3, v=2, g=2, f=2)
                parts = [(q[:, :, 0], q[:, :, 1], 8)]
                parts += [(kk[:, s, 0, :, 0], kk[:, s, 0, :, 1], 2) for s in range(3)]
                for lo, hi, n in parts:
                    cb = co.unsqueeze(1).broadcast_to([P, n, 32])
                    sb_ = si.unsqueeze(1).broadcast_to([P, n, 32])
                    t = [rt[:, a, 0:n * 32].rearrange("p (h d) -> p h d", d=32) for a in range(4)]
                    pool.tensor_tensor(t[0], lo, cb, ALU.mult)
                    pool.tensor_tensor(t[1], hi, sb_, ALU.mult)
                    pool.tensor_tensor(t[2], hi, cb, ALU.mult)
                    link(pool.tensor_tensor(t[3], lo, sb_, ALU.mult))
                    pool.tensor_tensor(lo, t[0], t[1], ALU.subtract)
                    link(pool.tensor_tensor(hi, t[2], t[3], ALU.add))
                pool.engine_nop().then_inc(roped, 1)
                for m in GATES_AFTER[i]:
                    pool.wait_ge(gate_ready, m + 1)
                    pool.dma_start(c.d["sig"][m], sg[:, m % 4]).then_inc(gate_stored[m % 4], 16)
            for i in range(4):
                pool.wait_ge(gate_stored[i], 64)


def by_channel(pw, r, k):
    return pw[:, r, k].unsqueeze(2).broadcast_to([P, ST, 16])


def ssm_build(nc, c):
    with ExitStack() as ctx:
        local = local_tensor(nc, ctx, "ssm_build")
        region = Region(local, 0, LOCAL)
        def sem(name):
            return c.sem("ssm_build_" + name)

        dd = region.take([P, GROUPS, 16])
        t4 = region.take([P, 2, 1024])
        pw, cc, Z = c.pw, c.cc, c.Z
        u_rows = region.take([NCH, CH, GROUPS, 16])
        ch = region.take([NCH, GROUPS, CH * 16])
        wt = region.take([P, 2, ST, P])
        mt = region.take([P, GROUPS * 16])
        c2 = region.take([P, 2, ST, 2, 16])

        d_in, u_in, u_grouped, c2_zero, c2_ready = (
            sem("d_in"), sem("u_in"), sem("u_grouped"), sem("c2_zero"), sem("c2_ready"))
        tr_ps, tr_out, mt_ps, mt_ready, kt_zero, kt_in, st_ps, st_out, h0_in = (
            sem("tr_ps"), sem("tr_out"), sem("mt_ps"), sem("mt_ready"), sem("kt_zero"), sem("kt_in"),
            sem("st_ps"), sem("st_out"), sem("h0_in"))
        UB = 4
        NU = GROUPS // UB
        NZ = 2 * ST // 4

        block = ctx.enter_context(nc.Block())

        @block.sync
        def _(sp):
            sp.dma_start(u_rows.rearrange("k s g e -> k (s g e)"), c.d["u"].rearrange("(k s) d -> k (s d)", s=CH)).then_inc(u_in, 16)
            sp.dma_start(dd[:], c.d["ssm_d"]).then_inc(d_in, 16)
            sp.dma_start(c.X[:, PCH + 1:PCH + 1 + NB], c.d["state"]).then_inc(h0_in, 16)
            sp.wait_ge(mt_ready, 1)
            sp.wait_ge(kt_zero, 1)
            for t in range(CH):
                sp.dma_start(c.KT[0:16 * (t + 1), t, :], mt[16 * (CH - 1 - t):P, :]).then_inc(kt_in, 16)
            sp.wait_ge(kt_in, 16 * CH)
            sp.wait_ge(h0_in, 16)

        @block.scalar
        def _(act):
            act.wait_ge(c2_zero, 1)
            for h in range(2):
                rows = slice(HD * h, HD * (h + 1))
                act.activation(c2[rows, :, :, h], cc[rows], ACT.Copy).then_inc(c2_ready, 1)
            for n in range(NZ + NU):
                act.wait_ge(tr_ps, n + 1)
                if n < NZ:
                    dst = wt[:].rearrange("p r s q -> p (r s q)")[:, 512 * n:512 * (n + 1)]
                    act.activation(dst, c.ps[:, n % 2, :], ACT.Copy).then_inc(tr_out, 1)
                else:
                    m = n - NZ
                    act.activation(c.U[:, UB * m:UB * (m + 1)],
                                   c.ps[:, n % 2, 0:UB * NCH].rearrange("p (g k) -> p g k", g=UB),
                                   ACT.Copy).then_inc(tr_out, 1)
            for tl in range(ST):
                act.wait_ge(st_ps, tl + 1)
                src = c.ps[:, 4 + tl % 2, 0:2 * NCH].rearrange("p (r k) -> p k r", r=2)
                act.activation(c.S[:, :, :, tl], src, ACT.Copy).then_inc(st_out, 1)

        @block.tensor
        def _(pe):
            zf = Z[:].rearrange("p r s k e -> p (r s) (k e)")
            for n in range(NZ):
                if n >= 2:
                    pe.wait_ge(tr_out, n - 1)
                for a in range(4):
                    mm = pe.transpose(c.ps[:, n % 2, a * P:(a + 1) * P], zf[:, 4 * n + a], c.k("ident"))
                mm.then_inc(tr_ps, 1)
            pe.wait_ge(c2_ready, 2)
            for tl in range(ST):
                for r in range(2):
                    mm = pe.matmul(c.ps[:, 2, tl * 32:(tl + 1) * 32], zf[:, r * ST + tl],
                                   c2[:, r, tl].rearrange("p h e -> p (h e)"), start=r == 0, stop=r == 1)
            mm.then_inc(mt_ps, 1)
            pe.wait_ge(u_grouped, 2)
            for n in range(NU):
                pe.wait_ge(tr_out, NZ + n - 1)
                for a in range(UB):
                    g = UB * n + a
                    mm = pe.transpose(c.ps[:, (NZ + n) % 2, a * NCH:(a + 1) * NCH], ch[:, g], c.k("ident")[0:NCH, 0:NCH])
                mm.then_inc(tr_ps, 1)
            pe.wait_ge(tr_out, NU + NZ)
            for tl in range(ST):
                if tl >= 2:
                    pe.wait_ge(st_out, tl - 1)
                for r in range(2):
                    for h in range(2):
                        mm = pe.matmul(c.ps[HD * h:HD * (h + 1), 4 + tl % 2, r * NCH:(r + 1) * NCH],
                                       wt[:, r, tl, HD * h:HD * (h + 1)], c.U[:, 2 * tl + h],
                                       start=True, stop=True)
                mm.then_inc(st_ps, 1)

        @block.gpsimd
        def _(pool):
            pool.memset(c2[:], 0.0).then_inc(c2_zero, 1)
            pool.memset(c.KT[:], 0.0).then_inc(kt_zero, 1)
            pool.memset(c.X[:, 0:1], 0.0)

        @block.vector
        def _(dve):
            link = c.vsteps.on(dve)

            def mul(o, a, bb_):
                return dve.tensor_tensor(o, a, bb_, ALU.mult)

            dve.wait_ge(u_in, 16)
            for a in range(2):
                half = slice(a * GROUPS // 2, (a + 1) * GROUPS // 2)
                dve.tensor_copy(ch[:, half].rearrange("k g (s e) -> k s g e", s=CH), u_rows[:, :, half]).then_inc(u_grouped, 1)
            dve.wait_ge(u_grouped, 2)
            tb, tt = ([t4[:, a, q * 256:(q + 1) * 256].rearrange("p (s e) -> p s e", s=ST) for q in range(4)]
                      for a in range(2))
            for t in range(CH):
                p_re, p_im = by_channel(pw, 0, t + 1), by_channel(pw, 1, t + 1)
                q4 = tt if t % 2 else tb
                mul(q4[0], cc[:, 0], p_re)
                mul(q4[1], cc[:, 1], p_im)
                mul(q4[2], cc[:, 1], p_re)
                link(mul(q4[3], cc[:, 0], p_im))
                dve.tensor_tensor(c.C[:, 0, :, t], q4[0], q4[1], ALU.add)
                link(dve.tensor_tensor(c.C[:, 1, :, t], q4[2], q4[3], ALU.subtract))
            dve.tensor_copy(c.A8[:, 0, 0], pw[:, 0, 8])
            dve.tensor_copy(c.A8[:, 0, 1], pw[:, 0, 8])
            dve.tensor_scalar(c.A8[:, 1, 0], pw[:, 1, 8], -1.0, None, ALU.mult)
            dve.tensor_copy(c.A8[:, 1, 1], pw[:, 1, 8])
            e7 = c.k("eye7").unsqueeze(1).broadcast_to([P, GROUPS, 16])
            dve.wait_ge(d_in, 16)
            link(mul(dd[:], dd[:], e7))
            dve.wait_ge(mt_ps, 1)
            dve.tensor_tensor(mt[:], c.ps[:, 2, :], dd[:].rearrange("p g e -> p (g e)"), ALU.add).then_inc(mt_ready, 1)


def prompt(nc, c):
    with ExitStack() as ctx:
        region = Region(local_tensor(nc, ctx, "prompt"), 0, LOCAL)
        def sem(name):
            return c.sem("prompt_" + name)

        kT = region.take([P, 2, SEQ])
        qT = region.take([P, HG, SEQ])
        rows = region.take([32, 2, 2, 16 * HD])
        hT = region.take([P, 32, 32])
        trail = region.take([HD, 4, 32])
        hid = region.take([HD, 4, 32])
        gt = region.take([HD, 2, 4, 32])
        kc = region.take([P, 32])
        vc = region.take([32, P])
        pr = region.take([P, 4, 512])
        pt = region.take([P, 2, 512])
        st = region.take([P, 8, 4])
        at = region.take([P, 4, 512])
        sc = region.take([P, 2, 2, ST])

        rows_in, tr_ps, tr_out, cmp_ps, trail_out, hid_scaled, hid_tanh, hid_ready, kc_ps, kc_out = (
            sem("rows_in"), sem("tr_ps"), sem("tr_out"), sem("cmp_ps"), sem("trail_out"),
            sem("hid_scaled"), sem("hid_tanh"), sem("hid_ready"), sem("kc_ps"), sem("kc_out"))
        score_ps, bias_ready, exp_done, pt_ps, pt_out, pv_ps, unit_out, at_ps, at_out, scanned, pe_ps = (
            sem("score_ps"), sem("bias_ready"), sem("exp_done"), sem("pt_ps"), sem("pt_out"), sem("pv_ps"),
            sem("unit_out"), sem("at_ps"), sem("at_out"), sem("scanned"), sem("pe_ps"))

        win_moved = sem("win_moved")

        work = [([c.z[:, i, ZK + 256 * (1 + s):ZK + 256 * (1 + s) + P] for i in range(4)], kT[:, s, :])
                for s in range(2)]
        for h in range(HG):
            work.append(([c.z[:, i, ZQ + h * P:ZQ + (h + 1) * P]
                          for i in range(4)], qT[:, h, :]))
        units = [(i, g, h, s) for i in range(4) for g in range(2) for h in range(HG) for s in range(3)]
        N = len(units)
        LAG = 3

        block = ctx.enter_context(nc.Block())

        @block.sync
        def _(sp):
            src = c.o["kv"][0:SEQ].rearrange("(n l) (s g d) -> n s g l d", l=16, s=4, g=2)
            for s in range(2):
                for g in range(2):
                    sp.dma_start(rows[:, s, g].rearrange("n (l d) -> n l d", l=16), src[:, s, g]).then_inc(rows_in, 16)
            sp.dma_start(c.o["win_s"][:, 0:SEQ - NT], c.d["win_rows"][:, NT:SEQ]).then_inc(win_moved, 16)
            sp.wait_ge(rows_in, 64)
            sp.wait_ge(win_moved, 16)

        @block.tensor
        def _(pe):
            for n, (srcs, _) in enumerate(work):
                if n >= 2:
                    pe.wait_ge(tr_out, n - 1)
                for a, src in enumerate(srcs):
                    mm = pe.transpose(c.ps[:, n % 2, a * P:(a + 1) * P], src, c.k("ident"))
                mm.then_inc(tr_ps, 1)
            pe.wait_ge(rows_in, 64)
            for n in range(2):
                pe.wait_ge(tr_out, len(work) + n - 1)
                for g in range(2):
                    for j in range(8):
                        a = g * 8 + j
                        mm = pe.transpose(c.ps[:, n % 2, a * 32:(a + 1) * 32], rows[:, n, g, j * P:(j + 1) * P], c.k("ident")[0:32, 0:32])
                mm.then_inc(tr_ps, 1)
            pe.wait_ge(tr_out, len(work) + 2)
            pe.wait_ge(c.w1_in, 16 * 4)
            for s in range(2):
                for g in range(2):
                    for j in range(8):
                        mm = pe.matmul(c.ps[:, 2, (s * 2 + g) * 32:(s * 2 + g + 1) * 32], c.w1[:, s, j],
                                       hT[:, s * 16 + g * 8 + j], start=j == 0, stop=j == 7)
            mm.then_inc(cmp_ps, 1)
            for s in range(2):
                for a in range(16):
                    mm = pe.matmul(c.ps[0:HD, 3, 64 + s:65 + s], c.w1[:, s, a % 8, a // 8 * HD:(a // 8 + 1) * HD],
                                   c.pe[:, s, a:a + 1], start=a == 0, stop=a == 15)
            mm.then_inc(pe_ps, 1)
            pe.wait_ge(hid_ready, 1)
            for g in range(2):
                pe.matmul(c.ps[HD * g:HD * (g + 1), 3, 0:32], c.w2[:, 0], hid[:, g], start=True, stop=True)
                mm = pe.matmul(c.ps[0:32, 4, g * HD:(g + 1) * HD], hid[:, 2 + g], c.w2[:, 1], start=True, stop=True)
            mm.then_inc(kc_ps, 1)
            pe.wait_ge(kc_out, 2)
            for step in range(N + LAG + 1):
                if step < N:
                    i, g, h, s = units[step]
                    lo, n = HD * g, 32 if s == 0 else (i + 1) * P
                    if step >= 4:
                        pe.wait_ge(exp_done, step - 3)
                    k = kc[lo:lo + HD, :] if s == 0 else kT[lo:lo + HD, s - 1, 0:n]
                    pe.matmul(c.ps[:, step % 4, 0:n], qT[lo:lo + HD, h, i * P:(i + 1) * P], k,
                              start=True, stop=True).then_inc(score_ps, 1)
                u = step - LAG
                if 0 <= u < N:
                    i, g, h, s = units[u]
                    pe.wait_ge(exp_done, u + 1)
                    if u >= 2:
                        pe.wait_ge(pt_out, u - 1)
                    if s == 0:
                        mm = pe.transpose(c.ps[0:32, 4 + u % 2, 0:P], pr[:, u % 4, 0:32], c.k("ident"))
                    else:
                        for a in range(i + 1):
                            mm = pe.transpose(c.ps[:, 4 + u % 2, a * P:(a + 1) * P], pr[:, u % 4, a * P:(a + 1) * P],
                                              c.k("ident"))
                    mm.then_inc(pt_ps, 1)
                u = step - LAG - 1
                if 0 <= u < N:
                    i, g, h, s = units[u]
                    pe.wait_ge(pt_out, u + 1)
                    if u >= 2:
                        pe.wait_ge(unit_out, u - 1)
                    if s == 0:
                        mm = pe.matmul(c.ps[:, 6 + u % 2, 0:HD], pt[0:31, u % 2, 0:P], vc[0:31, g * HD:(g + 1) * HD],
                                       start=True, stop=True)
                    else:
                        col = ZK + 256 * s + P + g * HD
                        for a in range(i + 1):
                            mm = pe.matmul(c.ps[:, 6 + u % 2, 0:HD], pt[:, u % 2, a * P:(a + 1) * P],
                                           c.z[:, a, col:col + HD], start=a == 0, stop=a == i)
                    mm.then_inc(pv_ps, 1)
            for n in range(4):
                if n == 0:
                    pe.wait_ge(unit_out, N)
                if n >= 2:
                    pe.wait_ge(at_out, n - 1)
                for i in range(4):
                    mm = pe.transpose(c.ps[:, n % 2, i * P:(i + 1) * P], at[:, i, n * P:(n + 1) * P], c.k("ident"))
                mm.then_inc(at_ps, 1)

        @block.scalar
        def _(act):
            for n, (_, dst) in enumerate(work):
                act.wait_ge(tr_ps, n + 1)
                act.activation(dst, c.ps[:, n % 2, :], ACT.Copy).then_inc(tr_out, 1)
            for n in range(2):
                act.wait_ge(tr_ps, len(work) + n + 1)
                act.activation(hT[:, n * 16:(n + 1) * 16], c.ps[:, n % 2, :].rearrange("p (a n) -> p a n", n=32),
                               ACT.Copy).then_inc(tr_out, 1)
            act.wait_ge(cmp_ps, 1)
            for s in range(2):
                act.activation(trail[:, 2 * s:2 * s + 2], c.ps[HD:P, 2, s * 64:(s + 1) * 64].rearrange("p (g n) -> p g n", g=2),
                               ACT.Copy).then_inc(trail_out, 1)
            act.wait_ge(hid_scaled, 1)
            act.activation(gt[:, 1, :, 0:31], gt[:, 0, :, 0:31], ACT.Tanh, scale=GELU_B).then_inc(hid_tanh, 1)
            act.wait_ge(kc_ps, 1)
            act.activation(kc[:], c.ps[:, 3, 0:32], ACT.Copy).then_inc(kc_out, 1)
            act.activation(vc[:], c.ps[0:32, 4, 0:P], ACT.Copy).then_inc(kc_out, 1)
            for step in range(N + LAG):
                if step < N:
                    i, g, h, s = units[step]
                    n = 32 if s == 0 else (i + 1) * P
                    act.wait_ge(bias_ready, step + 1)
                    if step >= 4:
                        act.wait_ge(pt_ps, step - 3)
                    if step >= 8:
                        act.wait_ge(unit_out, step - 7)
                    act.activation(pr[:, step % 4, 0:n], c.ps[:, step % 4, 0:n], ACT.Exp, bias=st[:, step % 8, 1:2],
                                   scale=SCALE, accum_out=st[:, step % 8, 2:3]).then_inc(exp_done, 1)
                u = step - LAG
                if u >= 0:
                    i, g, h, s = units[u]
                    act.wait_ge(pt_ps, u + 1)
                    if u >= 2:
                        act.wait_ge(pv_ps, u - 1)
                    r, n = (32, P) if s == 0 else (P, (i + 1) * P)
                    act.activation(pt[0:r, u % 2, 0:n], c.ps[0:r, 4 + u % 2, 0:n], ACT.Copy).then_inc(pt_out, 1)
            for n in range(4):
                act.wait_ge(at_ps, n + 1)
                act.activation(c.aT[:, n, 0:SEQ], c.ps[:, n % 2, :], ACT.Copy).then_inc(at_out, 1)

        @block.vector
        def _(dve):
            link = c.vsteps.on(dve)
            dve.tensor_copy(c.z4[:], c.z[:, 4])
            dve.wait_ge(pe_ps, 1)
            link(dve.tensor_tensor(c.b1[:], c.b1[:], c.ps[0:HD, 3, 64:66], ALU.add))
            dve.wait_ge(trail_out, 2)
            link(dve.memset(hid[:], 0.0))
            gelu_hidden(dve, link, c.b1, hid[:, :, 0:31],
                        c.ps[0:HD, 2, 0:P].rearrange("p (a n) -> p a n", a=4)[:, :, 0:31],
                        trail[:, :, 1:32], gt[:, :, :, 0:31], lambda ins: ins.then_inc(hid_scaled, 1),
                        lambda: dve.wait_ge(hid_tanh, 1))
            dve.engine_nop().then_inc(hid_ready, 1)
            for step in range(N + LAG + 1):
                if step < N:
                    i, g, h, s = units[step]
                    n = 32 if s == 0 else (i + 1) * P
                    dve.wait_ge(score_ps, step + 1)
                    S = c.ps[:, step % 4]
                    if s == 0:
                        link(dve.tensor_tensor(S[:, 0:32], S[:, 0:32], c.k("cmask")[:, i * 32:(i + 1) * 32], ALU.add))
                    else:
                        link(dve.tensor_tensor(S[:, i * P:n], S[:, i * P:n], c.k("causal"), ALU.add))
                    if step >= 4:
                        dve.wait_ge(exp_done, step - 3)
                    link(dve.tensor_reduce(st[:, step % 8, 0:1], S[:, 0:n], AX, ALU.max))
                    dve.tensor_scalar(st[:, step % 8, 1:2], st[:, step % 8, 0:1], -1.0e25, -SCALE, ALU.max,
                                      ALU.mult).then_inc(bias_ready, 1)
                u = step - LAG - 1
                if 0 <= u < N:
                    i, g, h, s = units[u]
                    head = g * HG + h
                    dve.wait_ge(exp_done, u + 1)
                    link(dve.tensor_scalar(st[:, u % 8, 3:4], st[:, u % 8, 2:3], 1.0e-30, None, ALU.max))
                    link(dve.reciprocal(st[:, u % 8, 3:4], st[:, u % 8, 3:4]))
                    link(dve.tensor_tensor(st[:, u % 8, 3:4], st[:, u % 8, 3:4], c.gate[:, i, head * 3 + s:head * 3 + s + 1],
                                           ALU.mult))
                    dve.wait_ge(pv_ps, u + 1)
                    o = at[:, i, head * HD:(head + 1) * HD]
                    if s == 0:
                        dve.tensor_scalar(o, c.ps[:, 6 + u % 2, 0:HD], st[:, u % 8, 3:4], None,
                                          ALU.mult).then_inc(unit_out, 1)
                    else:
                        dve.wait_ge(unit_out, u)
                        dve.scalar_tensor_tensor(o, c.ps[:, 6 + u % 2, 0:HD], st[:, u % 8, 3:4], o, ALU.mult,
                                                 ALU.add).then_inc(unit_out, 1)

        @block.gpsimd
        def _(pool):
            link = c.gsteps.on(pool)
            for k in range(PCH):
                x = c.X[:, k]
                pool.tensor_tensor(sc[:, 0], c.A8[:, 0], x, ALU.mult)
                link(pool.tensor_tensor(sc[:, 1], c.A8[:, 1], x[:, ::-1], ALU.mult))
                link(pool.tensor_tensor(sc[:, 0], sc[:, 0], c.S[:, k], ALU.add))
                link(pool.tensor_tensor(c.X[:, k + 1], sc[:, 0], sc[:, 1], ALU.add))
            pool.tensor_copy(c.XM[:, :, :, 0:PCH], c.X[:, 0:PCH].rearrange("p k r s -> p r s k"))
            pool.tensor_copy(c.XM[:, :, :, PCH:NCH], c.X[:, PCH + 1:PCH + 1 + NB].rearrange("p k r s -> p r s k"))
            pool.tensor_copy(c.fin[:, 0], c.X[:, PCH])
            for b in range(NB):
                x = c.X[:, PCH + 1 + b]
                pool.tensor_tensor(sc[:, 0], c.A8[:, 0], x, ALU.mult)
                link(pool.tensor_tensor(sc[:, 1], c.A8[:, 1], x[:, ::-1], ALU.mult))
                link(pool.tensor_tensor(sc[:, 0], sc[:, 0], c.S[:, PCH + b], ALU.add))
                link(pool.tensor_tensor(c.fin[:, 1 + b], sc[:, 0], sc[:, 1], ALU.add))
            pool.dma_start(c.o["ssm"], c.fin[:].rearrange("p k r s -> p (k r s)")).then_inc(scanned, 16)
            pool.wait_ge(scanned, 16)


def gelu_hidden(dve, link, bias, out, lead, trail, tmp, scaled, wait_tanh):
    n = out.shape[1] // 2
    for s in range(2):
        link(dve.scalar_tensor_tensor(out[:, s * n:(s + 1) * n], lead[:, s * n:(s + 1) * n], bias[:, s:s + 1],
                                      trail[:, s * n:(s + 1) * n], ALU.add, ALU.add))
    gelu_tail(dve, link, out, out, tmp[:, 0], tmp[:, 1], scaled, wait_tanh)


def gelu_tail(dve, link, out, x, t, e, scaled, wait_tanh):
    link(dve.tensor_tensor(t, x, x, ALU.mult))
    link(dve.tensor_scalar(t, t, GELU_A, 1.0, ALU.mult, ALU.add))
    scaled(dve.tensor_tensor(t, t, x, ALU.mult))
    wait_tanh()
    link(dve.tensor_scalar(e, e, 0.5, 0.5, ALU.mult, ALU.add))
    link(dve.tensor_tensor(out, x, e, ALU.mult))


def sample(nc, c):
    with ExitStack() as ctx:
        low = Region(c.arena, AT_STATE, AT_LOCAL)
        region = Region(local_tensor(nc, ctx, "sample"), 0, LOCAL)
        def sem(name):
            return c.sem("sample_" + name)

        NP = NB // 2
        pg = [Region(c.arena, AT_Z, AT_SSM).take([P, 2 * PAGES, 4, P]), region.take([P, 2 * PAGES, 4, P])]
        wk = low.take([P, 2, 2, SEQ])
        wv = low.take([P, 2, 2, 4, P])
        qs = low.take([P, HG, 64])
        gs = low.take([P, 4, 24])
        kn = region.take([P, 2, 64])
        qb = region.take([P, NB, 2, HG, NT])
        trail = region.take([HD, 4, P])
        hid = region.take([HD, 4, P])
        gt = region.take([HD, 2, 4, P])
        kc = region.take([P, P])
        vc = region.take([63, 2, P])
        S = region.take([P, 1088 + 576])
        pc = region.take([P, 64])
        imp = region.take([P, 70])
        half = region.take([P, 68])
        b17 = region.take([P, 6, 17])
        s1 = region.take([P, 16])
        gb = region.take([P, 3, 8])
        gsel = region.take([P, 3])
        pt = region.take([P, 16 * P])
        o = region.take([P, 2 * HD])

        imp_out = sem("imp_out")
        small_ps, small_out, qb_zero = (
            sem("small_ps"), sem("small_out"), sem("qb_zero"))
        rest_in = [sem(f"rest_of_pages_in{i}") for i in range(2)]
        cmp_in = [sem(f"cmp_pages_in{i}") for i in range(2)]
        window_in = [sem(f"window_in{i}") for i in range(2)]
        cmp_ps, trail_out, hid_scaled, hid_tanh, hid_ready, kc_ps, kc_out = (
            sem("s_cmp_ps"), sem("s_trail_out"), sem("s_hid_scaled"), sem("s_hid_tanh"), sem("s_hid_ready"),
            sem("s_kc_ps"), sem("s_kc_out"))
        wide_ps, sc_ps, bias_c, exp_c, pc_ready, imp_ps, pct_ps, pct_out = (
            sem("wide_ps"), sem("sc_ps"), sem("bias_c"), sem("exp_c"), sem("pc_ready"),
            sem("imp_ps"), sem("pct_ps"), sem("pct_out"))
        bias_w, exp_w, pt_ps, pt_out, pv_ps, o_ready, ot_ps, ot_out = (
            sem("bias_w"), sem("exp_w"), sem("s_pt_ps"), sem("s_pt_out"), sem("s_pv_ps"), sem("o_ready"),
            sem("ot_ps"), sem("ot_out"))
        def pages(eng, p, parts, arrived, which=range(2 * PAGES)):
            for a in which:
                at = 2 * PAGES * p + a
                v = eng.value_load(c.pages[0:1, at:at + 1], min_val=0, max_val=POOL - 1)
                eng.dma_start(pg[p % 2][:, a, parts], c.d["cache"][bass.ds(v, 1)].rearrange("o p s e -> (o p) s e")[:, parts]).then_inc(arrived, 16)

        KT = [(1, a, P) for a in range(4)] + [(1, 4, 64)] + [(0, a, P) for a in range(PAGES)] + [(0, PAGES, 64)]
        OFF = [1088 + a * P for a in range(4)] + [1088 + SEQ] + [a * P for a in range(PAGES)] + [PAST]
        GROUPED, BANK = [[0, 1, 2, 3], [4], [5, 6, 7, 8], [9, 10, 11, 12], [13]], [3, 4, 0, 1, 0]
        TURN = ((1, (0, 1)), (0, (2, 3, 4)))

        block = ctx.enter_context(nc.Block())

        @block.sync
        def _(sp):
            for p in range(NP):
                if p >= 2:
                    sp.wait_ge(cmp_ps, p - 1)
                pages(sp, p, slice(0, 2), cmp_in[p % 2], range(2 * PAGES if p else PAGES))
                if p >= 2:
                    sp.wait_ge(ot_out, 4 * (p - 1))
                sp.dma_start(wk[:, p % 2], c.d["win_kT"][:, 2 * p:2 * p + 2]).then_inc(window_in[p % 2], 16)
                sp.dma_start(wv[:, p % 2], c.d["win_v"][:, 2 * p:2 * p + 2]).then_inc(window_in[p % 2], 16)

        @block.gpsimd
        def _(pool):
            for p in range(NP):
                if p >= 2:
                    pool.wait_ge(ot_out, 4 * (p - 1))
                pages(pool, p, slice(2, 4), rest_in[p % 2])

        @block.tensor
        def _(pe):
            z4 = c.z4[0:64]
            idn = c.k("ident")[0:64, 0:64]
            for h in range(HG):
                pe.transpose(c.ps[:, 0, h * 64:(h + 1) * 64],
                             z4[:, ZQ + h * P:ZQ + (h + 1) * P], idn)
            for s in range(2):
                pe.transpose(c.ps[:, 0, 256 + s * 64:320 + s * 64], z4[:, ZK + 256 * (s + 1):ZK + 256 * (s + 1) + P], idn)
            for p in range(NP):
                mm = pe.matmul(c.ps[:, 1, p * 24:(p + 1) * 24], c.k("expand")[0:64, p * P:(p + 1) * P], c.gate[0:64, 4],
                               start=True, stop=True)
            mm.then_inc(small_ps, 1)
            pe.wait_ge(small_out, 3)
            pe.wait_ge(qb_zero, 9)

            def compress(p):
                pe.wait_ge(cmp_in[p % 2], 16 * 2 * PAGES * (p // 2 + 1))
                for s in range(2):
                    for g in range(2):
                        for j in range(8):
                            mov = pg[p % 2][:, :, s].rearrange("p a (g j n) -> p a g j n", g=2, j=8)[:, :, g, j]
                            mm = pe.matmul(c.ps[:, 5, (s * 2 + g) * P:(s * 2 + g + 1) * P], c.w1[:, s, j], mov,
                                           start=j == 0, stop=j == 7)
                mm.then_inc(cmp_ps, 1)

            for p in range(NP):
                b = p % 2
                if p == 0:
                    compress(0)
                else:
                    pe.wait_ge(ot_out, 4 * p)
                pe.wait_ge(rest_in[b], 16 * 2 * PAGES * (p // 2 + 1))
                pe.wait_ge(window_in[b], 32 * (p // 2 + 1))
                for e in range(2):
                    row = slice(HD * e, HD * (e + 1))
                    q = qb[:, 2 * p + e].rearrange("p g h t -> p (g h t)")
                    for a in range(2):
                        pe.matmul(c.ps[row, a, :], q, pg[b][:, e * PAGES + 4 * a:e * PAGES + 4 * a + 4, 2], start=True, stop=True)
                    pe.matmul(c.ps[row, 2, 0:64], q, kn[:, 0], start=True, stop=True)
                    pe.matmul(c.ps[row, 3, :], q, wk[:, b, e], start=True, stop=True)
                    mm = pe.matmul(c.ps[row, 4, 0:64], q, kn[:, 1], start=True, stop=True)
                mm.then_inc(wide_ps, 1)
                pe.wait_ge(hid_ready, p + 1)
                for g in range(2):
                    pe.matmul(c.ps[HD * g:HD * (g + 1), 6, 0:P], c.w2[:, 0], hid[:, g], start=True, stop=True)
                    for e in range(2):
                        mm = pe.matmul(c.ps[0:63, 7, e * P + g * HD:e * P + (g + 1) * HD], hid[:, 2 + g, e * 64:e * 64 + 63],
                                       c.w2[:, 1], start=True, stop=True)
                mm.then_inc(kc_ps, 1)
                pe.wait_ge(kc_out, 2 * p + 2)
                for e in range(2):
                    mm = pe.matmul(c.ps[HD * e:HD * (e + 1), 5, 0:63], qb[:, 2 * p + e].rearrange("p g h t -> p (g h t)"),
                                   kc[:, e * 64:e * 64 + 63], start=True, stop=True)
                mm.then_inc(sc_ps, 1)
                pe.wait_ge(pc_ready, p + 1)
                pe.matmul(c.ps[:, 7, 256:319], c.k("same"), pc[:, 0:63], start=True, stop=True).then_inc(imp_ps, 1)
                pe.transpose(c.ps[0:63, 6, 0:P], pc[:, 0:63], c.k("ident")).then_inc(pct_ps, 1)
                pe.wait_ge(pct_out, p + 1)
                pe.wait_ge(imp_out, p + 1)
                for e in range(2):
                    for g in range(2):
                        lo = 64 * e + 32 * g
                        mm = pe.matmul(c.ps[lo:lo + 32, 7, 0:HD], pt[0:63, lo:lo + 32], vc[0:63, e, g * HD:(g + 1) * HD],
                                       start=True, stop=True, tile_position=(0, lo))
                mm.then_inc(pv_ps, 1)
                if 0 < p < NP - 1:
                    compress(p + 1)
                for w, groups in TURN:
                    pe.wait_ge(exp_w, 2 * p + 2 - w)
                    for n in groups:
                        m = len(GROUPED) * p + n
                        if m >= 2:
                            pe.wait_ge(pt_out, m - 1)
                        for a, t in enumerate(GROUPED[n]):
                            r = KT[t][2]
                            mm = pe.transpose(c.ps[0:r, BANK[n], a * P:(a + 1) * P], S[:, OFF[t]:OFF[t] + r], c.k("ident"))
                        mm.then_inc(pt_ps, 1)
                    pe.wait_ge(pt_out, len(GROUPED) * p + groups[-1] + 1)
                    tiles = [t for t in range(len(KT)) if KT[t][0] == w]
                    for e in range(2):
                        for g in range(2):
                            lo = 64 * e + 32 * g
                            for t in tiles:
                                a, r = KT[t][1], KT[t][2]
                                if r == 64:
                                    v = c.z4[0:64, ZK + 256 * (w + 1) + P + g * HD:ZK + 256 * (w + 1) + P + (g + 1) * HD]
                                elif w == 0:
                                    v = pg[b][:, e * PAGES + a, 3, g * HD:(g + 1) * HD]
                                else:
                                    v = wv[:, b, e, a, g * HD:(g + 1) * HD]
                                mm = pe.matmul(c.ps[lo:lo + 32, 3 + w, 0:HD], pt[0:r, t * P + lo:t * P + lo + 32], v,
                                               start=t == tiles[0], stop=t == tiles[-1], tile_position=(0, lo))
                    mm.then_inc(pv_ps, 1)
                if p == 0:
                    compress(1)
                pe.wait_ge(o_ready, p + 1)
                pe.transpose(c.ps[:, 2, 0:P], o[:], c.k("ident")).then_inc(ot_ps, 1)

        @block.scalar
        def _(act):
            pages(act, 0, slice(0, 2), cmp_in[0], range(PAGES, 2 * PAGES))
            act.wait_ge(small_ps, 1)
            act.activation(qs[:], c.ps[:, 0, 0:256].rearrange("p (h t) -> p h t", h=HG), ACT.Copy).then_inc(small_out, 1)
            act.activation(kn[:], c.ps[:, 0, 256:384].rearrange("p (s t) -> p s t", s=2), ACT.Copy).then_inc(small_out, 1)
            act.activation(gs[:], c.ps[:, 1, 0:96].rearrange("p (a e) -> p a e", a=4), ACT.Copy).then_inc(small_out, 1)
            act.wait_ge(small_out, 1)
            act.wait_ge(qb_zero, 1)
            for g in range(2):
                r = slice(HD * g, HD * (g + 1))
                for h in range(HG):
                    act.activation(qb[r, :, g, h], qs[r, h].rearrange("p (b t) -> p b t", b=NB), ACT.Copy).then_inc(qb_zero, 1)
            for p in range(NP):
                act.wait_ge(cmp_ps, p + 1)
                if p:
                    act.wait_ge(hid_ready, p)
                for s in range(2):
                    act.activation(trail[:, 2 * s:2 * s + 2], c.ps[HD:P, 5, s * 256:(s + 1) * 256].rearrange("p (g n) -> p g n", g=2),
                                   ACT.Copy).then_inc(trail_out, 1)
                act.wait_ge(hid_scaled, p + 1)
                g4 = gt[:].rearrange("p r a (b n) -> p r (a b) n", b=2)[:, :, :, 0:63]
                act.activation(g4[:, 1], g4[:, 0], ACT.Tanh, scale=GELU_B).then_inc(hid_tanh, 1)
                act.wait_ge(kc_ps, p + 1)
                act.activation(kc[:], c.ps[:, 6, 0:P], ACT.Copy).then_inc(kc_out, 1)
                act.activation(vc[:], c.ps[0:63, 7, 0:2 * P].rearrange("p (e n) -> p e n", e=2), ACT.Copy).then_inc(kc_out, 1)
                act.wait_ge(bias_c, p + 1)
                act.activation(pc[:, 0:63], c.ps[:, 5, 0:63], ACT.Exp, bias=s1[:, 1:2], scale=SCALE,
                               accum_out=s1[:, 2:3]).then_inc(exp_c, 1)
                act.wait_ge(pct_ps, p + 1)
                act.activation(pt[0:63, 0:P], c.ps[0:63, 6, 0:P], ACT.Copy).then_inc(pct_out, 1)
                for w, groups in TURN:
                    act.wait_ge(bias_w, 2 * p + 2 - w)
                    s = S[:, 1088 * w:1088 + 576 * w]
                    act.activation(s, s, ACT.Exp, bias=s1[:, 4 + 3 * w:5 + 3 * w], scale=SCALE,
                                   accum_out=s1[:, 5 + 3 * w:6 + 3 * w]).then_inc(exp_w, 1)
                    if w == 1:
                        act.wait_ge(pv_ps, 3 * p + 1)
                    for n in groups:
                        tiles = GROUPED[n]
                        act.wait_ge(pt_ps, len(GROUPED) * p + n + 1)
                        full = [t for t in tiles if KT[t][2] == P]
                        for t0, t1, r in ([(tiles[0], tiles[-1] + 1, P)] if len(full) == len(tiles) else
                                          [(t, t + 1, KT[t][2]) for t in tiles]):
                            a = t0 - tiles[0]
                            ins = act.activation(pt[0:r, t0 * P:t1 * P], c.ps[0:r, BANK[n], a * P:(a + t1 - t0) * P], ACT.Copy)
                        ins.then_inc(pt_out, 1)
                act.wait_ge(ot_ps, p + 1)
                for h2 in range(2):
                    src = c.ps[HD * h2:HD * (h2 + 1), 2, 0:P].rearrange("p (b n f t) -> p b n f t", b=2, n=4, f=2)[:, :, :, h2]
                    dst = c.aT[HD * h2:HD * (h2 + 1), :, SEQ + 16 * p:SEQ + 16 * (p + 1)].rearrange("p n (b t) -> p b n t", b=2)
                    for e in range(2):
                        act.activation(dst[:, e], src[:, e], ACT.Copy).then_inc(ot_out, 1)

        @block.vector
        def _(dve):
            link = c.vsteps.on(dve)
            dve.memset(s1[:], 0.0)
            dve.memset(hid[:], 0.0)
            dve.memset(imp[:], 0.0)
            dve.memset(qb[:], 0.0).then_inc(qb_zero, 1)
            dve.wait_ge(small_out, 3)
            for p in range(NP):
                dve.wait_ge(trail_out, 2 * p + 2)
                if p:
                    dve.wait_ge(kc_ps, p)
                    dve.wait_ge(ot_out, 4 * p)

                def v3(ap):
                    return ap.rearrange("p a (b n) -> p (a b) n", b=2)
                gelu_hidden(dve, link, c.b1, v3(hid[:])[:, :, 0:63],
                            c.ps[0:HD, 5, :].rearrange("p (a n) -> p a n", n=64)[:, :, 0:63],
                            v3(trail[:])[:, :, 1:64],
                            gt[:].rearrange("p r a (b n) -> p r (a b) n", b=2)[:, :, :, 0:63],
                            lambda ins: ins.then_inc(hid_scaled, 1), lambda: dve.wait_ge(hid_tanh, p + 1))
                dve.engine_nop().then_inc(hid_ready, 1)
                g3 = gs[:, p].rearrange("p (h r) -> p r h", r=3)
                link(dve.tensor_tensor(gb[:], g3, c.k("headpick").unsqueeze(1).broadcast_to([P, 3, 8]), ALU.mult))
                link(dve.tensor_reduce(gsel[:], gb[:], AX, ALU.add))
                dve.wait_ge(sc_ps, p + 1)
                link(dve.tensor_reduce(s1[:, 0:1], c.ps[:, 5, 0:63], AX, ALU.max))
                dve.tensor_scalar(s1[:, 1:2], s1[:, 0:1], -SCALE, None, ALU.mult).then_inc(bias_c, 1)
                dve.wait_ge(exp_c, p + 1)
                link(dve.reciprocal(s1[:, 3:4], s1[:, 2:3]))
                dve.tensor_scalar(pc[:, 0:63], pc[:, 0:63], s1[:, 3:4], None, ALU.mult).then_inc(pc_ready, 1)
                dve.wait_ge(wide_ps, p + 1)
                W = S[:, 1088:1088 + 576]
                dve.tensor_tensor(W[:, 0:8], c.ps[:, 3, 0:8], c.k("winmask"), ALU.add)
                dve.tensor_copy(W[:, 8:SEQ], c.ps[:, 3, 8:SEQ])
                nm = c.k("newmask")[:, 64 * p:64 * (p + 1)]
                link(dve.tensor_tensor(W[:, SEQ:SEQ + 64], c.ps[:, 4, 0:64], nm, ALU.add))
                link(dve.tensor_reduce(s1[:, 6:7], W, AX, ALU.max))
                dve.tensor_scalar(s1[:, 7:8], s1[:, 6:7], -SCALE, None, ALU.mult).then_inc(bias_w, 1)
                dve.wait_ge(imp_ps, p + 1)
                dve.tensor_copy(imp[:, 1:64], c.ps[:, 7, 256:319]).then_inc(imp_out, 1)
                dve.wait_ge(imp_out, p + 1)
                link(dve.tensor_tensor(half[:], imp[:, 1:69], imp[:, 0:68], ALU.add))
                link(dve.tensor_reduce(b17[:, 0], half[:].rearrange("p (b n) -> p b n", n=4), AX, ALU.add))
                fo = c.k("force17")
                link(dve.tensor_scalar(b17[:, 1], fo, -1.0, 1.0, ALU.mult, ALU.add))
                link(dve.tensor_tensor(b17[:, 1], b17[:, 1], b17[:, 0], ALU.mult))
                link(dve.scalar_tensor_tensor(b17[:, 1], fo, 1.0e4, b17[:, 1], ALU.mult, ALU.add))
                link(dve.tensor_reduce(s1[:, 12:13], b17[:, 1], AX, ALU.min))
                link(dve.tensor_scalar(b17[:, 2], b17[:, 1], s1[:, 12:13], None, ALU.is_equal))
                link(dve.tensor_tensor(b17[:, 2], b17[:, 2], c.k("blk17"), ALU.mult))
                link(dve.tensor_reduce(s1[:, 13:14], b17[:, 2], AX, ALU.max))
                link(dve.tensor_scalar(b17[:, 3], b17[:, 2], s1[:, 13:14], NEG, ALU.is_equal, ALU.mult))
                for a in range(2):
                    link(dve.tensor_tensor(S[:, 512 * a:512 * (a + 1)].rearrange("p (b n) -> p b n", n=64),
                                           c.ps[:, a, :].rearrange("p (b n) -> p b n", n=64),
                                           b17[:, 3, 8 * a:8 * a + 8].unsqueeze(2).broadcast_to([P, 8, 64]), ALU.add))
                link(dve.tensor_tensor(S[:, PAST:PAST + 64], c.ps[:, 2, 0:64], nm, ALU.add))
                link(dve.tensor_reduce(s1[:, 14:15], S[:, 0:1088], AX, ALU.max))
                dve.tensor_scalar(s1[:, 4:5], s1[:, 14:15], -SCALE, None, ALU.mult).then_inc(bias_w, 1)
                dve.wait_ge(exp_w, 2 * p + 2)
                link(dve.reciprocal(s1[:, 9:10], s1[:, 5:6]))
                link(dve.reciprocal(s1[:, 10:11], s1[:, 8:9]))
                link(dve.tensor_tensor(s1[:, 9:11], s1[:, 9:11], gsel[:, 1:3], ALU.mult))
                dve.wait_ge(pv_ps, 3 * p + 3)
                link(dve.tensor_scalar(o[:, 0:HD], c.ps[:, 7, 0:HD], gsel[:, 0:1], None, ALU.mult))
                link(dve.scalar_tensor_tensor(o[:, 0:HD], c.ps[:, 3, 0:HD], s1[:, 9:10], o[:, 0:HD], ALU.mult, ALU.add))
                link(dve.scalar_tensor_tensor(o[:, 0:HD], c.ps[:, 4, 0:HD], s1[:, 10:11], o[:, 0:HD], ALU.mult, ALU.add))
                dve.tensor_copy(o[:, HD:2 * HD], o[:, 0:HD]).then_inc(o_ready, 1)


def merge(nc, c):
    with ExitStack() as ctx:
        def sem(name):
            return c.sem("merge_" + name)

        local = local_tensor(nc, ctx, "merge")
        region = Region(local, 0, LOCAL)
        small = Region(c.arena, AT_Z4 + 16 * TOK, AT_SSM)
        sig = Region(c.arena, AT_Z4, AT_SSM).take([P, 16, TOK])
        w_out = Region(c.arena, AT_KT, AT_XM).take([P, KD, D])
        late = Region(local, 0, 8192)
        w_glu = region.take([P, 4, D])
        w_ssm = region.take([P, 4, D])
        c.x2 = x = Region(c.arena, AT_XM, AT_X2_END).take([P, TILES, D])
        h = late.take([P, 2, D])
        hT = late.take([P, KD, P])
        w_attn = Region(c.arena, AT_X2_END, AT_LOCAL).take([P, 4, D])
        glu = Region(local, region.pos, LOCAL).take([P, 4, TOK])
        y = region.take([NCH, CH, SW])
        route = Region(local, region.pos, LOCAL)
        tmp = region.take([P, 2, 2, 512])
        yT = region.take([P, 4, TOK])
        g_ffn = small.take([P, D])
        w_route = small.take([P, KD, 36])
        b_route = small.take([P, 36])

        ss = route.take([P, TILES])
        lg = route.take([P, TILES, 36])
        gm = route.take([P, TILES])
        goh = route.take([P, TILES, 4])
        t4 = route.take([P, TILES, 4])
        gw = route.take([P, TILES])
        el = route.take([P, TILES, 32])
        t32 = route.take([P, TILES, 32])
        top = route.take([P, 2, TILES])
        pick = route.take([P, TILES])
        M = route.take([P, 3, TILES, 32])
        nb = route.take([P, 4, 32])
        dest = route.take([P, 2, TILES])
        reached = route.take([P, 2, TILES, TABLE + 1])
        in_block = route.take([P, 2, TILES])
        numbers = route.take([P, 2, TILES, TABLE, 2])
        at_slot = route.take([P, 2, TILES, SLOTS])
        be = route.take([1, BLOCKS, 32])
        bf = route.take([1, BLOCKS + 2])

        sig_in, wg_in, ws_in, wa_in, wo_in, x_in, rt_in = (
            sem("sig_in"), sem("wg_in"), sem("ws_in"), sem("wa_in"), sem("wo_in"), sem("m_x_in"), sem("rt_in"))
        y_ps, sq_done, u_ready, y_tanh, y_done, yt_ps, yt_out = (
            sem("y_ps"), sem("sq_done"), sem("u_ready"), sem("y_tanh"), sem("y_done"), sem("yt_ps"), sem("yt_out"))
        glu_ps, glu_tanh, glu_done, proj_ps, proj_done, out_ps, x_done = (
            sem("glu_ps"), sem("glu_tanh"), sem("glu_done"), sem("proj_ps"), sem("proj_done"), sem("out_ps"),
            sem("x_done"))
        sq2, h_ready, h_stored, ht_ps, ht_out, lg_ps = (
            sem("sq2"), sem("h_ready"), sem("h_stored"), sem("ht_ps"), sem("ht_out"), sem("lg_ps"))
        ge_ready, ge_exp, te_ready, te_exp, m_ready, rank_ps, pick_ready, table_ps = (
            sem("ge_ready"), sem("ge_exp"), sem("te_ready"), sem("te_exp"), sem("m_ready"), sem("rank_ps"),
            sem("pick_ready"), sem("table_ps"))
        mean2, root2, first_in = sem("mean2"), sem("root2"), sem("first_weights_in")
        NY = GROUPS // 4

        block = ctx.enter_context(nc.Block())

        @block.sync
        def _(sp):
            sp.dma_start(w_glu[:], c.d["w_glu"]).then_inc(wg_in, 16)
            sp.dma_start(w_ssm[:], c.d["w_ssm"]).then_inc(ws_in, 16)
            sp.dma_start(w_attn[:], c.d["w_attn"]).then_inc(wa_in, 16)
            sp.dma_start(sig[:], c.d["sig"].rearrange("m p t -> p m t")).then_inc(sig_in, 16)
            sp.dma_start(g_ffn[:], c.d["g_ffn"]).then_inc(rt_in, 16)
            sp.dma_start(w_route[:], c.d["w_route"]).then_inc(rt_in, 16)
            sp.dma_start(b_route[:], c.d["b_route"]).then_inc(rt_in, 16)
            sp.wait_ge(y_ps, NY)
            sp.dma_start(w_out[:], c.d["w_out"]).then_inc(wo_in, 16)
            sp.wait_ge(proj_ps, 32)
            sp.dma_start(x[:, 0:4], c.d["x"][0:SEQ].rearrange("(i p) d -> p i d", p=P)).then_inc(x_in, 16)
            sp.dma_start(x[0:64, 4], c.d["x"][SEQ:TOK]).then_inc(x_in, 16)
            for i in range(TILES):
                sp.wait_ge(h_ready, i + 1)
                sp.dma_start(c.d["h"][i * P:i * P + ROWS[i]], h[0:ROWS[i], i % 2]).then_inc(h_stored, 16)
                sp.wait_ge(h_stored, 16 * (i + 1))
            for p in range(PIECES):
                if p == PIECES - 1:
                    sp.wait_ge(m_ready, 1)
                sp.dma_start(c.raw[:, p], c.d["w_exp"][0, p]).then_inc(first_in, 16)
            sp.wait_ge(first_in, 16 * PIECES)

        @block.tensor
        def _(pe):
            for n in range(NY):
                if n >= 4:
                    pe.wait_ge(y_done, n - 3)
                for a in range(4):
                    g = 2 * (4 * (n // 2) + a) + n % 2
                    lo, tl = HD * (g % 2), g // 2
                    o = c.ps[0:NCH, n % 4, a * P:(a + 1) * P]
                    pe.matmul(o, c.U[:, g], c.KT[:, :, g * 16:(g + 1) * 16], start=True, stop=False)
                    for r in range(2):
                        mm = pe.matmul(o, c.XM[lo:lo + HD, r, tl], c.C[lo:lo + HD, r, tl].rearrange("p t e -> p (t e)"),
                                       start=False, stop=r == 1)
                mm.then_inc(y_ps, 1)
            pe.wait_ge(y_done, NY)
            for n in range(8):
                if n >= 2:
                    pe.wait_ge(yt_out, n - 1)
                for a in range(4):
                    t = 4 * (n % 2) + a
                    mm = pe.transpose(c.ps[:, 4 + n % 2, a * NCH:(a + 1) * NCH], y[:, t, n // 2 * P:(n // 2 + 1) * P],
                                      c.k("ident")[0:NCH, 0:NCH])
                mm.then_inc(yt_ps, 1)
            pe.wait_ge(yt_out, 8)
            pe.wait_ge(wg_in, 16)
            for u in range(8):
                j, t = u // 2, slice(u % 2 * HALF, (u % 2 + 1) * HALF)
                if u >= 2:
                    pe.wait_ge(glu_done, u - 1)
                for e in range(2):
                    for k in range(4):
                        mm = pe.matmul(c.ps[:, 2 * e + u % 2, 0:HALF], w_glu[:, k, (4 * e + j) * P:(4 * e + j + 1) * P],
                                       yT[:, k, t], start=k == 0, stop=k == 3)
                    mm.then_inc(glu_ps, 1)
            pe.wait_ge(glu_done, 8)
            pe.wait_ge(ws_in, 16)
            pe.wait_ge(wa_in, 16)
            for u in range(16):
                m, t = u // 2, slice(u % 2 * HALF, (u % 2 + 1) * HALF)
                if u >= 2:
                    pe.wait_ge(proj_done, u - 1)
                for e, (w, mov) in enumerate(((w_ssm, glu), (w_attn, c.aT))):
                    for k in range(4):
                        mm = pe.matmul(c.ps[:, 4 + 2 * e + u % 2, 0:HALF], w[:, k, m * P:(m + 1) * P], mov[:, k, t],
                                       start=k == 0, stop=k == 3)
                    mm.then_inc(proj_ps, 1)
            pe.wait_ge(proj_done, 16)
            pe.wait_ge(wo_in, 16)
            for i in range(TILES + 1):
                if i < TILES:
                    for n in range(2):
                        if i >= 1:
                            pe.wait_ge(x_done, 2 * i + n - 1)
                        for k in range(KD):
                            mm = pe.matmul(c.ps[0:ROWS[i], n, :], sig[:, k, i * P:i * P + ROWS[i]],
                                           w_out[:, k, n * 512:(n + 1) * 512], start=k == 0, stop=k == KD - 1)
                        mm.then_inc(out_ps, 1)
                if i >= 1:
                    r = ROWS[i - 1]
                    pe.wait_ge(h_ready, i)
                    if i >= 2:
                        pe.wait_ge(ht_out, 2 * (i - 1))
                    for n in range(2):
                        for a in range(4):
                            mm = pe.transpose(c.ps[:, 2 + n, a * P:a * P + r], h[0:r, (i - 1) % 2, (4 * n + a) * P:(4 * n + a + 1) * P],
                                              c.k("ident")[0:r, 0:r])
                        mm.then_inc(ht_ps, 1)
                    pe.wait_ge(ht_out, 2 * i)
                    pe.wait_ge(rt_in, 48)
                    for k in range(KD):
                        mm = pe.matmul(c.ps[0:r, 4, (i - 1) * 36:i * 36], hT[:, k, 0:r], w_route[:, k], start=k == 0,
                                       stop=k == KD - 1)
                    mm.then_inc(lg_ps, 1)
            pe.wait_ge(m_ready, 1)
            for i in range(TILES + 1):
                for a in range(min(i + 1, TILES)):
                    mm = pe.matmul(c.ps[:, 5, i * 32:(i + 1) * 32], c.k("tri") if a == i else c.k("ones"), M[:, 2, a],
                                   start=a == 0, stop=a == min(i, TILES - 1))
            mm.then_inc(rank_ps, 1)
            for j in range(2):
                pe.wait_ge(pick_ready, j + 1)
                for i in range(TILES):
                    mm = pe.matmul(c.ps[0:SLOTS, 6, 0:2 * TABLE], at_slot[0:ROWS[i], j, i],
                                   numbers[0:ROWS[i], j, i].rearrange("p b o -> p (b o)"),
                                   start=j == 0 and i == 0, stop=j == 1 and i == TILES - 1)
            mm.then_inc(table_ps, 1)

        @block.scalar
        def _(act):
            def square(n):
                act.wait_ge(y_ps, n + 1)
                if n >= 2:
                    act.wait_ge(y_tanh, n - 1)
                act.activation(tmp[0:NCH, n % 2, 0], c.ps[0:NCH, n % 4, :], ACT.Square).then_inc(sq_done, 1)

            square(0)
            for n in range(NY):
                if n + 1 < NY:
                    square(n + 1)
                act.wait_ge(u_ready, n + 1)
                if n >= 2:
                    act.wait_ge(y_done, n - 1)
                act.activation(tmp[0:NCH, n % 2, 1], tmp[0:NCH, n % 2, 0], ACT.Tanh, scale=GELU_B).then_inc(y_tanh, 1)
            for n in range(8):
                act.wait_ge(yt_ps, n + 1)
                dst = yT[:, n // 2].rearrange("p (k t) -> p t k", t=CH)[:, 4 * (n % 2):4 * (n % 2) + 4]
                act.activation(dst, c.ps[:, 4 + n % 2, 0:4 * NCH].rearrange("p (t k) -> p t k", t=4), ACT.Copy).then_inc(yt_out, 1)
            for u in range(8):
                act.wait_ge(glu_ps, 2 * u + 2)
                if u >= 2:
                    act.wait_ge(glu_done, u - 1)
                act.activation(tmp[:, u % 2, 0, 0:HALF], c.ps[:, 2 + u % 2, 0:HALF], ACT.Tanh, scale=0.5).then_inc(glu_tanh, 1)
            for i in range(TILES):
                act.wait_ge(x_done, 2 * i + 2)
                if i:
                    act.wait_ge(h_ready, i)
                if i >= 2:
                    act.wait_ge(h_stored, 16 * (i - 1))
                act.activation(h[:, i % 2], x[:, i], ACT.Square, accum_out=ss[:, i:i + 1]).then_inc(sq2, 1)
                act.wait_ge(mean2, i + 1)
                act.activation(ss[:, i:i + 1], ss[:, i:i + 1], ACT.Sqrt).then_inc(root2, 1)
                for n in range(2):
                    act.wait_ge(ht_ps, 2 * i + n + 1)
                    if i and n == 0:
                        act.wait_ge(lg_ps, i)
                    r = ROWS[i]
                    src = c.ps[:, 2 + n, :].rearrange("p (a t) -> p a t", a=4)[:, :, 0:r]
                    act.activation(hT[:, 4 * n:4 * n + 4, 0:r], src, ACT.Copy).then_inc(ht_out, 1)
            act.wait_ge(ge_ready, 1)
            act.activation(t4[:], t4[:], ACT.Exp).then_inc(ge_exp, 1)
            act.wait_ge(te_ready, 1)
            act.activation(c.wt[:, 1], c.wt[:, 1], ACT.Exp).then_inc(te_exp, 1)

        @block.vector
        def _(dve):
            link = c.vsteps.on(dve)

            def before_exp(n):
                t, ps = tmp[0:NCH, n % 2, 0], c.ps[0:NCH, n % 4, :]
                dve.wait_ge(sq_done, n + 1)
                link(dve.tensor_scalar(t, t, GELU_A, 1.0, ALU.mult, ALU.add))
                dve.tensor_tensor(t, t, ps, ALU.mult).then_inc(u_ready, 1)

            before_exp(0)
            for n in range(NY):
                if n + 1 < NY:
                    before_exp(n + 1)
                e = tmp[0:NCH, n % 2, 1]
                dve.wait_ge(y_tanh, n + 1)
                link(dve.tensor_scalar(e, e, 0.5, 0.5, ALU.mult, ALU.add))
                by4 = "k (g t e) -> k g t e"
                dve.tensor_tensor(y[:].rearrange("k t (s h e) -> k s h t e", h=2, e=16)[:, 4 * (n // 2):4 * (n // 2) + 4, n % 2],
                                  c.ps[0:NCH, n % 4, :].rearrange(by4, g=4, t=CH),
                                  e.rearrange(by4, g=4, t=CH), ALU.mult).then_inc(y_done, 1)
            for u in range(8):
                e = tmp[:, u % 2, 0, 0:HALF]
                dve.wait_ge(glu_tanh, u + 1)
                link(dve.tensor_scalar(e, e, 0.5, 0.5, ALU.mult, ALU.add))
                if u == 0:
                    dve.wait_ge(yt_ps, 8)
                dve.tensor_tensor(glu[:, u // 2, u % 2 * HALF:(u % 2 + 1) * HALF], c.ps[:, u % 2, 0:HALF], e,
                                  ALU.mult).then_inc(glu_done, 1)
            dve.wait_ge(sig_in, 16)
            for u in range(16):
                m, t = u // 2, slice(u % 2 * HALF, (u % 2 + 1) * HALF)
                dve.wait_ge(proj_ps, 2 * u + 2)
                dve.tensor_tensor(sig[:, m, t], sig[:, m, t], c.ps[:, 4 + u % 2, 0:HALF], ALU.mult)
                link(dve.tensor_tensor(sig[:, 8 + m, t], sig[:, 8 + m, t], c.ps[:, 6 + u % 2, 0:HALF], ALU.mult))
                dve.tensor_tensor(sig[:, m, t], sig[:, m, t], sig[:, 8 + m, t], ALU.add).then_inc(proj_done, 1)
            dve.wait_ge(x_in, 32)
            dve.wait_ge(rt_in, 48)
            link(dve.memset(x[64:P, 4], 0.0))
            for i in range(TILES):
                r = ROWS[i]
                for n in range(2):
                    dve.wait_ge(out_ps, 2 * i + n + 1)
                    xs = x[0:r, i, n * 512:(n + 1) * 512]
                    dve.tensor_tensor(xs, c.ps[0:r, n, :], xs, ALU.add).then_inc(x_done, 1)
                dve.wait_ge(sq2, i + 1)
                dve.tensor_scalar(ss[:, i:i + 1], ss[:, i:i + 1], 1.0 / D, EPS, ALU.mult, ALU.add).then_inc(mean2, 1)
                dve.wait_ge(root2, i + 1)
                link(dve.reciprocal(ss[:, i:i + 1], ss[:, i:i + 1]))
                dve.scalar_tensor_tensor(h[:, i % 2], x[:, i], ss[:, i:i + 1], g_ffn[:], ALU.mult,
                                         ALU.mult).then_inc(h_ready, 1)
            dve.wait_ge(lg_ps, TILES)
            link(dve.memset(lg[:], 0.0))
            ps = c.ps[:, 4, 0:TILES * 36].rearrange("p (i e) -> p i e", e=36)
            link(dve.tensor_tensor(lg[:, 0:4], ps[:, 0:4], b_route.unsqueeze(1).broadcast_to([P, 4, 36]), ALU.add))
            link(dve.tensor_tensor(lg[0:64, 4], ps[0:64, 4], b_route[0:64], ALU.add))

            def wide(col, n):
                return col.unsqueeze(2).broadcast_to([P, TILES, n])

            def first_of_max(out, vals, mx, desc, n):
                link(dve.tensor_tensor(out, vals, wide(mx, n), ALU.is_equal))
                link(dve.tensor_tensor(out, out, desc.unsqueeze(1).broadcast_to([P, TILES, n]), ALU.mult))
                link(dve.tensor_reduce(pick[:], out, AX, ALU.max))
                link(dve.tensor_tensor(out, out, wide(pick[:], n), ALU.is_equal))

            gl = lg[:, :, 0:4]
            link(dve.tensor_reduce(gm[:], gl, AX, ALU.max))
            dve.tensor_tensor(t4[:], gl, wide(gm[:], 4), ALU.subtract).then_inc(ge_ready, 1)
            first_of_max(goh[:], gl, gm[:], c.k("desc4"), 4)
            dve.wait_ge(ge_exp, 1)
            link(dve.tensor_reduce(gw[:], t4[:], AX, ALU.add))
            link(dve.reciprocal(gw[:], gw[:]))
            link(dve.tensor_scalar(t4[:], goh[:], -1.0, -NEG, ALU.add, ALU.mult))
            link(dve.tensor_tensor(el[:].rearrange("p i (g e) -> p i g e", g=4),
                                   lg[:, :, 4:36].rearrange("p i (g e) -> p i g e", g=4),
                                   t4[:].unsqueeze(3).broadcast_to([P, TILES, 4, 8]), ALU.add))
            link(dve.tensor_reduce(top[:, 0], el[:], AX, ALU.max))
            first_of_max(M[:, 0], el[:], top[:, 0], c.k("desc32"), 32)
            link(dve.scalar_tensor_tensor(t32[:], M[:, 0], -3.0e38, el[:], ALU.mult, ALU.add))
            link(dve.tensor_reduce(top[:, 1], t32[:], AX, ALU.max))
            first_of_max(M[:, 1], t32[:], top[:, 1], c.k("desc32"), 32)
            for j in range(2):
                link(dve.tensor_tensor(M[:, j], M[:, j], wide(c.k("valid"), 32), ALU.mult))
            dve.tensor_tensor(M[:, 2], M[:, 0], M[:, 1], ALU.add).then_inc(m_ready, 1)
            dve.tensor_tensor(c.wt[:, 1], top[:, 1], top[:, 0], ALU.subtract).then_inc(te_ready, 1)
            dve.wait_ge(te_exp, 1)
            link(dve.tensor_scalar(c.wt[:, 0], c.wt[:, 1], 1.0, None, ALU.add))
            link(dve.reciprocal(c.wt[:, 0], c.wt[:, 0]))
            link(dve.tensor_tensor(c.wt[:, 0], c.wt[:, 0], gw[:], ALU.mult))
            link(dve.tensor_tensor(c.wt[:, 1], c.wt[:, 1], c.wt[:, 0], ALU.mult))
            dve.wait_ge(rank_ps, 1)
            cnt = c.ps[:, 5, 5 * 32:6 * 32]
            over = numbers[:, 0].rearrange("p i b o -> p (i b o)")[:, 0:32 * TOK // SLOTS].rearrange("p (e k) -> p e k", e=32)
            link(dve.tensor_tensor(over, cnt.unsqueeze(2).broadcast_to([P, 32, TOK // SLOTS]),
                                   c.k("blkslot")[:, 0:TOK // SLOTS].unsqueeze(1).broadcast_to([P, 32, TOK // SLOTS]), ALU.is_gt))
            link(dve.tensor_reduce(nb[:, 0], over, AX, ALU.add))
            link(dve.tensor_scalar(nb[:, 0, 0:1], nb[:, 0, 0:1], 1.0, None, ALU.max))
            link(dve.tensor_tensor_scan(nb[:, 1], c.k("ones")[:, 0:32], nb[:, 0], 0.0, ALU.mult, ALU.add))
            link(dve.tensor_tensor(nb[:, 2], nb[:, 1], nb[:, 0], ALU.subtract))
            link(dve.tensor_scalar(nb[:, 2], nb[:, 2], float(SLOTS), None, ALU.mult))
            link(dve.tensor_tensor(t32[:], c.ps[:, 5, 0:5 * 32].rearrange("p (i e) -> p i e", e=32),
                                   nb[:, 2].unsqueeze(1).broadcast_to([P, TILES, 32]), ALU.add))
            wide10 = [P, TILES, TABLE]
            for j in range(2):
                link(dve.tensor_tensor(el[:], M[:, j], t32[:], ALU.mult))
                link(dve.tensor_reduce(dest[:, j], el[:], AX, ALU.add))
                link(dve.tensor_tensor(reached[:, j], c.k("blkslot").unsqueeze(1).broadcast_to([P, TILES, TABLE + 1]),
                                       dest[:, j].unsqueeze(2).broadcast_to([P, TILES, TABLE + 1]), ALU.is_le))
                link(dve.tensor_reduce(in_block[:, j], reached[:, j], AX, ALU.add))
                link(dve.tensor_tensor(reached[:, j, :, 0:TABLE], reached[:, j, :, 0:TABLE], reached[:, j, :, 1:TABLE + 1],
                                       ALU.subtract))
                link(dve.scalar_tensor_tensor(in_block[:, j], in_block[:, j], -float(SLOTS), dest[:, j], ALU.mult, ALU.add))
                ids = c.k("ids").rearrange("p (j i o) -> p j i o", j=2, o=2)
                for o in range(2):
                    link(dve.tensor_tensor(numbers[:, j, :, :, o], reached[:, j, :, 0:TABLE],
                                           ids[:, j, :, o:o + 1].broadcast_to(wide10), ALU.mult))
                dve.tensor_tensor(at_slot[:, j], c.k("slot").unsqueeze(1).broadcast_to([P, TILES, SLOTS]),
                                  in_block[:, j].unsqueeze(2).broadcast_to([P, TILES, SLOTS]), ALU.is_equal).then_inc(pick_ready, 1)
            link(dve.tensor_tensor(be[:], nb[0:1, 1].unsqueeze(1).broadcast_to([1, BLOCKS, 32]),
                                   c.k("blkno")[0:1].unsqueeze(2).broadcast_to([1, BLOCKS, 32]), ALU.is_le))
            link(dve.tensor_reduce(bf[:, 0:BLOCKS], be[:], AX, ALU.add))
            link(dve.tensor_scalar(bf[:, 0:BLOCKS], bf[:, 0:BLOCKS], float(N_EXP - 1), None, ALU.min))
            half = BLOCKS // 2
            link(dve.tensor_scalar(be[:, 0, 0:half], c.k("blkno")[0:1, 0:half], 2.0, nb[0:1, 1, 31:32], ALU.mult, ALU.is_lt))
            link(dve.tensor_reduce(bf[:, BLOCKS:BLOCKS + 1], be[:, 0, 0:half], AX, ALU.add))
            link(dve.tensor_scalar(bf[:, BLOCKS + 1:BLOCKS + 2], bf[:, BLOCKS:BLOCKS + 1], -1.0, None, ALU.add))
            dve.tensor_copy(c.blocks[:], bf[:])
            dve.wait_ge(table_ps, 1)
            dve.tensor_scalar(c.table[:].rearrange("p b o -> p (b o)"), c.ps[0:SLOTS, 6, 0:2 * TABLE], float(BIG), None, ALU.add)


def experts(nc, c):
    with ExitStack() as ctx:
        def sem(name):
            return c.sem("experts_" + name)

        region = Region(c.arena, AT_Z4, AT_XM)
        raw = c.raw
        region.pos += PIECES * 2048
        X = region.take([SLOTS, 2, D])
        e = region.take([SLOTS, DE])
        H = region.take([SLOTS, DE])
        Y = region.take([SLOTS, 2, D])
        token = region.take([SLOTS, 2, 1], I32)
        dest = region.take([SLOTS, 2, 1], I32)
        none = region.take([SLOTS, 1], I32)
        tick = region.take([1, 8])
        SPLIT = 3
        split = Region(local_tensor(nc, ctx, "experts", F32R), 0, LOCAL)
        W = split.take([P, SPLIT, 2, 4, 512], F32)
        XT = split.take([P, 2, KD, SLOTS], F32)
        HT = split.take([P, 2, KE, SLOTS], F32)

        piece_in = [sem(f"piece_in{i}") for i in range(PIECES)]
        w_hi, w_lo, w_used = sem("w_hi"), sem("w_lo"), sem("w_used")
        idx_copied = sem("idx_copied")
        rows_in = [sem(f"rows_in{i}") for i in range(2)]
        y_stored = [sem(f"y_stored{i}") for i in range(2)]
        x_zero, gate_tanh, h_ready, y_out, silu_steps = (
            sem("e_x_zero"), sem("gate_tanh"), sem("e_h_ready"), sem("y_out"),
            sem("silu_steps"))
        xt_ps, xt_hi, xt_lo, ht_ps, ht_hi, ht_lo = (
            sem("xt_ps"), sem("xt_hi"), sem("xt_lo"), sem("e_ht_ps"), sem("e_ht_hi"), sem("e_ht_lo"))
        XT0, Y0, TURN0, STORED0, LO0, USED0 = 1, 2, 1, 16, PIECES, SPLIT
        turn, store_turn = sem("turn"), sem("store_turn")

        def pairs(eng, less=0):
            at = BLOCKS + less
            return eng.value_load(c.blocks[0:1, at:at + 1], min_val=TOK // SLOTS - less, max_val=BLOCKS // 2)

        block = ctx.enter_context(nc.Block())

        @block.sync
        def _(sp):
            n = pairs(sp)
            for p in range(PIECES):
                sp.nop().then_inc(piece_in[p], 16)

            def load(b):
                x = sp.value_load(c.blocks[0:1, bass.ds(b, 1)], min_val=0, max_val=N_EXP - 1)
                for p in range(PIECES):
                    sp.wait_ge(w_lo, b * PIECES + p + 1)
                    sp.dma_start(raw[:, p], c.d["w_exp"][bass.ds(x, 1), p].rearrange("o p k n -> (o p) k n")).then_inc(piece_in[p], 16)

            before_last = pairs(sp, 1)
            with sp.Fori(0, before_last) as i:
                load(i * 2 + 1)
                load(i * 2 + 2)
            load(before_last * 2 + 1)
            for p in range(2):
                sp.wait_ge(w_lo, n * 12 + p + 1)
                sp.dma_start(raw[:, p], c.d["w_exp"][0, p]).then_inc(piece_in[p], 16)

        @block.gpsimd
        def _(pool):
            def gather(q):
                pool.indirect_dma_start(X[:, q], None, c.d["h"], bass.IndirectOffsetOnAxis(ap=token[:, q].bitcast(U32), axis=0),
                                        bounds_check=TOK - 1, oob_is_err=False).then_inc(rows_in[q], 16)

            def scatter(q, at):
                pool.indirect_dma_start(c.d["rows"], bass.IndirectOffsetOnAxis(ap=at.bitcast(U32), axis=0), Y[:, q], None,
                                        bounds_check=2 * TOK - 1, oob_is_err=False).then_inc(y_stored[q], 16)

            n = pairs(pool)
            pool.memset(tick, 0.0)
            pool.engine_nop().then_inc(store_turn, TURN0)
            pool.memset(none[:], BIG).then_inc(x_zero, 1)
            pool.memset(Y[:], 0.0).then_inc(x_zero, 1)
            pool.memset(X[:], 0.0).then_inc(x_zero, 1)
            pool.tensor_copy(token[:], c.table[:, 0:2, 0:1]).then_inc(idx_copied, 1)
            pool.wait_ge(x_zero, 3)
            pool.wait_ge(idx_copied, 1)
            pool.engine_nop().then_inc(turn, 1)
            gather(0)
            gather(1)
            for q in range(2):
                scatter(q, none[:])
            with pool.Fori(0, n) as i:
                for q in range(2):
                    pool.wait_ge(xt_ps, i * 2 + q + 1 + XT0)
                    pool.tensor_copy(token[:, q], c.table[:, bass.ds(i * 2 + q + 2, 1), 0:1].rearrange("p a b -> p (a b)")).then_inc(idx_copied, 1)
                    pool.wait_ge(idx_copied, i * 4 + 2 * q + 2)
                    pool.tensor_tensor(tick[:, 1 + q:2 + q], tick[:, 0:1], tick[:, 0:1], ALU.mult).then_inc(turn, 1)
                    gather(q)
                    pool.wait_ge(y_stored[q], i * 16 + STORED0)
                    pool.tensor_copy(dest[:, q], c.table[:, bass.ds(i * 2 + q, 1), 1:2].rearrange("p a b -> p (a b)")).then_inc(idx_copied, 1)
                    pool.wait_ge(idx_copied, i * 4 + 2 * q + 3)
                    pool.wait_ge(y_out, i * 4 + 2 * q + 2 + Y0)
                    pool.tensor_tensor(tick[:, 3 + q:4 + q], tick[:, 0:1], tick[:, 0:1], ALU.mult).then_inc(store_turn, 1)
                    scatter(q, dest[:, q])
            pool.wait_ge(rows_in[1], n * 16 + 16)
            pool.tensor_tensor(tick[:, 7:8], tick[:, 0:1], tick[:, 0:1], ALU.mult)
            for q in range(2):
                pool.wait_ge(y_stored[q], n * 16 + STORED0)
                pool.tensor_tensor(tick[:, 5 + q:6 + q], tick[:, 0:1], tick[:, 0:1], ALU.mult)

        @block.tensor
        def _(pe):
            def turn_over(k, out, rows):
                return pe.transpose(out, rows, ident) if k else pe.matmul(out, rows, ident, start=True, stop=True)

            def transpose_rows(q):
                for k in range(KD):
                    mm = turn_over(k, c.ps[:, 0, k * SLOTS:(k + 1) * SLOTS], X[:, q, k * P:(k + 1) * P])
                mm.then_inc(xt_ps, 1)

            ident = c.k("ident")[0:SLOTS, 0:SLOTS]
            n = pairs(pe)
            pe.nop().then_inc(xt_ps, XT0)
            pe.nop().then_inc(w_used, USED0)
            pe.wait_ge(rows_in[0], 16)
            transpose_rows(0)

            with pe.Fori(0, n) as i:
                def piece(q, p, bank, tokens, k0, first, last):
                    pe.wait_ge(w_lo, i * 12 + 6 * q + p + 1 + LO0)
                    for k in range(4):
                        for n_, (a, b) in enumerate(((0, 0), (0, 1), (1, 0))):
                            mm = pe.matmul(c.ps[0:SLOTS, bank, :], tokens[:, a, k0 + k], W[:, p % SPLIT, b, k],
                                           start=first and k == 0 and n_ == 0, stop=last and k == 3 and n_ == 2)
                    mm.then_inc(w_used, 1)

                for q in range(2):
                    pe.wait_ge(xt_lo, i * 2 + q + 1)
                    piece(q, 0, 2, XT, 0, True, False)
                    piece(q, 1, 2, XT, 4, False, True)
                    piece(q, 2, 3, XT, 0, True, False)
                    piece(q, 3, 3, XT, 4, False, True)
                    pe.wait_ge(turn, i * 2 + q + 1)
                    pe.wait_ge(rows_in[1 - q], i * 16 + 16 * (1 + q))
                    transpose_rows(1 - q)
                    pe.wait_ge(h_ready, i * 2 + q + 1)
                    for k in range(KE):
                        mm = turn_over(k, c.ps[:, 4, k * SLOTS:(k + 1) * SLOTS], H[:, k * P:(k + 1) * P])
                    mm.then_inc(ht_ps, 1)
                    pe.wait_ge(ht_lo, i * 2 + q + 1)
                    pe.wait_ge(y_out, i * 4 + 2 * q + Y0)
                    for h in range(2):
                        piece(q, 4 + h, 6 + h, HT, 0, True, True)

        @block.scalar
        def _(act):
            n = pairs(act)
            act.nop().then_inc(y_out, Y0)

            def rows_hi():
                act.activation(XT[:, 0], c.ps[:, 0, :].rearrange("p (k t) -> p k t", k=KD), ACT.Copy).then_inc(xt_hi, 1)

            def hi(p, arrived, used):
                act.wait_ge(piece_in[p], arrived)
                act.wait_ge(w_used, used)
                act.activation(W[:, p % SPLIT, 0], raw[:, p], ACT.Copy).then_inc(w_hi, 1)

            for p in range(2):
                hi(p, 16, p + 1)
            act.wait_ge(xt_ps, 1 + XT0)
            rows_hi()
            with act.Fori(0, n) as i:
                for q in range(2):
                    m = i * 12 + 6 * q + 1
                    for p in (2, 3, 4):
                        hi(p, i * 32 + 16 * q + 16, m + p)
                    act.wait_ge(w_used, m + 1 + USED0)
                    act.activation(e[:], c.ps[0:SLOTS, 2, :], ACT.Tanh, scale=0.5).then_inc(gate_tanh, 1)
                    hi(5, i * 32 + 16 * q + 16, m + 5)
                    act.wait_ge(xt_ps, i * 2 + q + 2 + XT0)
                    rows_hi()
                    act.wait_ge(ht_ps, i * 2 + q + 1)
                    act.activation(HT[:, 0], c.ps[:, 4, 0:KE * SLOTS].rearrange("p (k t) -> p k t", k=KE), ACT.Copy).then_inc(ht_hi, 1)
                    for h in range(2):
                        hi(h, i * 32 + 16 * q + 32, m + 6 + h)
                        if h == 0:
                            act.wait_ge(store_turn, i * 2 + q + TURN0)
                            act.wait_ge(y_stored[q], i * 16 + STORED0)
                        act.wait_ge(w_used, m + 4 + h + USED0)
                        act.activation(Y[:, q, h * 512:(h + 1) * 512], c.ps[0:SLOTS, 6 + h, :], ACT.Copy).then_inc(y_out, 1)

        @block.vector
        def _(dve):
            n = pairs(dve)
            dve.engine_nop().then_inc(w_lo, LO0)

            def rows_lo(done):
                dve.wait_ge(xt_hi, done)
                dve.tensor_tensor(XT[:, 1], c.ps[:, 0, :].rearrange("p (k t) -> p k t", k=KD), XT[:, 0].bitcast(F32),
                                  ALU.subtract).then_inc(xt_lo, 1)

            def lo(p, done):
                dve.wait_ge(w_hi, done)
                dve.tensor_tensor(W[:, p % SPLIT, 1], raw[:, p], W[:, p % SPLIT, 0].bitcast(F32), ALU.subtract).then_inc(w_lo, 1)

            for p in range(2):
                lo(p, p + 1)
            rows_lo(1)
            with dve.Fori(0, n) as i:
                for q in range(2):
                    m = i * 12 + 6 * q + 1
                    for p in (2, 3, 4):
                        lo(p, m + p)
                    dve.wait_ge(gate_tanh, i * 2 + q + 1)
                    dve.scalar_tensor_tensor(H[:], e[:], 1.0, c.ps[0:SLOTS, 2, :], ALU.add, ALU.mult).then_inc(silu_steps, 1)
                    dve.wait_ge(silu_steps, i * 2 + q + 1)
                    dve.wait_ge(w_used, m + 3 + USED0)
                    dve.scalar_tensor_tensor(H[:], H[:], 0.5, c.ps[0:SLOTS, 3, :], ALU.mult, ALU.mult).then_inc(h_ready, 1)
                    rows_lo(i * 2 + q + 2)
                    dve.wait_ge(ht_hi, i * 2 + q + 1)
                    dve.tensor_tensor(HT[:, 1], c.ps[:, 4, 0:KE * SLOTS].rearrange("p (k t) -> p k t", k=KE),
                                      HT[:, 0].bitcast(F32), ALU.subtract).then_inc(ht_lo, 1)
                    for p in (5, 6, 7):
                        lo(p % PIECES, m + p)


def combine(nc, c):
    with ExitStack() as ctx:
        def sem(name):
            return c.sem("combine_" + name)

        region = Region(c.arena, AT_Z4, AT_XM)
        R = region.take([P, TILES, 2, D])
        g = region.take([P, D])
        y = region.take([P, TILES, D])
        ss = region.take([P, TILES])
        g_in, r_in, x_done, sq_done, y_done, stored = (
            sem("g_final_in"), [[sem(f"r_in{i}{j}") for j in range(2)] for i in range(TILES)], sem("c_x_done"),
            sem("c_sq_done"), sem("c_y_done"), sem("c_stored"))
        mean_ready, root_done = sem("c_mean_ready"), sem("c_root_done")

        block = ctx.enter_context(nc.Block())

        @block.sync
        def _(sp):
            sp.dma_start(g[:], c.d["g_final"]).then_inc(g_in, 16)
            for i in range(TILES):
                for j in range(2):
                    at = j * TOK + i * P
                    sp.dma_start(R[0:ROWS[i], i, j], c.d["rows"][at:at + ROWS[i]]).then_inc(r_in[i][j], 16)
            for i in range(TILES):
                sp.wait_ge(y_done, i + 1)
                sp.dma_start(c.o["y"][i * P:i * P + ROWS[i]], y[0:ROWS[i], i]).then_inc(stored, 16)
            sp.wait_ge(stored, 16 * TILES)

        @block.scalar
        def _(act):
            for i in range(TILES):
                r = ROWS[i]
                act.wait_ge(x_done, i + 1)
                act.activation(y[0:r, i], c.x2[0:r, i], ACT.Square, accum_out=ss[0:r, i:i + 1]).then_inc(sq_done, 1)
                act.wait_ge(mean_ready, i + 1)
                act.activation(ss[0:r, i:i + 1], ss[0:r, i:i + 1], ACT.Sqrt).then_inc(root_done, 1)

        @block.vector
        def _(dve):
            link = c.vsteps.on(dve)
            def add_rows(i):
                x = c.x2[0:ROWS[i], i]
                for j in range(2):
                    dve.wait_ge(r_in[i][j], 16)
                    ins = dve.scalar_tensor_tensor(x, R[0:ROWS[i], i, j], c.wt[0:ROWS[i], j, i:i + 1], x, ALU.mult, ALU.add)
                    if j == 0:
                        link(ins)
                ins.then_inc(x_done, 1)

            dve.wait_ge(g_in, 16)
            add_rows(0)
            for i in range(TILES):
                r = ROWS[i]
                x, s = c.x2[0:r, i], ss[0:r, i:i + 1]
                if i + 1 < TILES:
                    add_rows(i + 1)
                dve.wait_ge(sq_done, i + 1)
                dve.tensor_scalar(s, s, 1.0 / D, EPS, ALU.mult, ALU.add).then_inc(mean_ready, 1)
                dve.wait_ge(root_done, i + 1)
                link(dve.reciprocal(s, s))
                dve.scalar_tensor_tensor(y[0:r, i], x, s, g[0:r], ALU.mult, ALU.mult).then_inc(y_done, 1)


def build(nc, d, o):
    c = Core()
    c.d, c.o = d, o
    with ExitStack() as ctx:
        c.arena = ctx.enter_context(nc.sbuf_tensor("arena", [P, AT_LOCAL], F32))
        c.ps = ctx.enter_context(nc.psum_tensor("ps", [P, 8, 512], F32))
        taken = []

        def phase_semaphore(name):
            taken.append(nc.alloc_semaphore(name))
            return taken[-1]

        c.sem = phase_semaphore
        c.vsteps = Steps(ctx.enter_context(nc.semaphore("vector_steps")))
        c.gsteps = Steps(ctx.enter_context(nc.semaphore("gpsimd_steps")))
        c.asteps = Steps(ctx.enter_context(nc.semaphore("scalar_steps")))
        c.w1_in = ctx.enter_context(nc.semaphore("cmp_weights_in"))
        low = Region(c.arena, 0, AT_Z4)
        c.K = low.take([P, CW])
        c.k = lambda name: c.K[:, COFF[name]:COFF[name] + CONST[name]]
        c.pages = low.take([1, NB * PAGES], I32)
        c.gate = low.take([P, TILES, 24])
        c.w1 = low.take([P, 2, 8, P])
        c.w2 = low.take([HD, 2, HD])
        c.pe = low.take([P, 2, 16])
        c.b1 = low.take([HD, 2])
        c.A8 = low.take([P, 2, 2, ST])
        c.fin = low.take([P, 1 + NB, 2, ST])
        c.wt = low.take([P, 2, TILES])
        c.raw = Region(c.arena, AT_Z4, AT_XM).take([P, PIECES, 4, 512])
        over_attn = Region(c.arena, AT_X2_END, AT_LOCAL)
        c.table = over_attn.take([SLOTS, TABLE, 2], I32)
        c.blocks = over_attn.take([1, BLOCKS + 2], I32)
        c.pw = Region(c.arena, AT_Z4, AT_Z).take([P, 2, 9, ST])
        build_s5 = Region(c.arena, AT_XM, AT_STATE)
        c.Z = build_s5.take([P, 2, ST, CH, 16])
        c.cc = build_s5.take([P, 2, ST, 16])
        c.z4 = Region(c.arena, AT_Z4, AT_Z).take([P, ZW])
        c.z = Region(c.arena, AT_Z, AT_SSM).take([P, TILES, ZW])
        s5 = Region(c.arena, AT_SSM, AT_LOCAL)
        c.U = s5.take([P, GROUPS, NCH])
        c.KT = s5.take([P, CH, GROUPS * 16])
        c.C = s5.take([P, 2, ST, CH, 16])
        c.XM = s5.take([P, 2, ST, NCH])
        c.aT = s5.take([P, 4, TOK])
        c.X = s5.take([P, NCH + 1, 2, ST])
        c.S = s5.take([P, NCH, 2, ST])
        for phase in (project, ssm_build, prompt, sample, merge, experts, combine):
            phase(nc, c)
            if phase is not combine:
                nc.clear_and_free_semaphores(taken)
                taken.clear()
                nc.all_engine_barrier()


_OUTS = {"y": (TOK, D), "kv": (TOK, 512), "win_p": (SEQ, 256), "win_s": (NB, SEQ, 256), "ssm": (P, (1 + NB) * 2 * ST)}
_SCRATCH = {"u": ((TOK, SW), F32), "sig": ((16, P, TOK), F32), "h": ((TOK, D), F32),
            "rows": ((2 * TOK, D), F32)}


def layouts(i):
    def by_state(a):
        a = a.reshape((ST, 2 * HD) + a.shape[2:])
        return np.moveaxis(a, 0, 1)

    def k_tiles(w, tiles):
        return w.reshape(tiles, P, -1).transpose(1, 0, 2)

    x = np.concatenate([i["x_prompt"][0], i["x_sample"].reshape(NB * NT, D)], 0)
    w = i["w_in"][0]
    q = w[:, SW:SW + 512].reshape(D, 2, HG, HD).transpose(0, 2, 1, 3).reshape(D, 512)
    w = np.concatenate([w[:, :SW], q, w[:, SW + 512:]], 1)
    wt = k_tiles(w, KD)
    o = {"x": x, "xT": k_tiles(x.T, KD), "g_mix": i["g_mix"][0].reshape(KD, P).T}
    o["w_wide"] = wt[:, :, :6 * PW].reshape(P, KD, 6, PW).transpose(2, 0, 1, 3)
    o["w_rest"] = wt[:, :, 6 * PW:].reshape(P, KD, W_PIECES - 6, 256).transpose(2, 0, 1, 3)
    dt = np.repeat(i["ssm_log_dt"][0][:, None], HD, 1)
    o["ssm_par"] = np.stack([by_state(i["ssm_a_re"][0]), by_state(i["ssm_a_im"][0]), by_state(dt)], 1)
    o["ssm_b"] = np.stack([by_state(i["ssm_b_re"][0]), by_state(i["ssm_b_im"][0])], 1)
    o["ssm_c"] = np.stack([by_state(i["ssm_c_re"][0].transpose(0, 2, 1)), by_state(i["ssm_c_im"][0].transpose(0, 2, 1))], 1)
    o["ssm_d"] = np.broadcast_to(i["ssm_d"][0], (P, GROUPS, 16))
    o["state"] = i["state_ssm"][0].reshape(NB, ST, P, 2).transpose(2, 0, 3, 1)
    w1 = np.stack([i["cmp_w1_k"][0], i["cmp_w1_v"][0]]).reshape(2, 2, 8, P, HD)
    o["cmp_w1"] = w1.transpose(3, 0, 2, 1, 4).reshape(P, 2, 8, P)
    o["cmp_w2"] = np.stack([i["cmp_w2_k"][0], i["cmp_w2_v"][0]]).transpose(1, 0, 2)
    o["cmp_pe"] = np.stack([i["cmp_pe_k"][0], i["cmp_pe_v"][0]]).reshape(2, 16, P).transpose(2, 0, 1)
    o["cmp_b1"] = np.stack([i["cmp_b1_k"][0], i["cmp_b1_v"][0]]).T
    cache = i["cache_kv"][0]
    cmp_ = cache[:, :, 0:2].reshape(POOL, 8, 8, 2, 2, 2, HD)
    cmp_ = cmp_.transpose(0, 3, 6, 4, 5, 2, 1).reshape(POOL, P, 2, P)
    ks = cache[:, :, 2].reshape(POOL, P, P).transpose(0, 2, 1)[:, :, None]
    vs = cache[:, :, 3].reshape(POOL, P, 1, P)
    o["cache"] = np.concatenate([cmp_, ks, vs], 2)
    win = i["cache_win"][0]
    o["win_rows"] = win.reshape(NB, SEQ, 256)
    o["win_kT"] = win[:, :, 0].reshape(NB, SEQ, P).transpose(2, 0, 1)
    o["win_v"] = win[:, :, 1].reshape(NB, 4, P, P).transpose(2, 0, 1, 3)
    o["page_table"] = i["page_table"].reshape(1, -1)
    o["w_glu"] = k_tiles(i["w_glu"][0], 4)
    o["w_ssm"] = k_tiles(i["w_ssm_proj"][0], 4)
    o["w_attn"] = k_tiles(i["w_attn_proj"][0], 4)
    o["w_out"] = k_tiles(i["w_out"][0], KD)
    o["g_ffn"] = np.broadcast_to(i["g_ffn"][0], (P, D))
    o["g_final"] = np.broadcast_to(i["g_final"], (P, D))
    o["w_route"] = k_tiles(np.concatenate([i["w_router_group"][0], i["w_router_expert"][0]], 1), KD)
    o["b_route"] = np.broadcast_to(np.concatenate([i["b_router_group"][0], i["b_router_expert"][0]]), (P, 36))
    def by_k(w):
        return w.reshape(N_EXP, 2, 4, P, DE).transpose(0, 1, 3, 2, 4)

    down = i["w_exp_down"][0].reshape(N_EXP, KE, P, 2, 512).transpose(0, 3, 2, 1, 4)
    o["w_exp"] = np.concatenate([by_k(i["w_exp_gate"][0]), by_k(i["w_exp_up"][0]), down], 1)
    o["consts"] = constants()
    return {k: np.ascontiguousarray(v) for k, v in o.items()}


def kernel(**inputs):
    import concourse.bacc as _bacc
    from concourse.bass_utils import run_bass_kernel_spmd as _run

    nc = _bacc.Bacc("TRN2", target_bir_lowering=False, num_devices=1)
    arrays, d, o = {}, {}, {}
    for name, a in layouts({k: np.asarray(v) for k, v in inputs.items()}).items():
        arrays[f"in_{name}"] = a
        d[name] = nc.dram_tensor(f"in_{name}", a.shape, mybir.dt.from_np(a.dtype), kind="ExternalInput").ap()
    for name, shape in _OUTS.items():
        o[name] = nc.dram_tensor(f"out_{name}", shape, F32, kind="ExternalOutput").ap()
    for name, (shape, dt) in _SCRATCH.items():
        d[name] = nc.dram_tensor(f"scratch_{name}", shape, dt, kind="Internal").ap()
    build(nc, d, o)
    r = _run(nc, [arrays], core_ids=[0]).results[0]
    y, kv, win_p, win_s, ssm = (np.asarray(r[f"out_{n}"]) for n in _OUTS)
    ssm = ssm.reshape(P, 1 + NB, 2, ST).transpose(1, 3, 0, 2).reshape(1 + NB, GROUPS, HD, 2)
    return (y[:SEQ].reshape(1, SEQ, D), y[SEQ:].reshape(NB, NT, D),
            kv[:SEQ].reshape(1, 1, SEQ, 4, 2, HD), kv[SEQ:].reshape(1, NB, NT, 4, 2, HD),
            win_p.reshape(1, 1, SEQ, 2, 2, HD), win_s.reshape(1, NB, SEQ, 2, 2, HD),
            ssm[None, :1], ssm[None, 1:])
```
